# Optimizing a Trainium2 kernel written in Bass

```python
import math
import jax
import jax.numpy as jnp
from jax import lax
import numpy as np

D_MODEL = 1024
BATCH = 1
SEQ = 512
DEPTH = 2

CHUNK = 64
N_MEM = 256
NORM_EPS = 1e-6
GROUP_NORM_EPS = 64e-5

A_HEAD_DIM = 128
A_WIDTH = D_MODEL // 2
A_HEADS = A_WIDTH // A_HEAD_DIM
CONV_WIDTH = 4
A_COLS = 4 * A_WIDTH + 2 * A_HEADS

B_HEAD_DIM = 64
B_WIDTH = D_MODEL // 2
B_HEADS = B_WIDTH // B_HEAD_DIM
B_DECAY_LORA = 64
B_ICLR_LORA = 64
B_GATE_LORA = 128
B_COLS = 3 * B_WIDTH + B_DECAY_LORA + B_ICLR_LORA + B_GATE_LORA
B_SPLIT_IDX = (B_WIDTH, 2 * B_WIDTH, 3 * B_WIDTH, 3 * B_WIDTH + B_DECAY_LORA,
               3 * B_WIDTH + B_DECAY_LORA + B_ICLR_LORA)
AB_COLS = A_COLS + B_COLS
MIX_WIDTH_AB = A_WIDTH + B_WIDTH

C_KEY_DIM = 128
C_HEADS = D_MODEL // C_KEY_DIM
C_VAL_DIM = D_MODEL // C_HEADS
C_KEY_WIDTH = C_HEADS * C_KEY_DIM
C_VAL_WIDTH = C_HEADS * C_VAL_DIM
C_COLS = 2 * C_KEY_WIDTH + 2 * C_VAL_WIDTH

XA_HEADS = 4
XA_HEAD_DIM = D_MODEL // XA_HEADS

N_GROUPS = 4
EXPERTS_PER_GROUP = 4
N_EXPERTS = N_GROUPS * EXPERTS_PER_GROUP
TOP_K_IN_GROUP = 2
EXPERT_FF = D_MODEL // 4

N_EVEN = (DEPTH + 1) // 2
N_ODD = DEPTH // 2

kernel_name = 'hybrid_gdn_rwkv7_hgrn2_hmoe_encoder'

F32 = jnp.float32

def rms_norm(x, gain):
    xf = x.astype(F32)
    y = xf * lax.rsqrt(jnp.mean(xf * xf, axis=-1, keepdims=True) + NORM_EPS)
    return (y * gain.astype(F32)).astype(x.dtype)

def layer_norm(x, gain, bias, eps):
    xf = x.astype(F32)
    mu = jnp.mean(xf, axis=-1, keepdims=True)
    var = jnp.mean(jnp.square(xf - mu), axis=-1, keepdims=True)
    return ((xf - mu) * lax.rsqrt(var + eps) * gain.astype(F32) + bias.astype(F32)).astype(x.dtype)

def l2_normalize(x):
    xf = x.astype(F32)
    return (xf * lax.rsqrt(jnp.sum(xf * xf, axis=-1, keepdims=True) + 1e-6)).astype(x.dtype)

def causal_short_conv(x, w):
    return lax.conv_general_dilated(
        x, w[:, None, :].astype(x.dtype), window_strides=(1,),
        padding=[(w.shape[0] - 1, 0)], dimension_numbers=('NWC', 'WIO', 'NWC'),
        feature_group_count=x.shape[-1])

def token_shift_lerp(p, mu):
    prev = jnp.pad(p, ((0, 0), (1, 0), (0, 0)))[:, :-1]
    return p + mu.astype(p.dtype) * (prev - p)

def split_heads(t, n_heads, head_dim):
    b, s, _ = t.shape
    return t.reshape(b, s, n_heads, head_dim).transpose(0, 2, 1, 3).astype(F32)

def gated_delta_rule_chunked(q, k, v, log_alpha, beta):
    b, h, s, dk = q.shape
    dv = v.shape[-1]
    nc = s // CHUNK
    q = q.reshape(b, h, nc, CHUNK, dk)
    k = k.reshape(b, h, nc, CHUNK, dk)
    v = v.reshape(b, h, nc, CHUNK, dv)
    beta = beta.reshape(b, h, nc, CHUNK)
    g = jnp.cumsum(log_alpha.reshape(b, h, nc, CHUNK), axis=-1)
    idx = jnp.arange(CHUNK)
    incl = idx[:, None] >= idx[None, :]
    strict = idx[:, None] > idx[None, :]
    decay = jnp.exp(jnp.where(incl, g[..., :, None] - g[..., None, :], -jnp.inf))
    k_beta = k * beta[..., None]
    a_low = jnp.where(strict, jnp.einsum('bhnid,bhnjd->bhnij', k_beta, k) * decay, 0.0)
    m = a_low + jnp.eye(CHUNK, dtype=F32)
    rhs = jnp.concatenate([v * beta[..., None], k_beta * jnp.exp(g)[..., None]], axis=-1)
    sol = lax.linalg.triangular_solve(m, rhs, left_side=True, lower=True, unit_diagonal=True)
    u, w = sol[..., :dv], sol[..., dv:]
    qk = jnp.einsum('bhnid,bhnjd->bhnij', q, k) * decay
    q_dec = q * jnp.exp(g)[..., None]
    k_dec = k * jnp.exp(g[..., -1:] - g)[..., None]
    g_last = jnp.exp(g[..., -1])

    def step(state, inp):
        qk_c, qd_c, w_c, u_c, kd_c, gl_c = inp
        v_new = u_c - jnp.einsum('bhcd,bhde->bhce', w_c, state)
        o = jnp.einsum('bhcd,bhde->bhce', qd_c, state) + jnp.einsum('bhij,bhje->bhie', qk_c, v_new)
        state = state * gl_c[..., None, None] + jnp.einsum('bhcd,bhce->bhde', kd_c, v_new)
        return state, o

    xs = tuple(jnp.moveaxis(t, 2, 0) for t in (qk, q_dec, w, u, k_dec, g_last))
    _, o = lax.scan(step, jnp.zeros((b, h, dk, dv), F32), xs)
    return jnp.moveaxis(o, 0, 2).reshape(b, h, s, dv)

def rwkv7_recurrence(r, w, k, v, kk, a):
    b, _, h, n = r.shape

    def step(state, inp):
        r_t, w_t, k_t, v_t, kk_t, a_t = inp
        sa = jnp.einsum('bhvk,bhk->bhv', state, -kk_t)
        state = (state * w_t[:, :, None, :] + sa[..., None] * (kk_t * a_t)[:, :, None, :]
                 + v_t[..., None] * k_t[:, :, None, :])
        return state, jnp.einsum('bhvk,bhk->bhv', state, r_t)

    xs = tuple(jnp.moveaxis(t, 1, 0) for t in (r, w, k, v, kk, a))
    _, o = lax.scan(step, jnp.zeros((b, h, n, n), F32), xs)
    return jnp.moveaxis(o, 0, 1)

def hgrn2_chunked(q, k, v, log_f):
    b, h, s, dk = q.shape
    dv = v.shape[-1]
    nc = s // CHUNK

    def to_chunks(t):
        return jnp.moveaxis(t.reshape(b, h, nc, CHUNK, t.shape[-1]), 2, 0)

    qc, kc, vc = to_chunks(q), to_chunks(k), to_chunks(v)
    gc = jnp.cumsum(to_chunks(log_f), axis=3)
    idx = jnp.arange(CHUNK)
    incl = (idx[:, None] >= idx[None, :])[:, :, None]

    def step(state, inp):
        q_c, k_c, v_c, g_c = inp
        g_last = g_c[:, :, -1:, :]
        dec = jnp.exp(jnp.where(incl, g_c[:, :, :, None, :] - g_c[:, :, None, :, :], -jnp.inf))
        scores = jnp.einsum('bhid,bhjd,bhijd->bhij', q_c, k_c, dec)
        o = (jnp.einsum('bhid,bhde->bhie', q_c * jnp.exp(g_c), state)
             + jnp.einsum('bhij,bhje->bhie', scores, v_c))
        state = (state * jnp.exp(g_last)[:, :, 0, :, None]
                 + jnp.einsum('bhjd,bhje->bhde', k_c * jnp.exp(g_last - g_c), v_c))
        return state, o

    _, o = lax.scan(step, jnp.zeros((b, h, dk, dv), F32), (qc, kc, vc, gc))
    return jnp.moveaxis(o, 0, 2).reshape(b, h, s, dv)

def deltanet_rwkv_mixer(h, w_in, conv_w, a_log, dt_bias, onorm_a, shift_mu, w0, w2, a0, a2, g2,
                        k_k, k_a, r_k, ln_w, ln_b, w_out):
    bsz, s, _ = h.shape
    proj = h @ w_in
    p_a, p_b = proj[..., :A_COLS], proj[..., A_COLS:]

    qkv = jax.nn.silu(causal_short_conv(p_a[..., :3 * A_WIDTH], conv_w))
    q, k, v = jnp.split(qkv, 3, axis=-1)
    gate_a = p_a[..., 3 * A_WIDTH:4 * A_WIDTH].astype(F32)
    decay_in = p_a[..., 4 * A_WIDTH:4 * A_WIDTH + A_HEADS].astype(F32)
    beta_in = p_a[..., 4 * A_WIDTH + A_HEADS:].astype(F32)
    q = l2_normalize(split_heads(q, A_HEADS, A_HEAD_DIM)) * (A_HEAD_DIM ** -0.5)
    k = l2_normalize(split_heads(k, A_HEADS, A_HEAD_DIM))
    v = split_heads(v, A_HEADS, A_HEAD_DIM)
    log_alpha = (-jnp.exp(a_log.astype(F32)) * jax.nn.softplus(decay_in + dt_bias.astype(F32))).transpose(0, 2, 1)
    beta = jax.nn.sigmoid(beta_in).transpose(0, 2, 1)
    o_a = gated_delta_rule_chunked(q, k, v, log_alpha, beta).transpose(0, 2, 1, 3)
    o_a = rms_norm(o_a, onorm_a) * jax.nn.silu(gate_a.reshape(bsz, s, A_HEADS, A_HEAD_DIM))
    o_a = o_a.reshape(bsz, s, A_WIDTH)

    p_b = token_shift_lerp(p_b, shift_mu)
    r, kb, vb, wl, al, gl = jnp.split(p_b, B_SPLIT_IDX, axis=-1)
    hd = (bsz, s, B_HEADS, B_HEAD_DIM)
    w_raw = (w0 + jnp.tanh(wl) @ w2).astype(F32)
    decay_b = jnp.exp(-jnp.exp(-jax.nn.softplus(-w_raw) - 0.5)).reshape(hd)
    iclr = jax.nn.sigmoid((a0 + al @ a2).astype(F32)).reshape(hd)
    gate_b = (jax.nn.sigmoid(gl) @ g2).astype(F32)
    r = r.astype(F32).reshape(hd)
    kb = kb.astype(F32).reshape(hd)
    vb = vb.astype(F32).reshape(hd)
    kk = l2_normalize(kb * k_k.astype(F32).reshape(B_HEADS, B_HEAD_DIM))
    kb = kb * (1.0 + (iclr - 1.0) * k_a.astype(F32).reshape(B_HEADS, B_HEAD_DIM))
    o_b = rwkv7_recurrence(r, decay_b, kb, vb, kk, iclr)
    o_b = layer_norm(o_b, ln_w.reshape(B_HEADS, B_HEAD_DIM), ln_b.reshape(B_HEADS, B_HEAD_DIM), GROUP_NORM_EPS)
    o_b = o_b + jnp.sum(r * kb * r_k.astype(F32), axis=-1, keepdims=True) * vb
    o_b = o_b.reshape(bsz, s, B_WIDTH) * gate_b

    o = jnp.concatenate([o_a, o_b], axis=-1).astype(h.dtype)
    return o @ w_out

def hgrn_lower_bounds(lb_param):
    p = jax.nn.softmax(lb_param.astype(F32), axis=0)
    return jnp.cumsum(p, axis=0) - p[0]

def hgrn2_mixer(h, w_in, lower_bound, onorm, w_out):
    bsz, s, _ = h.shape
    proj = h @ w_in
    q = proj[..., :C_KEY_WIDTH]
    f = proj[..., C_KEY_WIDTH:2 * C_KEY_WIDTH]
    i = proj[..., 2 * C_KEY_WIDTH:2 * C_KEY_WIDTH + C_VAL_WIDTH]
    g = proj[..., 2 * C_KEY_WIDTH + C_VAL_WIDTH:]
    q = jax.nn.silu(q.astype(F32))
    lb = lower_bound.astype(F32)
    log_f = jnp.logaddexp(jnp.log(lb), jnp.log1p(-lb) + jax.nn.log_sigmoid(f.astype(F32)))
    k = -jnp.expm1(log_f)
    o = hgrn2_chunked(split_heads(q, C_HEADS, C_KEY_DIM), split_heads(k, C_HEADS, C_KEY_DIM),
                      split_heads(i, C_HEADS, C_VAL_DIM), split_heads(log_f, C_HEADS, C_KEY_DIM))
    o = rms_norm(o.transpose(0, 2, 1, 3), onorm) * jax.nn.silu(g.astype(F32).reshape(bsz, s, C_HEADS, C_VAL_DIM))
    return o.reshape(bsz, s, C_VAL_WIDTH).astype(h.dtype) @ w_out

def memory_cross_attention(h, mem_n, wq, wkv, wo):
    bsz, s, d = h.shape
    m = mem_n.shape[1]
    q = (h @ wq).reshape(bsz, s, XA_HEADS, XA_HEAD_DIM)
    k, v = jnp.split(mem_n @ wkv, 2, axis=-1)
    k = k.reshape(bsz, m, XA_HEADS, XA_HEAD_DIM)
    v = v.reshape(bsz, m, XA_HEADS, XA_HEAD_DIM)
    scores = jnp.einsum('bthd,bmhd->bhtm', q, k).astype(F32) * (XA_HEAD_DIM ** -0.5)
    p = jax.nn.softmax(scores, axis=-1).astype(v.dtype)
    o = jnp.einsum('bhtm,bmhd->bthd', p, v).reshape(bsz, s, d)
    return o @ wo

def hierarchical_moe(h, w_group, b_group, w_expert, b_expert, w1, w3, w2):
    bsz, s, d = h.shape
    x = h.reshape(bsz * s, d)
    group_logits = (x @ w_group + b_group).astype(F32)
    group_prob = jax.nn.softmax(group_logits, axis=-1)
    group_sel = jnp.argmax(group_logits, axis=-1)
    group_gate = jnp.take_along_axis(group_prob, group_sel[:, None], axis=-1)
    expert_logits = (x @ w_expert + b_expert).astype(F32).reshape(-1, N_GROUPS, EXPERTS_PER_GROUP)
    in_group = jnp.take_along_axis(expert_logits, group_sel[:, None, None], axis=1)[:, 0]
    top_p, top_i = lax.top_k(jax.nn.softmax(in_group, axis=-1), TOP_K_IN_GROUP)
    gates = group_gate * top_p / jnp.sum(top_p, axis=-1, keepdims=True)
    expert_id = group_sel[:, None] * EXPERTS_PER_GROUP + top_i
    combine = jnp.einsum('nk,nke->ne', gates, jax.nn.one_hot(expert_id, N_EXPERTS, dtype=F32))
    hid = jax.nn.silu(jnp.einsum('nd,edf->nef', x, w1)) * jnp.einsum('nd,edf->nef', x, w3)
    hid = hid * combine[:, :, None].astype(hid.dtype)
    y = jnp.einsum('nef,efd->nd', hid, w2)
    return y.reshape(bsz, s, d)

def setup_inputs(seed: int = 0) -> dict:
    key = jax.random.key(seed)
    ks = iter(jax.random.split(key, 64))

    def nrm(shape, scale):
        return jax.random.normal(next(ks), shape, F32) * scale

    def uni(shape, lo, hi):
        return jax.random.uniform(next(ks), shape, F32, lo, hi)

    d = D_MODEL
    ne, no = N_EVEN, N_ODD
    dt = jnp.exp(uni((ne, A_HEADS), math.log(1e-3), math.log(1e-1)))
    return {
        'x': nrm((BATCH, SEQ, d), 1.0),
        'mem': nrm((BATCH, N_MEM, d), 1.0),
        'norm_mix': 1.0 + nrm((DEPTH, d), 0.02),
        'norm_xattn': 1.0 + nrm((DEPTH, d), 0.02),
        'norm_mem': 1.0 + nrm((DEPTH, d), 0.02),
        'norm_ffn': 1.0 + nrm((DEPTH, d), 0.02),
        'norm_final': 1.0 + nrm((d,), 0.02),
        'ab_w_in': nrm((ne, d, AB_COLS), d ** -0.5),
        'ab_conv': nrm((ne, CONV_WIDTH, 3 * A_WIDTH), CONV_WIDTH ** -0.5),
        'ab_a_log': jnp.log(uni((ne, A_HEADS), 1.0, 16.0)),
        'ab_dt_bias': dt + jnp.log(-jnp.expm1(-dt)),
        'ab_onorm': 1.0 + nrm((ne, A_HEAD_DIM), 0.02),
        'ab_shift_mu': uni((ne, B_COLS), 0.0, 1.0),
        'ab_w0': uni((ne, B_WIDTH), -3.0, 1.0),
        'ab_w2': nrm((ne, B_DECAY_LORA, B_WIDTH), 0.5 * B_DECAY_LORA ** -0.5),
        'ab_a0': nrm((ne, B_WIDTH), 0.5),
        'ab_a2': nrm((ne, B_ICLR_LORA, B_WIDTH), B_ICLR_LORA ** -0.5),
        'ab_g2': nrm((ne, B_GATE_LORA, B_WIDTH), B_GATE_LORA ** -0.5),
        'ab_k_k': 0.85 + nrm((ne, B_WIDTH), 0.05),
        'ab_k_a': 1.0 + nrm((ne, B_WIDTH), 0.05),
        'ab_r_k': nrm((ne, B_HEADS, B_HEAD_DIM), 0.1),
        'ab_ln_w': 1.0 + nrm((ne, B_WIDTH), 0.02),
        'ab_ln_b': nrm((ne, B_WIDTH), 0.02),
        'ab_w_out': nrm((ne, MIX_WIDTH_AB, d), 0.5 * MIX_WIDTH_AB ** -0.5),
        'c_w_in': nrm((no, d, C_COLS), d ** -0.5),
        'c_lb_param': nrm((DEPTH, C_KEY_WIDTH), 0.5),
        'c_onorm': 1.0 + nrm((no, C_VAL_DIM), 0.02),
        'c_w_out': nrm((no, C_VAL_WIDTH, d), 0.5 * C_VAL_WIDTH ** -0.5),
        'xa_wq': nrm((DEPTH, d, d), d ** -0.5),
        'xa_wkv': nrm((DEPTH, d, 2 * d), d ** -0.5),
        'xa_wo': nrm((DEPTH, d, d), 0.5 * d ** -0.5),
        'moe_w_group': nrm((DEPTH, d, N_GROUPS), d ** -0.5),
        'moe_b_group': nrm((DEPTH, N_GROUPS), 0.01),
        'moe_w_expert': nrm((DEPTH, d, N_EXPERTS), d ** -0.5),
        'moe_b_expert': nrm((DEPTH, N_EXPERTS), 0.01),
        'moe_w1': nrm((DEPTH, N_EXPERTS, d, EXPERT_FF), d ** -0.5),
        'moe_w3': nrm((DEPTH, N_EXPERTS, d, EXPERT_FF), d ** -0.5),
        'moe_w2': nrm((DEPTH, N_EXPERTS, EXPERT_FF, d), EXPERT_FF ** -0.5),
    }

def reference(x, mem, norm_mix, norm_xattn, norm_mem, norm_ffn, norm_final,
              ab_w_in, ab_conv, ab_a_log, ab_dt_bias, ab_onorm, ab_shift_mu, ab_w0, ab_w2,
              ab_a0, ab_a2, ab_g2, ab_k_k, ab_k_a, ab_r_k, ab_ln_w, ab_ln_b, ab_w_out,
              c_w_in, c_lb_param, c_onorm, c_w_out,
              xa_wq, xa_wkv, xa_wo,
              moe_w_group, moe_b_group, moe_w_expert, moe_b_expert, moe_w1, moe_w3, moe_w2):
    lower_bounds = hgrn_lower_bounds(c_lb_param)
    for layer in range(DEPTH):
        h = rms_norm(x, norm_mix[layer])
        if layer % 2 == 0:
            e = layer // 2
            mix = deltanet_rwkv_mixer(h, ab_w_in[e], ab_conv[e], ab_a_log[e], ab_dt_bias[e], ab_onorm[e],
                                      ab_shift_mu[e], ab_w0[e], ab_w2[e], ab_a0[e], ab_a2[e], ab_g2[e],
                                      ab_k_k[e], ab_k_a[e], ab_r_k[e], ab_ln_w[e], ab_ln_b[e], ab_w_out[e])
        else:
            o = layer // 2
            mix = hgrn2_mixer(h, c_w_in[o], lower_bounds[layer], c_onorm[o], c_w_out[o])
        x = x + mix.astype(x.dtype)
        xa = memory_cross_attention(rms_norm(x, norm_xattn[layer]), rms_norm(mem, norm_mem[layer]),
                                    xa_wq[layer], xa_wkv[layer], xa_wo[layer])
        x = x + xa.astype(x.dtype)
        ff = hierarchical_moe(rms_norm(x, norm_ffn[layer]), moe_w_group[layer], moe_b_group[layer],
                              moe_w_expert[layer], moe_b_expert[layer], moe_w1[layer], moe_w3[layer],
                              moe_w2[layer])
        x = x + ff.astype(x.dtype)
    return rms_norm(x, norm_final)


_drawn_inputs = setup_inputs


def setup_inputs(seed=0):
    import zlib

    import numpy as np

    out = dict(_drawn_inputs(seed))
    spreads = {}
    factors = {'norm_xattn': 5.576,
     'norm_mem': 6.628,
     'norm_final': 8.228,
     'ab_k_k': 2.804,
     'ab_ln_w': 3.447,
     'ab_ln_b': 2.747,
     'c_onorm': 4.418,
     'norm_ffn': 3.034,
     'moe_b_group': 3.043,
     'moe_b_expert': 6.933}
    for name, (base, spread) in spreads.items():
        noise = np.random.default_rng([zlib.crc32(name.encode()), seed]).standard_normal(out[name].shape)
        drawn = base * np.exp(spread * noise) if base else spread * noise
        out[name] = jnp.asarray(drawn.astype(out[name].dtype))
    for name, factor in factors.items():
        out[name] = (out[name] * factor).astype(out[name].dtype)
    return out
```

```python
from contextlib import ExitStack

import numpy as np
import concourse.bass as bass
from concourse import mybir

F32 = mybir.dt.float32
I32 = mybir.dt.int32
ALU = mybir.AluOpType
ACT = mybir.ActivationFunctionType
AX = mybir.AxisListType

P = 128
D = 1024
T = 512
M = 256
DT = D // P
CH = T // P
AH = 4
BT = 4
CHEADS = 8
XH = 4
NE, NG, EG = 16, 4, 4
FF = 256
ITEMS = 24
BLK = 2048
RING = 4
LEVELS = [1, 2, 4, 8, 16, 32, 64]

C_ID, C_ONE, C_BLK, C_INC, C_STR = 0, P, 2 * P, 3 * P, 4 * P
C_LVL = 5 * P
C_RST = C_LVL + 7 * P
C_SEL = C_RST + T
C_IOTA = C_SEL + 8 * P
C_WTS = C_IOTA + ITEMS
C_EPS = C_WTS + 4
NCONST = C_EPS + 4

_names = [("mix", 16), ("xat", 16), ("mem", 16), ("ffn", 16), ("fin", 8), ("conv", 48), ("alog", 1),
          ("dt", 1), ("onA", 1), ("onC", 1), ("mu", 14), ("w0", 4), ("a0", 4), ("kk", 4), ("ka", 4),
          ("rk", 4), ("lnw", 4), ("lnb", 4), ("lb", 16), ("w2a2", 512), ("g2", 512), ("wge", 320),
          ("wdb", 64), ("bge", 40)]
PC, NPAR = {}, 0
for _n, _w in _names:
    PC[_n] = NPAR
    NPAR += _w

B_IN, B_AOUT, B_XA0, B_CIN = 0, 15, 19, 35
B_COUT, B_XA1 = 51, 55
NBLK = 71


def build(nc, wst, moe13, moe2, par_d, con_d, x_d, mem_d, out_d, rows_d):
    ctx = ExitStack()
    with ctx:
        def sb(name, shape, dt=F32):
            return ctx.enter_context(nc.sbuf_tensor(name, shape, dt))

        sems = {}

        def S(name):
            if name not in sems:
                sems[name] = ctx.enter_context(nc.semaphore(name))
            return sems[name]

        con = sb("con", [P, NCONST])
        par = sb("par", [P, NPAR])
        xT = sb("xT", [P, DT, T])
        hT = sb("hT", [P, DT, T])
        memT = sb("memT", [P, DT, M])
        proj = sb("proj", [P, 32, T])
        ring = sb("ring", [P, 6, BLK])
        work = sb("work", [P, 14, T])
        small = sb("small", [P, 1024])
        smalli = sb("smalli", [P, 64], I32)
        bank = [ctx.enter_context(nc.psum_tensor(f"bank{i}", [P, T], F32)) for i in range(8)]
        extra = ring[:, 4:6, :].rearrange("p a (b n) -> p (a b) n", n=T)

        ident = con[:, C_ID:C_ID + P]
        ones = con[:, C_ONE:C_ONE + P]
        bones = con[:, C_BLK:C_BLK + P]
        incl = con[:, C_INC:C_INC + P]
        strict = con[:, C_STR:C_STR + P]
        lvl = [con[:, C_LVL + P * i:C_LVL + P * (i + 1)] for i in range(7)]
        reset = con[:, C_RST:C_RST + T]
        sel8 = [con[0:8, C_SEL + P * i:C_SEL + P * (i + 1)] for i in range(8)]
        eps6 = con[:, C_EPS:C_EPS + 1]
        epsg = con[:, C_EPS + 1:C_EPS + 2]

        def pc(name, i=0, rows=P):
            return par[0:rows, PC[name] + i:PC[name] + i + 1]

        def chunks(ap):
            return ap.rearrange("p (c n) -> p c n", n=P)

        def over4(ap):
            return ap.unsqueeze(1).broadcast_to([P, CH, P])

        block = ctx.enter_context(nc.Block())

        class Line:

            def __init__(self, eng, name):
                self.eng, self.sem, self.n = eng, S(name), 0

            def __call__(self, ins):
                self.n += 1
                ins.then_inc(self.sem, 1)
                self.eng.wait_ge(self.sem, self.n)

        NORMS = {"mix0": 0, "mem0": 1, "xat0": 2, "ffn0": 3, "mix1": 4, "mem1": 5, "xat1": 6, "ffn1": 7, "fin": 8}

        def sq_of(n):
            return work[:, 0:8, 0:n]

        def norm_act(act, step, k, src, n):
            if k > 0:
                act.wait_ge(S("norm_summed"), k)
            for t in range(DT):
                nc.scalar.activation(work[:, t, 0:n], src[:, t, 0:n], ACT.Square).then_inc(S("norm_squared"), 1)
            act.wait_ge(S("norm_summed"), k + 1)
            step(nc.scalar.activation(work[:, 8, 0:n], bank[7][:, 0:n], ACT.Ln, bias=eps6, scale=1.0 / D))
            nc.scalar.activation(work[:, 9, 0:n], work[:, 8, 0:n], ACT.Exp, scale=-0.5).then_inc(S("norm_rstd"), 1)

        def norm_pe(pe, k, n):
            for t in range(DT):
                pe.wait_ge(S("norm_squared"), DT * k + t + 1)
                mm = nc.tensor.matmul(bank[7][:, 0:n], ones, work[:, t, 0:n], start=(t == 0), stop=(t == DT - 1))
            mm.then_inc(S("norm_summed"), 1)

        def norm_dve(dve, k, src, dst, n, gain):
            dve.wait_ge(S("norm_rstd"), k + 1)
            for t in range(DT):
                nc.vector.scalar_tensor_tensor(
                    out=dst[:, t, 0:n], in0=src[:, t, 0:n], scalar=gain[:, t:t + 1], in1=work[:, 9, 0:n],
                    op0=ALU.mult, op1=ALU.mult).then_inc(S("norm_done"), 1)
            dve.wait_ge(S("norm_done"), DT * (k + 1))

        def gains(name, layer=0):
            return par[:, PC[name] + DT * layer:PC[name] + DT * layer + DT]

        def each_block(eng, first, count, body):
            turns = count // RING
            if turns > 1:
                with eng.Fori(0, turns) as i:
                    for s in range(RING):
                        body(i, first + s)
            else:
                turns = 0
            for b in range(first + turns * RING, first + count):
                body(0, b)

        def project_pe(pe, first, count, src, n, tokens_out=False):
            def body(i, b):
                w = ring[:, b % RING, :].rearrange("p (k n) -> p k n", k=DT)
                pe.wait_ge(S(f"weights{b % RING}"), (b // RING + 1 + i) * 16)
                for h in range(2):
                    bk = bank[(2 * b + h) % 4]
                    pe.wait_ge(S(f"tile_free{h}"), b + RING * i + 1)
                    for k in range(DT):
                        if tokens_out:
                            mm = nc.tensor.matmul(bk[:, 0:256], src[:, k, h * P:h * P + P], w[:, k, :],
                                                  start=(k == 0), stop=(k == DT - 1))
                        else:
                            mm = nc.tensor.matmul(bk[:, 0:n], w[:, k, h * P:h * P + P], src[:, k, 0:n],
                                                  start=(k == 0), stop=(k == DT - 1))
                    mm.then_inc(S(f"tile_ready{h}"), 1)
            each_block(pe, first, count, body)

        def drain(eng, first, count, halves, write):
            def body(i, b):
                for h in halves:
                    eng.wait_ge(S(f"tile_ready{h}"), b + RING * i + 1)
                    write(h, i, b, bank[(2 * b + h) % 4]).then_inc(S(f"tile_free{h}"), 1)
            each_block(eng, first, count, body)

        def tile_at(buf, base, i, b, h, first):
            n = base + 2 * (b - first) + h
            if isinstance(i, int):
                return buf[:, n + 8 * i, :]
            return buf[:, bass.ds(i * 8 + n, 1), :].rearrange("p a n -> p (a n)")

        def drain_copies(act_or_dve, eng, first, count, half, buf, base, n):
            def write(h, i, b, bk):
                dst = tile_at(buf, base, i, b, h, first)[:, 0:n]
                if act_or_dve == "act":
                    return nc.scalar.activation(dst, bk[:, 0:n], ACT.Copy)
                return nc.vector.tensor_copy(dst, bk[:, 0:n])
            drain(eng, first, count, [half], write)

        def drain_residual(dve, first):
            def write(h, i, b, bk):
                dst = tile_at(xT, 0, i, b, h, first)
                return nc.vector.tensor_tensor(dst, dst, bk[:, :], ALU.add)
            drain(dve, first, 4, [0, 1], write)
            dve.wait_ge(S("tile_free1"), 2 + first + 4)

        inv_rounds = {"n": 0}

        def inv_pe(pe, r, bufs):
            for li in range(7):
                for g, (MT, Tt, TT, X, Cm) in enumerate(bufs):
                    if li == 0:
                        pe.wait_ge(S(f"inv_tt{g}"), 7 * r + 1)
                        for c in range(CH):
                            mm = nc.tensor.transpose(bank[g][:, c * P:c * P + P], chunks(TT)[:, c, :], ident)
                        mm.then_inc(S(f"inv_t_ready{g}"), 1)
                        continue
                    pe.wait_ge(S(f"inv_c{g}"), 7 * r + li + 1)
                    pe.wait_ge(S(f"inv_t{g}"), 6 * r + li)
                    for c in range(CH):
                        mm = nc.tensor.matmul(bank[g][:, c * P:c * P + P], chunks(Cm)[:, c, :], chunks(Tt)[:, c, :],
                                              start=True, stop=True)
                    mm.then_inc(S(f"inv_x_ready{g}"), 1)
                for g, (MT, Tt, TT, X, Cm) in enumerate(bufs):
                    if li == 0:
                        continue
                    pe.wait_ge(S(f"inv_x{g}"), 6 * r + li)
                    pe.wait_ge(S(f"inv_tt{g}"), 7 * r + li)
                    if li < 6:
                        for c in range(CH):
                            mm = nc.tensor.matmul(bank[2 + g][:, c * P:c * P + P], chunks(TT)[:, c, :], chunks(X)[:, c, :],
                                                  start=True, stop=True)
                    for c in range(CH):
                        mm = nc.tensor.matmul(bank[4 + g][:, c * P:c * P + P], chunks(X)[:, c, :], chunks(TT)[:, c, :],
                                              start=True, stop=True)
                    mm.then_inc(S(f"inv_tct_ready{g}"), 1)

        def inv_act(act, r, bufs):
            for li in range(1, 7):
                for g, (MT, Tt, TT, X, Cm) in enumerate(bufs):
                    act.wait_ge(S(f"inv_x_ready{g}"), 6 * r + li)
                    nc.scalar.activation(X, bank[g][:, :], ACT.Copy).then_inc(S(f"inv_x{g}"), 1)

        def inv_pool(pool, r, bufs):
            for li in range(7):
                for g, (MT, Tt, TT, X, Cm) in enumerate(bufs):
                    pool.wait_ge(S(f"inv_mt{g}"), r + 1)
                    if li == 1:
                        pool.wait_ge(S(f"inv_tt{g}"), 7 * r + 1)
                    if li > 1:
                        pool.wait_ge(S(f"inv_x_ready{g}"), 6 * r + li - 1)
                    nc.gpsimd.tensor_tensor(chunks(Cm), chunks(MT), over4(lvl[li]), ALU.mult).then_inc(S(f"inv_c{g}"), 1)

        def inv_dve(dve, r, bufs):
            for g, (MT, Tt, TT, X, Cm) in enumerate(bufs):
                dve.wait_ge(S(f"inv_c{g}"), 7 * r + 1)
                nc.vector.tensor_tensor(chunks(TT), over4(ident), chunks(Cm), ALU.subtract).then_inc(S(f"inv_tt{g}"), 1)
            for g, (MT, Tt, TT, X, Cm) in enumerate(bufs):
                dve.wait_ge(S(f"inv_t_ready{g}"), r + 1)
                nc.vector.tensor_copy(Tt, bank[g][:, :]).then_inc(S(f"inv_t{g}"), 1)
            for li in range(1, 7):
                for g, (MT, Tt, TT, X, Cm) in enumerate(bufs):
                    dve.wait_ge(S(f"inv_tct_ready{g}"), 6 * r + li)
                    if li < 6:
                        dve.wait_ge(S(f"inv_t{g}"), 6 * r + li)
                        nc.vector.tensor_tensor(Tt, Tt, bank[2 + g][:, :], ALU.subtract).then_inc(S(f"inv_t{g}"), 1)
                    dve.wait_ge(S(f"inv_tt{g}"), 7 * r + li)
                    nc.vector.tensor_tensor(TT, TT, bank[4 + g][:, :], ALU.subtract).then_inc(S(f"inv_tt{g}"), 1)
            for g in range(2):
                dve.wait_ge(S(f"inv_tt{g}"), 7 * r + 7)

        W = [work[:, i, :] for i in range(14)]
        X = [extra[:, i, :] for i in range(8)]
        beta8, g8 = W[12][0:8, :], W[13][0:8, :]
        cols = small[:, 16:80].rearrange("p (a c h) -> p a c h", a=2, c=CH)
        glast = small[:, 80:96].rearrange("p (h c) -> p h c", h=AH)
        e_glast = small[:, 96:112].rearrange("p (h c) -> p h c", h=AH)
        e_rest = small[:, 112:128].rearrange("p (h c) -> p h c", h=AH)
        e_col = small[:, 128:144].rearrange("p (h c) -> p h c", h=AH)
        nbeta_e = small[:, 144:160].rearrange("p (h c) -> p h c", h=AH)
        a_neg = small[0:8, 0:1]
        a_inv = [(hT[:, 0, :], hT[:, 1, :], None, hT[:, 2, :], hT[:, 3, :]),
                 (hT[:, 4, :], hT[:, 5, :], None, hT[:, 6, :], hT[:, 7, :])]
        PT = X[0:4]
        TTa = X[4:8]
        ktok = W[8:12]
        state = proj[:, 30, :]

        def a_bufs(r):
            return [(MT, Tt, TTa[2 * r + g], Xb, Cm) for g, (MT, Tt, _, Xb, Cm) in enumerate(a_inv)]

        def delta_dve(dve, step):
            dve.wait_ge(S("tile_free0"), 2 + 15)
            dve.wait_ge(S("tile_free1"), 2 + 15)
            for j in range(12):
                cv, p = W[j % 2], proj[:, j, :]
                if j >= 2:
                    dve.wait_ge(S("a_silu"), j - 1)
                step(nc.vector.tensor_scalar(cv, p, pc("conv", 4 * j + 3), None, ALU.mult))
                for s in range(1, 4):
                    ins = nc.vector.scalar_tensor_tensor(out=cv[:, s:T], in0=p[:, 0:T - s], scalar=pc("conv", 4 * j + 3 - s),
                                                         in1=cv[:, s:T], op0=ALU.mult, op1=ALU.add)
                    if s < 3:
                        step(ins)
                ins.then_inc(S("a_conv"), 1)
            for j in range(8):
                p = proj[:, j, :]
                dve.wait_ge(S("head_rstd"), j + 1)
                nc.vector.scalar_tensor_tensor(out=p, in0=p, scalar=(P ** -0.5 if j < 4 else 1.0), in1=W[6 + j % 2],
                                               op0=ALU.mult, op1=ALU.mult).then_inc(S("a_unit"), 1)
            dve.wait_ge(S("a_unit"), 8)
            dve.wait_ge(S("a_softplus"), 1)
            z, l = W[9][0:8, :], W[11][0:8, :]
            step(nc.vector.tensor_scalar(z, z, 0.0, None, ALU.max))
            step(nc.vector.tensor_tensor(z, z, l, ALU.add))
            step(nc.vector.tensor_scalar(z, z, a_neg, -1.0, ALU.mult, ALU.mult))
            nc.vector.tensor_tensor_scan(g8, reset[0:8, :], z, 0.0, ALU.mult, ALU.add).then_inc(S("a_decay"), 1)
            dve.wait_ge(S("a_cols"), 1)
            step(nc.vector.tensor_copy(small[:, 16:80], bank[7][:, 0:64]))
            for r in range(2):
                for g in range(2):
                    h = 2 * r + g
                    dve.wait_ge(S("a_bcast"), h + 1)
                    for c in range(CH):
                        nc.vector.tensor_scalar(chunks(W[g])[:, c, :], chunks(bank[4 + g][:, :])[:, c, :], cols[:, 0, c, h:h + 1],
                                                0.0, ALU.subtract, ALU.min).then_inc(S("a_diff"), 1)
                    step(nc.vector.tensor_copy(glast[:, h, :], bank[4 + g][:, P - 1:T:P]))
                    nc.vector.tensor_tensor(e_rest[:, h, :], glast[:, h, :], cols[:, 0, :, h], ALU.subtract).then_inc(S("a_diff"), 1)
                    nc.vector.tensor_tensor(W[2 + g], proj[:, 4 + h, :], bank[6 + g][:, :], ALU.mult).then_inc(S("a_diff"), 1)
                for g in range(2):
                    h = 2 * r + g
                    dve.wait_ge(S("a_exps"), h + 1)
                    step(nc.vector.tensor_tensor(chunks(W[6 + g]), chunks(W[g]), over4(incl), ALU.mult))
                    dve.wait_ge(S("a_scores"), h + 1)
                    nc.vector.tensor_tensor(a_inv[g][0], bank[g][:, :], W[g], ALU.mult).then_inc(S(f"inv_mt{g}"), 1)
                    step(nc.vector.tensor_tensor(PT[h], bank[2 + g][:, :], W[6 + g], ALU.mult))
                    step(nc.vector.tensor_tensor(proj[:, h, :], proj[:, h, :], W[4 + g], ALU.mult))
                    step(nc.vector.scalar_tensor_tensor(out=nbeta_e[:, h, :], in0=e_col[:, h, :], scalar=-1.0,
                                                        in1=cols[:, 1, :, 4 + h], op0=ALU.mult, op1=ALU.mult))
                for g in range(2):
                    h = 2 * r + g
                    dve.wait_ge(S("a_turned"), h + 1)
                    for c in range(CH):
                        nc.vector.tensor_scalar(chunks(ktok[h])[:, c, :], chunks(bank[4 + g][:, :])[:, c, :],
                                                e_rest[:, h, c:c + 1], None, ALU.mult)
                        ins = nc.vector.tensor_scalar(chunks(proj[:, 8 + h, :])[:, c, :], chunks(bank[6 + g][:, :])[:, c, :],
                                                      cols[:, 1, c, 4 + h:5 + h], None, ALU.mult)
                    ins.then_inc(S("a_tok"), 1)
                dve.wait_ge(S("a_tok"), 2 * r + 2)
                inv_dve(dve, r, a_bufs(r))
            for c in range(CH):
                if c > 0:
                    dve.wait_ge(S("a_ks"), c)
                    for h in range(AH):
                        nc.vector.scalar_tensor_tensor(
                            out=W[c % 2][:, h * P:h * P + P], in0=bank[0][:, h * P:h * P + P], scalar=nbeta_e[:, h, c:c + 1],
                            in1=chunks(proj[:, 8 + h, :])[:, c, :], op0=ALU.mult, op1=ALU.add).then_inc(S("a_r"), 1)
                if c < CH - 1:
                    dve.wait_ge(S("a_out"), c + 1)
                    if c == 0:
                        nc.vector.tensor_copy(state, bank[3][:, :]).then_inc(S("a_state"), 1)
                    else:
                        for h in range(AH):
                            sl = state[:, h * P:h * P + P]
                            ins = nc.vector.scalar_tensor_tensor(out=sl, in0=sl, scalar=e_glast[:, h, c:c + 1],
                                                                 in1=bank[3][:, h * P:h * P + P], op0=ALU.mult, op1=ALU.add)
                            if h < AH - 1:
                                step(ins)
                        ins.then_inc(S("a_state"), 1)
                    dve.wait_ge(S("a_state"), c + 1)
            for h in range(AH):
                o = hT[:, h, :]
                dve.wait_ge(S("head_rstd"), h + 1 + 8)
                step(nc.vector.scalar_tensor_tensor(out=o, in0=o, scalar=pc("onA"), in1=W[6 + h % 2], op0=ALU.mult, op1=ALU.mult))
                nc.vector.tensor_tensor(o, o, proj[:, 12 + h, :], ALU.mult).then_inc(S("a_done"), 1)
            dve.wait_ge(S("a_done"), AH)

        def delta_act(act, step):
            act.wait_ge(S("tile_free0"), 2 + 15)
            act.wait_ge(S("tile_free1"), 2 + 15)
            for j in range(12):
                act.wait_ge(S("a_conv"), j + 1)
                nc.scalar.activation(proj[:, j, :], W[j % 2], ACT.Silu).then_inc(S("a_silu"), 1)
            for h in range(AH):
                nc.scalar.activation(proj[:, 12 + h, :], proj[:, 12 + h, :], ACT.Silu).then_inc(S("a_silu"), 1)
            act.wait_ge(S("a_silu"), 16)
            act.wait_ge(S("a_db"), 1)
            step(nc.scalar.activation(beta8, bank[6][0:8, :], ACT.Sigmoid))
            step(nc.scalar.activation(W[9][0:8, :], bank[6][0:8, :], ACT.Identity, bias=pc("dt", 0, 8)))
            step(nc.scalar.activation(W[10][0:8, :], W[9][0:8, :], ACT.Abs))
            step(nc.scalar.activation(W[10][0:8, :], W[10][0:8, :], ACT.Exp, scale=-1.0))
            step(nc.scalar.activation(W[11][0:8, :], W[10][0:8, :], ACT.Ln, bias=con[0:8, C_ONE:C_ONE + 1]))
            nc.scalar.activation(a_neg, pc("alog", 0, 8), ACT.Exp).then_inc(S("a_softplus"), 1)
            act.wait_ge(S("a_softplus"), 1)
            for j in range(9):
                if j < 8:
                    if j >= 2:
                        act.wait_ge(S("head_summed"), j - 1)
                    nc.scalar.activation(W[2 + j % 2], proj[:, j, :], ACT.Square).then_inc(S("head_squared"), 1)
                if j > 0:
                    act.wait_ge(S("head_summed"), j)
                    if j > 2:
                        act.wait_ge(S("a_unit"), j - 2)
                    step(nc.scalar.activation(W[4], bank[4 + (j - 1) % 2][:, :], ACT.Ln, bias=eps6))
                    nc.scalar.activation(W[6 + (j - 1) % 2], W[4], ACT.Exp, scale=-0.5).then_inc(S("head_rstd"), 1)
                    act.wait_ge(S("head_rstd"), j)
            for r in range(2):
                for g in range(2):
                    h = 2 * r + g
                    act.wait_ge(S("a_diff"), 6 * h + 6)
                    step(nc.scalar.activation(W[4 + g], bank[4 + g][:, :], ACT.Exp))
                    step(nc.scalar.activation(W[g], W[g], ACT.Exp))
                    step(nc.scalar.activation(e_glast[:, h, :], glast[:, h, :], ACT.Exp))
                    step(nc.scalar.activation(e_rest[:, h, :], e_rest[:, h, :], ACT.Exp))
                    nc.scalar.activation(e_col[:, h, :], cols[:, 0, :, h], ACT.Exp).then_inc(S("a_exps"), 1)
                inv_act(act, r, a_bufs(r))
            for c in range(CH):
                act.wait_ge(S("a_v"), c + 1)
                nc.scalar.activation(W[2 + c % 2], bank[1][:, :], ACT.Copy).then_inc(S("a_vnew"), 1)
                act.wait_ge(S("a_out"), c + 1)
                nc.scalar.activation(hT[:, 0:4, c * P:c * P + P], chunks(bank[2][:, :]), ACT.Copy).then_inc(S("a_o"), 1)
            act.wait_ge(S("a_o"), CH)
            for h in range(AH + 1):
                if h < AH:
                    if h >= 2:
                        act.wait_ge(S("head_summed"), h - 1 + 8)
                    nc.scalar.activation(W[4 + h % 2], hT[:, h, :], ACT.Square).then_inc(S("head_squared"), 1)
                if h > 0:
                    act.wait_ge(S("head_summed"), h + 8)
                    if h > 2:
                        act.wait_ge(S("a_done"), h - 2)
                    step(nc.scalar.activation(W[8], bank[4 + (h - 1) % 2][:, :], ACT.Ln, bias=eps6, scale=1.0 / P))
                    nc.scalar.activation(W[6 + (h - 1) % 2], W[8], ACT.Exp, scale=-0.5).then_inc(S("head_rstd"), 1)
                    act.wait_ge(S("head_rstd"), h + 8)

        def delta_pe(pe):
            wdb = par[:, PC["wdb"]:PC["wdb"] + 64].rearrange("p (k n) -> p k n", k=DT)
            for k in range(DT):
                mm = nc.tensor.matmul(bank[6][0:8, :], wdb[:, k, :], hT[:, k, :], start=(k == 0), stop=(k == DT - 1))
            mm.then_inc(S("a_db"), 1)
            for j in range(8):
                pe.wait_ge(S("head_squared"), j + 1)
                if j >= 2:
                    pe.wait_ge(S("head_rstd"), j - 1)
                nc.tensor.matmul(bank[4 + j % 2][:, :], ones, W[2 + j % 2], start=True, stop=True).then_inc(S("head_summed"), 1)
            pe.wait_ge(S("a_decay"), 1)
            for a, rows in enumerate((g8, beta8)):
                for c in range(CH):
                    o = a * 32 + c * 8
                    mm = nc.tensor.transpose(bank[7][:, o:o + 8], rows[:, c * P:c * P + P], ident[0:8, 0:8])
            mm.then_inc(S("a_cols"), 1)
            pe.wait_ge(S("a_unit"), 8)
            pe.wait_ge(S("head_rstd"), 8)
            for r in range(2):
                for g in range(2):
                    h = 2 * r + g
                    if r == 0 and g == 1:
                        pe.wait_ge(S("a_diff"), 5)
                    if r > 0:
                        pe.wait_ge(S("a_tok"), 2 * r)
                        pe.wait_ge(S(f"inv_tt{g}"), 7 * r)
                    nc.tensor.matmul(bank[4 + g][:, :], sel8[h], g8, start=True, stop=True)
                    nc.tensor.matmul(bank[6 + g][:, :], sel8[4 + h], beta8, start=True, stop=True).then_inc(S("a_bcast"), 1)
                for g in range(2):
                    h = 2 * r + g
                    pe.wait_ge(S("a_diff"), 6 * h + 6)
                    for c in range(CH):
                        k = chunks(proj[:, 4 + h, :])[:, c, :]
                        nc.tensor.matmul(bank[g][:, c * P:c * P + P], k, chunks(W[2 + g])[:, c, :], start=True, stop=True)
                        mm = nc.tensor.matmul(bank[2 + g][:, c * P:c * P + P], k, chunks(proj[:, h, :])[:, c, :],
                                              start=True, stop=True)
                    mm.then_inc(S("a_scores"), 1)
                for g in range(2):
                    h = 2 * r + g
                    pe.wait_ge(S("a_exps"), h + 1)
                    for c in range(CH):
                        nc.tensor.transpose(bank[4 + g][:, c * P:c * P + P], chunks(proj[:, 4 + h, :])[:, c, :], ident)
                        mm = nc.tensor.transpose(bank[6 + g][:, c * P:c * P + P], chunks(proj[:, 8 + h, :])[:, c, :], ident)
                    mm.then_inc(S("a_turned"), 1)
                pe.wait_ge(S("a_tok"), 2 * r + 2)
                inv_pe(pe, r, a_bufs(r))
            for g in range(2):
                pe.wait_ge(S(f"inv_tt{g}"), 14)
            for c in range(CH):
                if c > 0:
                    pe.wait_ge(S("a_state"), c)
                    for h in range(AH):
                        mm = nc.tensor.matmul(bank[0][:, h * P:h * P + P], chunks(proj[:, 4 + h, :])[:, c, :],
                                              state[:, h * P:h * P + P], start=True, stop=True)
                    mm.then_inc(S("a_ks"), 1)
                    pe.wait_ge(S("a_r"), AH * c)
                for h in range(AH):
                    r_h = W[c % 2][:, h * P:h * P + P] if c > 0 else chunks(proj[:, 8 + h, :])[:, 0, :]
                    mm = nc.tensor.matmul(bank[1][:, h * P:h * P + P], chunks(TTa[h])[:, c, :], r_h, start=True, stop=True)
                mm.then_inc(S("a_v"), 1)
                pe.wait_ge(S("a_vnew"), c + 1)
                if c > 0:
                    pe.wait_ge(S("a_o"), c)
                for h in range(AH):
                    v = W[2 + c % 2][:, h * P:h * P + P]
                    if c > 0:
                        nc.tensor.matmul(bank[2][:, h * P:h * P + P], state[:, h * P:h * P + P], chunks(proj[:, h, :])[:, c, :],
                                         start=True, stop=False)
                    nc.tensor.matmul(bank[2][:, h * P:h * P + P], v, chunks(PT[h])[:, c, :], start=(c == 0), stop=True)
                for h in range(AH):
                    v = W[2 + c % 2][:, h * P:h * P + P]
                    mm = nc.tensor.matmul(bank[3][:, h * P:h * P + P], chunks(ktok[h])[:, c, :], v, start=True, stop=True)
                mm.then_inc(S("a_out"), 1)
            for h in range(AH):
                pe.wait_ge(S("head_squared"), h + 1 + 8)
                if h >= 2:
                    pe.wait_ge(S("head_rstd"), h - 1 + 8)
                nc.tensor.matmul(bank[4 + h % 2][:, :], ones, W[4 + h % 2], start=True, stop=True).then_inc(S("head_summed"), 1)

        E_HALF = float(np.exp(-0.5))
        KR = work[:, 2:4, :].rearrange("p a n -> p (a n)").rearrange("p (c x n) -> p c x n", c=CH, x=2)
        KM, BM, VT, KMT, BMT, Rb, Yb = W[4], W[5], W[6], W[7], W[8], W[9], W[10]
        Zb = W[11][:, 0:P]
        egm = small[:, 160:164]
        engm = small[:, 164:168]
        omka = small[:, 168:172]
        b_inv = [tuple(X[0:5]), (X[5], X[6], X[7], proj[:, 30, :], proj[:, 31, :])]

        def b_scores(q, g):
            return (W[12], W[13], proj[:, 28, :]) if g == 0 else (proj[:, 29, :], proj[:, q, :], proj[:, 12 + q, :])

        def mid(q):
            return proj[:, q, 63:T:P]

        def rwkv_dve(dve, step):
            for n, j in enumerate([12, 13] + list(range(12))):
                p, d = proj[:, 16 + j, :], W[n % 2]
                step(nc.vector.tensor_tensor(d[:, 1:T], p[:, 0:T - 1], p[:, 1:T], ALU.subtract))
                step(nc.vector.tensor_scalar(d[:, 0:1], p[:, 0:1], -1.0, None, ALU.mult))
                nc.vector.scalar_tensor_tensor(out=p, in0=d, scalar=pc("mu", j), in1=p, op0=ALU.mult,
                                               op1=ALU.add).then_inc(S("b_lerp"), 1)
            dve.wait_ge(S("b_lerp"), 14)
            step(nc.vector.tensor_scalar(omka, par[:, PC["ka"]:PC["ka"] + 4], -1.0, 1.0, ALU.mult, ALU.add))
            for q in range(BT):
                k, kk = proj[:, 20 + q, :], proj[:, 12 + q, :]
                nc.vector.tensor_scalar(kk, k, pc("kk", q), None, ALU.mult).then_inc(S("b_kraw"), 1)
            dve.wait_ge(S("b_kraw"), 4)
            for q in range(BT):
                g, b, k, kk = proj[:, q, :], proj[:, 4 + q, :], proj[:, 20 + q, :], proj[:, 12 + q, :]
                dve.wait_ge(S("b_rates"), q + 1)
                step(nc.vector.tensor_scalar(W[0], g, -E_HALF, None, ALU.mult))
                step(nc.vector.tensor_tensor_scan(g, reset, W[0], 0.0, ALU.mult, ALU.add))
                step(nc.vector.tensor_scalar(W[1], b, pc("ka", q), omka[:, q:q + 1], ALU.mult, ALU.add))
                step(nc.vector.tensor_tensor(k, k, W[1], ALU.mult))
                dve.wait_ge(S("head_rstd"), q + 1 + 12)
                nc.vector.tensor_tensor(kk, kk, W[8 + q % 2], ALU.mult).then_inc(S("b_kk"), 1)
                dve.wait_ge(S("b_kk"), q + 1)
                step(nc.vector.tensor_tensor(b, b, kk, ALU.mult))
            for q in range(BT):
                g, b, k, kk, rr = proj[:, q, :], proj[:, 4 + q, :], proj[:, 20 + q, :], proj[:, 12 + q, :], proj[:, 16 + q, :]
                nc.vector.tensor_tensor(chunks(W[0]), chunks(g), mid(q).unsqueeze(2).broadcast_to([P, CH, P]),
                                        ALU.subtract).then_inc(S("b_diff"), 1)
                dve.wait_ge(S("b_exps"), q + 1)
                step(nc.vector.tensor_tensor(KR[:, :, 1, :], chunks(rr), chunks(W[1]), ALU.mult))
                step(nc.vector.tensor_tensor(KR[:, :, 0, 1:P], chunks(kk)[:, :, 1:P], chunks(W[1])[:, :, 0:P - 1], ALU.mult))
                step(nc.vector.tensor_tensor(KR[:, :, 0, 0], kk[:, 0:T:P], engm, ALU.mult))
                step(nc.vector.tensor_tensor(KM, k, Rb, ALU.mult))
                nc.vector.tensor_tensor(BM, b, Rb, ALU.mult).then_inc(S("b_scaled"), 1)
                for g2 in range(2):
                    strict_v, with_y, with_v = b_scores(q, g2)
                    dve.wait_ge(S("b_scores"), 2 * q + g2 + 1)
                    for cc in range(2):
                        by, bv = bank[4 * g2 + cc][:, :], bank[4 * g2 + 2 + cc][:, :]
                        by = by.rearrange("p (c x n) -> p c x n", c=2, x=2)
                        bv = bv.rearrange("p (c x n) -> p c x n", c=2, x=2)
                        two = slice(2 * cc, 2 * cc + 2)
                        m_i = incl.unsqueeze(1).broadcast_to([P, 2, P])
                        m_s = strict.unsqueeze(1).broadcast_to([P, 2, P])
                        step(nc.vector.tensor_tensor(chunks(with_y)[:, two, :], by[:, :, 1, :], m_i, ALU.mult))
                        step(nc.vector.tensor_tensor(chunks(strict_v)[:, two, :], bv[:, :, 0, :], m_s, ALU.mult))
                        step(nc.vector.tensor_tensor(chunks(with_v)[:, two, :], bv[:, :, 1, :], m_i, ALU.mult))
                        ins = nc.vector.tensor_copy(chunks(b_inv[g2][0])[:, two, :], by[:, :, 0, :])
                        if cc == 0:
                            step(ins)
                    ins.then_inc(S(f"inv_mt{g2}"), 1)
                    dve.wait_ge(S(f"inv_mt{g2}"), 2 + q + 1)
                inv_dve(dve, 2 + q, b_inv)
                for c in range(CH):
                    dve.wait_ge(S("b_r"), CH * q + c + 1)
                    nc.vector.tensor_copy(Rb[:, 0:P], bank[0][:, 0:P]).then_inc(S("b_rset"), 1)
                    dve.wait_ge(S("b_y"), CH * q + c + 1)
                    nc.vector.tensor_scalar(Yb[:, 0:P], bank[1][:, 0:P], -1.0, None, ALU.mult).then_inc(S("b_yset"), 1)
                    dve.wait_ge(S("b_out"), CH * q + c + 1)
                    if c < CH - 1:
                        tmp = W[11][:, P:2 * P]
                        step(nc.vector.tensor_tensor(tmp, bank[3][:, 0:P], bones, ALU.mult))
                        if c > 0:
                            step(nc.vector.tensor_tensor(tmp, tmp, Zb, ALU.add))
                        nc.vector.tensor_scalar(Zb, tmp, W[1][:, c * P + P - 1:c * P + P], egm[:, c + 1:c + 2], ALU.mult,
                                                ALU.mult).then_inc(S("b_state"), 1)
                        dve.wait_ge(S("b_state"), (CH - 1) * q + c + 1)
            for q in range(BT):
                o = hT[:, 4 + q, :]
                dve.wait_ge(S("b_mean"), q + 1)
                nc.vector.scalar_tensor_tensor(out=o, in0=bank[4][:, :], scalar=-1.0 / 64, in1=o, op0=ALU.mult,
                                               op1=ALU.add).then_inc(S("b_centred"), 1)
                nc.vector.scalar_tensor_tensor(out=W[0], in0=proj[:, 16 + q, :], scalar=pc("rk", q), in1=proj[:, 20 + q, :],
                                               op0=ALU.mult, op1=ALU.mult).then_inc(S("b_rk"), 1)
                dve.wait_ge(S("b_bonus"), q + 1)
                step(nc.vector.tensor_tensor(W[1], bank[6][:, :], proj[:, 24 + q, :], ALU.mult))
                dve.wait_ge(S("head_rstd"), q + 1 + 16)
                step(nc.vector.scalar_tensor_tensor(out=o, in0=o, scalar=pc("lnw", q), in1=W[4], op0=ALU.mult, op1=ALU.mult))
                step(nc.vector.scalar_tensor_tensor(out=o, in0=o, scalar=pc("lnb", q), in1=W[1], op0=ALU.add, op1=ALU.add))
                nc.vector.tensor_tensor(o, o, proj[:, 8 + q, :], ALU.mult).then_inc(S("b_done"), 1)
            dve.wait_ge(S("b_done"), BT)

        def rwkv_act(act, step):
            act.wait_ge(S("b_lerp"), 2)
            step(nc.scalar.activation(W[2][0:64, :], proj[0:64, 28, :], ACT.Tanh))
            nc.scalar.activation(W[3], proj[:, 29, :], ACT.Sigmoid).then_inc(S("b_lora"), 1)
            for q in range(BT):
                act.wait_ge(S("b_low"), q + 1)
                step(nc.scalar.activation(proj[:, q, :], bank[q % 2][:, :], ACT.Sigmoid, bias=pc("w0", q)))
                step(nc.scalar.activation(proj[:, 4 + q, :], bank[2 + q % 2][:, :], ACT.Sigmoid, bias=pc("a0", q)))
                nc.scalar.activation(proj[:, 8 + q, :], bank[4 + q % 2][:, :], ACT.Copy).then_inc(S("b_rates"), 1)
            for q in range(BT):
                act.wait_ge(S("b_kraw"), q + 1)
                if q > 1:
                    act.wait_ge(S("head_summed"), q - 1 + 12)
                nc.scalar.activation(W[4 + q % 2], proj[:, 12 + q, :], ACT.Square).then_inc(S("head_squared"), 1)
                act.wait_ge(S("head_summed"), q + 1 + 12)
                step(nc.scalar.activation(W[6], bank[6 + q % 2][:, :], ACT.Ln, bias=eps6))
                if q > 1:
                    act.wait_ge(S("b_kk"), q - 1)
                nc.scalar.activation(W[8 + q % 2], W[6], ACT.Exp, scale=-0.5).then_inc(S("head_rstd"), 1)
                act.wait_ge(S("head_rstd"), q + 1 + 12)
            for q in range(BT):
                act.wait_ge(S("b_diff"), q + 1)
                step(nc.scalar.activation(W[1], W[0], ACT.Exp))
                step(nc.scalar.activation(Rb, W[0], ACT.Exp, scale=-1.0))
                step(nc.scalar.activation(egm, mid(q), ACT.Exp))
                nc.scalar.activation(engm, mid(q), ACT.Exp, scale=-1.0).then_inc(S("b_exps"), 1)
                act.wait_ge(S("b_turned"), q + 1)
                step(nc.scalar.activation(VT, bank[4][:, :], ACT.Copy))
                step(nc.scalar.activation(KMT, bank[5][:, :], ACT.Copy))
                nc.scalar.activation(BMT, bank[6][:, :], ACT.Copy).then_inc(S("b_tok"), 1)
                inv_act(act, 2 + q, b_inv)
                for c in range(CH):
                    act.wait_ge(S("b_out"), CH * q + c + 1)
                    nc.scalar.activation(hT[:, 4 + q, c * P:c * P + P], bank[2][:, 0:P], ACT.Copy).then_inc(S("b_o"), 1)
            act.wait_ge(S("b_o"), CH * BT)
            for q in range(BT):
                act.wait_ge(S("b_centred"), q + 1)
                nc.scalar.activation(W[5], hT[:, 4 + q, :], ACT.Square).then_inc(S("head_squared"), 1)
                act.wait_ge(S("head_summed"), q + 1 + 16)
                step(nc.scalar.activation(W[6], bank[5][:, :], ACT.Ln, bias=epsg, scale=1.0 / 64))
                if q > 0:
                    act.wait_ge(S("b_done"), q)
                nc.scalar.activation(W[4], W[6], ACT.Exp, scale=-0.5).then_inc(S("head_rstd"), 1)

        def rwkv_pe(pe):
            w2 = par[0:64, PC["w2a2"]:PC["w2a2"] + 512]
            a2 = par[64:128, PC["w2a2"]:PC["w2a2"] + 512]
            g2w = par[:, PC["g2"]:PC["g2"] + 512]
            pe.wait_ge(S("b_lora"), 1)
            pe.wait_ge(S("a_done"), AH)
            for q in range(BT):
                if q > 1:
                    pe.wait_ge(S("b_rates"), q - 1)
                nc.tensor.matmul(bank[q % 2][:, :], w2[:, q * P:q * P + P], W[2][0:64, :], start=True, stop=True)
                nc.tensor.matmul(bank[2 + q % 2][:, :], a2[:, q * P:q * P + P], proj[64:128, 28, :], start=True, stop=True)
                nc.tensor.matmul(bank[4 + q % 2][:, :], g2w[:, q * P:q * P + P], W[3], start=True,
                                 stop=True).then_inc(S("b_low"), 1)
            for q in range(BT):
                pe.wait_ge(S("head_squared"), q + 1 + 12)
                if q > 1:
                    pe.wait_ge(S("head_rstd"), q - 1 + 12)
                nc.tensor.matmul(bank[6 + q % 2][:, :], bones, W[4 + q % 2], start=True, stop=True).then_inc(S("head_summed"), 1)
            pe.wait_ge(S("b_rates"), 4)
            pe.wait_ge(S("head_rstd"), 4 + 12)
            for q in range(BT):
                pe.wait_ge(S("b_scaled"), q + 1)
                if q > 0:
                    pe.wait_ge(S("b_o"), CH * q)
                for g in range(2):
                    sl = slice(64 * g, 64 * g + 64)
                    for c in range(CH):
                        o = slice((c % 2) * 256, (c % 2) * 256 + 256)
                        kr = KR[sl, c, :, :].rearrange("p x n -> p (x n)")
                        nc.tensor.matmul(bank[4 * g + c // 2][:, o], chunks(BM)[sl, c, :], kr, start=True, stop=True)
                        mm = nc.tensor.matmul(bank[4 * g + 2 + c // 2][:, o], chunks(KM)[sl, c, :], kr, start=True, stop=True)
                    mm.then_inc(S("b_scores"), 1)
                pe.wait_ge(S("inv_mt1"), 2 + q + 1)
                for n, src in enumerate((proj[:, 24 + q, :], KM, BM)):
                    for c in range(CH):
                        mm = nc.tensor.transpose(bank[4 + n][:, c * P:c * P + P], chunks(src)[:, c, :], ident)
                mm.then_inc(S("b_turned"), 1)
                pe.wait_ge(S("b_tok"), q + 1)
                inv_pe(pe, 2 + q, b_inv)
                for g in range(2):
                    pe.wait_ge(S(f"inv_tt{g}"), 7 * (3 + q))
                for c in range(CH):
                    n = CH * q + c
                    (sv0, wy0, wv0), (sv1, wy1, wv1) = b_scores(q, 0), b_scores(q, 1)
                    if c > 0:
                        pe.wait_ge(S("b_state"), (CH - 1) * q + c)
                        nc.tensor.matmul(bank[0][:, 0:P], KR[:, c, 0, :], Zb, start=True, stop=True)
                    for g, sv in enumerate((sv0, sv1)):
                        hs = slice(64 * g, 64 * g + 64)
                        mm = nc.tensor.matmul(bank[0][:, hs], chunks(sv)[:, c, :], chunks(VT)[:, c, hs], start=(c == 0), stop=True,
                                              skip_group_check=True)
                    mm.then_inc(S("b_r"), 1)
                    pe.wait_ge(S("b_rset"), n + 1)
                    for g in range(2):
                        hs = slice(64 * g, 64 * g + 64)
                        mm = nc.tensor.matmul(bank[1][:, hs], chunks(b_inv[g][2])[:, c, :], Rb[:, hs], start=True, stop=True)
                    mm.then_inc(S("b_y"), 1)
                    pe.wait_ge(S("b_yset"), n + 1)
                    if n > 0:
                        pe.wait_ge(S("b_o"), n)
                    if c > 0:
                        nc.tensor.matmul(bank[2][:, 0:P], Zb, KR[:, c, 1, :], start=True, stop=True)
                    for g, (wy, wv) in enumerate(((wy0, wv0), (wy1, wv1))):
                        hs = slice(64 * g, 64 * g + 64)
                        nc.tensor.matmul(bank[2][hs, 0:P], chunks(VT)[:, c, hs], chunks(wv)[:, c, :], start=(c == 0), stop=(c > 0),
                                         skip_group_check=True)
                        nc.tensor.matmul(bank[2][hs, 0:P], Yb[:, hs], chunks(wy)[:, c, :], start=False, stop=True,
                                         skip_group_check=True)
                    nc.tensor.matmul(bank[3][:, 0:P], chunks(KMT)[:, c, :], chunks(VT)[:, c, :], start=True, stop=False)
                    nc.tensor.matmul(bank[3][:, 0:P], chunks(BMT)[:, c, :], Yb[:, 0:P], start=False,
                                     stop=True).then_inc(S("b_out"), 1)
            pe.wait_ge(S("b_o"), CH * BT)
            for q in range(BT):
                o = hT[:, 4 + q, :]
                nc.tensor.matmul(bank[4][:, :], bones, o, start=True, stop=True).then_inc(S("b_mean"), 1)
                pe.wait_ge(S("b_rk"), q + 1)
                nc.tensor.matmul(bank[6][:, :], bones, W[0], start=True, stop=True).then_inc(S("b_bonus"), 1)
                pe.wait_ge(S("head_squared"), q + 1 + 16)
                nc.tensor.matmul(bank[5][:, :], bones, W[5], start=True, stop=True).then_inc(S("head_summed"), 1)
                pe.wait_ge(S("head_rstd"), q + 1 + 16)
                pe.wait_ge(S("b_done"), q + 1)

        Dt, Et, Qs, Ks = W[0:3], W[3:6], W[6:9], X[0:3]
        ACC, KD, KDT, VTc = X[3:5], W[9:11], [X[5]] * 2, [X[6]] * 2
        St = [X[7]] * 2
        sqt, lnt, rst = W[11], W[12], W[13]
        UN = 8
        UNITS = UN * CHEADS
        sbk = [bank[0], bank[1], bank[7]]

        def ended(u, after):
            h, r = divmod(u - after + 1, UN)
            return [h - 1] if r == 0 and 1 <= h <= CHEADS else []

        def halves(ap, s):
            return ap.rearrange("p (b x s) -> p b x s", x=2, s=s)

        def middle(ap, s):
            return halves(ap, s)[:, :, 0, s - 1:s].broadcast_to([P, T // (2 * s), s])

        lbv, oml = small[:, 200:208], small[:, 208:216]
        eC = small[:, 216:224].rearrange("p (a c) -> p a c", a=2)

        def hgrn_dve(dve, step):
            nc.vector.tensor_tensor(small[:, 192:200], par[:, PC["lb"]:PC["lb"] + 8], par[:, PC["lb"] + 8:PC["lb"] + 16],
                                    ALU.subtract).then_inc(S("c_lb"), 1)
            dve.wait_ge(S("tile_free0"), 2 + B_COUT)
            dve.wait_ge(S("tile_free1"), 2 + B_COUT)
            for h in range(CHEADS):
                f, k = proj[:, 8 + h, :], hT[:, h, :]
                dve.wait_ge(S("c_sig"), h + 1)
                step(nc.vector.tensor_scalar(k, k, oml[:, h:h + 1], None, ALU.mult))
                nc.vector.tensor_scalar(f, f, oml[:, h:h + 1], lbv[:, h:h + 1], ALU.mult, ALU.add).then_inc(S("c_f"), 1)
            for h in range(CHEADS):
                dve.wait_ge(S("c_ln"), h + 1)
                step(nc.vector.tensor_tensor_scan(proj[:, 8 + h, :], reset, W[h], 0.0, ALU.mult, ALU.add))

            def spread(u):
                h, li = divmod(u, UN)
                if li == 7:
                    return
                n, s = 7 * h + li, LEVELS[li]
                g = proj[:, 8 + h, :]
                if n >= 3:
                    dve.wait_ge(S("c_e"), n - 2)
                nc.vector.tensor_tensor(halves(Dt[n % 3], s)[:, :, 1, :], halves(g, s)[:, :, 1, :], middle(g, s), ALU.subtract)
                nc.vector.tensor_tensor(halves(Dt[n % 3], s)[:, :, 0, :], middle(g, s), halves(g, s)[:, :, 0, :],
                                        ALU.subtract).then_inc(S("c_d"), 1)

            def queries(u):
                h, li = divmod(u, UN)
                if li == 7:
                    return
                n, s = 7 * h + li, LEVELS[li]
                dve.wait_ge(S("c_e"), n + 1)
                if n >= 3:
                    dve.wait_ge(S("c_s"), u - 2 - (1 if li < 3 and h > 0 else 0))
                nc.vector.tensor_tensor(halves(Qs[n % 3], s)[:, :, 1, :], halves(proj[:, h, :], s)[:, :, 1, :],
                                        halves(Et[n % 3], s)[:, :, 1, :], ALU.mult).then_inc(S("c_q"), 1)

            def gather(u):
                h, li = divmod(u, UN)
                acc = chunks(ACC[h % 2])
                if li == 0:
                    if h >= 2:
                        dve.wait_ge(S("c_o"), h - 1)
                    step(nc.vector.memset(ACC[h % 2], 0.0))
                dve.wait_ge(S("c_s"), u + 1)
                m = lvl[li] if li < 7 else ident
                nc.vector.copy_predicated(acc, over4(m).bitcast(I32), chunks(sbk[u % 3][:, :])).then_inc(S("c_acc"), 1)
                dve.wait_ge(S("c_acc"), u + 1)

            def rest(h):
                g = proj[:, 8 + h, :]
                last = chunks(g)[:, :, P - 1:P].broadcast_to([P, CH, P])
                if h >= 2:
                    dve.wait_ge(S("c_turned"), h - 1)
                nc.vector.tensor_tensor(chunks(KD[h % 2]), last, chunks(g), ALU.subtract).then_inc(S("c_rest"), 1)

            def decayed_q(h):
                dve.wait_ge(S("c_tail_e"), h + 1)
                nc.vector.tensor_tensor(proj[:, h, :], proj[:, h, :], proj[:, 8 + h, :], ALU.mult).then_inc(S("c_qg"), 1)

            def states(h):
                dve.wait_ge(S("c_incr"), h + 1)
                if h >= 1:
                    dve.wait_ge(S("c_o"), h)
                st = chunks(St[h % 2])
                step(nc.vector.tensor_copy(st[:, 1, :], bank[4][:, 0:P]))
                step(nc.vector.scalar_tensor_tensor(out=st[:, 2, :], in0=st[:, 1, :], scalar=eC[:, h % 2, 1:2],
                                                    in1=bank[4][:, P:2 * P], op0=ALU.mult, op1=ALU.add))
                nc.vector.scalar_tensor_tensor(out=st[:, 3, :], in0=st[:, 2, :], scalar=eC[:, h % 2, 2:3],
                                               in1=bank[4][:, 2 * P:3 * P], op0=ALU.mult, op1=ALU.add).then_inc(S("c_state"), 1)

            def close(h):
                o = hT[:, h, :]
                dve.wait_ge(S("head_rstd"), h + 1 + 20)
                step(nc.vector.scalar_tensor_tensor(out=o, in0=o, scalar=pc("onC"), in1=rst, op0=ALU.mult, op1=ALU.mult))
                nc.vector.tensor_tensor(o, o, proj[:, 24 + h, :], ALU.mult).then_inc(S("c_done"), 1)

            spread(0)
            spread(1)
            for u in range(UNITS + 12):
                if u + 2 < UNITS:
                    spread(u + 2)
                if u < UNITS:
                    queries(u)
                if 0 <= u - 2 < UNITS:
                    gather(u - 2)
                for h in ended(u, 1):
                    rest(h)
                for h in ended(u, 3):
                    decayed_q(h)
                for h in ended(u, 6):
                    states(h)
                for h in ended(u, 11):
                    close(h)
            dve.wait_ge(S("c_done"), CHEADS)

        def hgrn_act(act, step):
            act.wait_ge(S("c_lb"), 1)
            step(nc.scalar.activation(lbv, small[:, 192:200], ACT.Sigmoid, scale=-1.0))
            step(nc.scalar.activation(oml, small[:, 192:200], ACT.Sigmoid))
            act.wait_ge(S("tile_free0"), 2 + B_COUT)
            act.wait_ge(S("tile_free1"), 2 + B_COUT)
            for h in range(CHEADS):
                nc.scalar.activation(hT[:, h, :], proj[:, 8 + h, :], ACT.Sigmoid, scale=-1.0).then_inc(S("c_sigk"), 1)
                act.wait_ge(S("c_sigk"), h + 1)
                nc.scalar.activation(proj[:, 8 + h, :], proj[:, 8 + h, :], ACT.Sigmoid).then_inc(S("c_sig"), 1)
            for h in range(CHEADS):
                step(nc.scalar.activation(proj[:, h, :], proj[:, h, :], ACT.Silu))
                nc.scalar.activation(proj[:, 24 + h, :], proj[:, 24 + h, :], ACT.Silu).then_inc(S("c_silu"), 1)
            act.wait_ge(S("c_silu"), CHEADS)
            for h in range(CHEADS):
                act.wait_ge(S("c_f"), h + 1)
                nc.scalar.activation(W[h], proj[:, 8 + h, :], ACT.Ln).then_inc(S("c_ln"), 1)

            def exps(u):
                h, li = divmod(u, UN)
                if li == 7:
                    return
                n = 7 * h + li
                act.wait_ge(S("c_d"), n + 1)
                if n >= 3:
                    act.wait_ge(S("c_q"), n - 2)
                    act.wait_ge(S("c_k"), n - 2)
                nc.scalar.activation(Et[n % 3], Dt[n % 3], ACT.Exp).then_inc(S("c_e"), 1)

            exps(0)
            exps(1)
            for u in range(UNITS + 12):
                if u + 2 < UNITS:
                    exps(u + 2)
                for h in ended(u, 2):
                    act.wait_ge(S("c_rest"), h + 1)
                    step(nc.scalar.activation(KD[h % 2], KD[h % 2], ACT.Exp))
                    if h >= 2:
                        act.wait_ge(S("c_state"), h - 1)
                    step(nc.scalar.activation(eC[:, h % 2, :], proj[:, 8 + h, P - 1:T:P], ACT.Exp))
                    nc.scalar.activation(proj[:, 8 + h, :], proj[:, 8 + h, :], ACT.Exp).then_inc(S("c_tail_e"), 1)
                for h in ended(u, 4):
                    act.wait_ge(S("c_turned"), h + 1)
                    if h >= 1:
                        act.wait_ge(S("c_o"), h)
                    step(nc.scalar.activation(KDT[h % 2], bank[2][:, :], ACT.Copy))
                    nc.scalar.activation(VTc[h % 2], bank[3][:, :], ACT.Copy).then_inc(S("c_tok"), 1)
                for h in ended(u, 8):
                    act.wait_ge(S("c_o"), h + 1)
                    nc.scalar.activation(hT[:, h, :], bank[5][:, :], ACT.Copy).then_inc(S("c_oset"), 1)
                    act.wait_ge(S("c_oset"), h + 1)
                    nc.scalar.activation(sqt, hT[:, h, :], ACT.Square).then_inc(S("head_squared"), 1)
                for h in ended(u, 10):
                    act.wait_ge(S("head_summed"), h + 1 + 20)
                    step(nc.scalar.activation(lnt, bank[6][:, :], ACT.Ln, bias=eps6, scale=1.0 / P))
                    if h > 0:
                        act.wait_ge(S("c_done"), h)
                    nc.scalar.activation(rst, lnt, ACT.Exp, scale=-0.5).then_inc(S("head_rstd"), 1)

        def hgrn_pool(pool):
            for u in range(UNITS + 12):
                h, li = divmod(u, UN)
                if u < UNITS and li < 7:
                    n, s = 7 * h + li, LEVELS[li]
                    pool.wait_ge(S("c_e"), n + 1)
                    if n >= 3:
                        pool.wait_ge(S("c_s"), u - 2 - (1 if li < 3 and h > 0 else 0))
                    nc.gpsimd.tensor_tensor(halves(Ks[n % 3], s)[:, :, 0, :], halves(hT[:, h, :], s)[:, :, 0, :],
                                            halves(Et[n % 3], s)[:, :, 0, :], ALU.mult).then_inc(S("c_k"), 1)
                for h in ended(u, 3):
                    pool.wait_ge(S("c_tail_e"), h + 1)
                    nc.gpsimd.tensor_tensor(KD[h % 2], KD[h % 2], hT[:, h, :], ALU.mult).then_inc(S("c_kd"), 1)

        def hgrn_pe(pe):
            pe.wait_ge(S("c_silu"), CHEADS)
            pe.wait_ge(S("c_f"), CHEADS)
            for u in range(UNITS + 12):
                if u < UNITS:
                    h, li = divmod(u, UN)
                    if u >= 3:
                        pe.wait_ge(S("c_acc"), u - 2)
                    n = 7 * h + li
                    k, q = hT[:, h, :], proj[:, h, :]
                    if li < 7:
                        pe.wait_ge(S("c_q"), n + 1)
                        pe.wait_ge(S("c_k"), n + 1)
                        k, q = Ks[n % 3], Qs[n % 3]
                    for c in range(CH):
                        mm = nc.tensor.matmul(sbk[u % 3][:, c * P:c * P + P], chunks(k)[:, c, :], chunks(q)[:, c, :],
                                              start=True, stop=True)
                    mm.then_inc(S("c_s"), 1)
                for h in ended(u, 3):
                    if h > 0:
                        pe.wait_ge(S("c_tok"), h)
                    for c in range(CH):
                        nc.tensor.transpose(bank[3][:, c * P:c * P + P], chunks(proj[:, 16 + h, :])[:, c, :], ident)
                    pe.wait_ge(S("c_kd"), h + 1)
                    for c in range(CH):
                        mm = nc.tensor.transpose(bank[2][:, c * P:c * P + P], chunks(KD[h % 2])[:, c, :], ident)
                    mm.then_inc(S("c_turned"), 1)
                for h in ended(u, 5):
                    pe.wait_ge(S("c_tok"), h + 1)
                    if h > 0:
                        pe.wait_ge(S("c_state"), h)
                    for c in range(CH - 1):
                        mm = nc.tensor.matmul(bank[4][:, c * P:c * P + P], chunks(KDT[h % 2])[:, c, :], chunks(VTc[h % 2])[:, c, :],
                                              start=True, stop=True)
                    mm.then_inc(S("c_incr"), 1)
                for h in ended(u, 7):
                    pe.wait_ge(S("c_state"), h + 1)
                    pe.wait_ge(S("c_qg"), h + 1)
                    pe.wait_ge(S("c_acc"), UN * (h + 1))
                    if h > 0:
                        pe.wait_ge(S("c_oset"), h)
                    for c in range(CH):
                        if c > 0:
                            nc.tensor.matmul(bank[5][:, c * P:c * P + P], chunks(St[h % 2])[:, c, :], chunks(proj[:, h, :])[:, c, :],
                                             start=True, stop=False)
                        mm = nc.tensor.matmul(bank[5][:, c * P:c * P + P], chunks(VTc[h % 2])[:, c, :],
                                              chunks(ACC[h % 2])[:, c, :], start=(c == 0), stop=True)
                    mm.then_inc(S("c_o"), 1)
                for h in ended(u, 9):
                    pe.wait_ge(S("head_squared"), h + 1 + 20)
                    if h > 0:
                        pe.wait_ge(S("head_rstd"), h + 20)
                    nc.tensor.matmul(bank[6][:, :], ones, sqt, start=True, stop=True).then_inc(S("head_summed"), 1)

        memn = proj[:, 24:32, :]
        PX = [work[:, 2 * i:2 * i + 2, :].rearrange("p a (t n) -> p (a t) n", n=M) for i in range(2)]
        PXT = W[4:6]
        mx = small[:, 224:232].rearrange("p (a t) -> p a t", a=2)
        sm = small[:, 232:240].rearrange("p (a t) -> p a t", a=2)
        XSC = (D // XH) ** -0.5

        def sbank(x):
            return [bank[4 + 2 * (x % 2) + i][:, :].rearrange("p (t n) -> p t n", n=M) for i in range(2)]

        def xattn_dve(dve, step, L):
            for x in range(XH):
                n = XH * L + x
                dve.wait_ge(S("x_scores"), n + 1)
                if x >= 1:
                    dve.wait_ge(S("x_probs"), n)
                for i in range(2):
                    step(nc.vector.tensor_reduce(mx[:, x % 2, 2 * i:2 * i + 2], sbank(x)[i], AX.X, ALU.max))
                nc.vector.tensor_scalar(mx[:, x % 2, :], mx[:, x % 2, :], -XSC, None, ALU.mult).then_inc(S("x_max"), 1)
                dve.wait_ge(S("x_exp"), n + 1)
                step(nc.vector.reciprocal(sm[:, x % 2, :], sm[:, x % 2, :]))
                for t in range(CH):
                    ins = nc.vector.tensor_scalar(PX[x % 2][:, t, :], PX[x % 2][:, t, :], sm[:, x % 2, t:t + 1], None, ALU.mult)
                ins.then_inc(S("x_probs"), 1)
                dve.wait_ge(S("x_turned"), n + 1)
                step(nc.vector.tensor_copy(PXT[0], bank[0][:, :]))
                nc.vector.tensor_copy(PXT[1], bank[1][:, :]).then_inc(S("x_pt"), 1)

        def xattn_act(act, step, L):
            def out(x):
                act.wait_ge(S("x_out"), XH * L + x + 1)
                step(nc.scalar.activation(hT[:, 2 * x, :], bank[2][:, :], ACT.Copy))
                nc.scalar.activation(hT[:, 2 * x + 1, :], bank[3][:, :], ACT.Copy).then_inc(S("x_o"), 1)

            for x in range(XH):
                n = XH * L + x
                act.wait_ge(S("x_max"), n + 1)
                if x >= 2:
                    act.wait_ge(S("x_turned"), n - 1)
                for t in range(CH):
                    ins = nc.scalar.activation(PX[x % 2][:, t, :], sbank(x)[t // 2][:, t % 2, :], ACT.Exp, bias=mx[:, x % 2, t:t + 1],
                                               scale=XSC, accum_out=sm[:, x % 2, t:t + 1])
                    if t < CH - 1:
                        step(ins)
                ins.then_inc(S("x_exp"), 1)
                if x > 0:
                    out(x - 1)
            out(XH - 1)

        def xattn_pe(pe, L):
            first = B_XA0 if L == 0 else B_XA1
            pe.wait_ge(S("tile_free0"), 2 + first + 12)
            pe.wait_ge(S("tile_free1"), 2 + first + 12)

            def scores(x):
                if x >= 2:
                    pe.wait_ge(S("x_exp"), XH * L + x - 1)
                for t in range(CH):
                    for d in range(2):
                        mm = nc.tensor.matmul(sbank(x)[t // 2][:, t % 2, :], chunks(proj[:, 16 + 2 * x + d, :])[:, t, :],
                                              proj[:, 2 * x + d, 0:M], start=(d == 0), stop=(d == 1))
                mm.then_inc(S("x_scores"), 1)

            scores(0)
            for x in range(XH):
                n = XH * L + x
                if x + 1 < XH:
                    scores(x + 1)
                pe.wait_ge(S("x_probs"), n + 1)
                if x > 0:
                    pe.wait_ge(S("x_pt"), n)
                for m in range(2):
                    for t in range(CH):
                        mm = nc.tensor.transpose(bank[m][:, t * P:t * P + P], PX[x % 2][:, t, m * P:m * P + P], ident)
                mm.then_inc(S("x_turned"), 1)
                pe.wait_ge(S("x_pt"), n + 1)
                if x > 0:
                    pe.wait_ge(S("x_o"), n)
                for d in range(2):
                    for m in range(2):
                        mm = nc.tensor.matmul(bank[2 + d][:, :], proj[:, 8 + 2 * x + m, d * P:d * P + P], PXT[m],
                                              start=(m == 0), stop=(m == 1))
                mm.then_inc(S("x_out"), 1)
            pe.wait_ge(S("x_o"), XH * (L + 1))

        htok = proj[:, 0:8, :].rearrange("p (t a) n -> p t (a n)", a=2)
        y1 = htok
        y2 = proj[:, 8:16, :].rearrange("p (t a) n -> p t (a n)", a=2)
        xg = [proj[:, 8 + 2 * i:10 + 2 * i, :].rearrange("p a n -> p (a n)") for i in range(2)]
        xgT = [proj[:, 12 + 2 * i:14 + 2 * i, :].rearrange("p a (b n) -> p (a b) n", n=P) for i in range(2)]
        ysb = [proj[:, 16 + 2 * i:18 + 2 * i, :] for i in range(2)]
        hs = [W[i][:, 0:FF] for i in range(2)]
        hid = [W[2 + i][:, 0:FF] for i in range(2)]
        hidT = [W[4 + i][:, 0:FF].rearrange("p (a n) -> p a n", a=2) for i in range(2)]
        w13 = [ring[:, 3 * i:3 * i + 2, :].rearrange("p a n -> p (a n)").rearrange("p (k n) -> p k n", k=DT) for i in range(2)]
        w2e = [ring[:, 3 * i + 2, :].rearrange("p (k n) -> p k n", k=2) for i in range(2)]

        def sm3(o, *dims):
            n = int(np.prod(dims))
            names = ["a", "b", "c"][:len(dims)]
            pat = f"p ({' '.join(names)}) -> p {' '.join(names)}"
            return small[:, o:o + n].rearrange(pat, **dict(zip(names, dims)))

        lg = sm3(256, CH, 20)
        gl, el = lg[:, :, 0:4], lg[:, :, 4:20].rearrange("p t (g i) -> p t g i", g=4)
        oh = sm3(336, CH, NG)
        oh1, oh2 = sm3(352, CH, EG), sm3(368, CH, EG)
        ing, sh = sm3(384, CH, EG), sm3(400, CH, NG)
        wt = sm3(416, CH, 4)
        gmax, gsum, m1, m2 = (small[:, 432 + 4 * i:436 + 4 * i] for i in range(4))
        gate1, gate2, e2, tmp4 = (small[:, 448 + 4 * i:452 + 4 * i] for i in range(4))
        sel1, sel2, sel = sm3(464, CH, NG, EG), sm3(528, CH, NG, EG), sm3(592, CH, NE)
        pre = sm3(656, CH, NE)
        tot = small[:, 720:736]
        nblk, incl_b = small[:, 736:752], small[:, 752:768]
        tmp64 = sm3(768, CH, NE)
        row12 = small[:, 832:840]
        rowbase = small[:, 840:856]
        emapf = small[:, 856:856 + ITEMS]
        rows_i = smalli[:, 0:8]
        emap_i = smalli[:, 8:8 + ITEMS]
        pairs_i = smalli[0:1, 8 + ITEMS:10 + ITEMS]
        pairs_f = small[:, 880:888]

        def item_turns(eng, L):
            def load(l):
                return eng.value_load(pairs_i[:, l:l + 1], min_val=2, max_val=ITEMS // 2)
            return load(L), (load(0) if L else 0)
        cmp = W[6][:, 0:ITEMS * NE].rearrange("p (i e) -> p i e", e=NE)
        wts = con[:, C_WTS:C_WTS + 4]
        iota = con[:, C_IOTA:C_IOTA + ITEMS]

        def bc3(ap, n):
            return ap.unsqueeze(2).broadcast_to([P, CH, n])

        def first_only(step, dst, src, m):
            step(nc.vector.tensor_tensor(dst, src, bc3(m, 4), ALU.is_equal))
            step(nc.vector.tensor_tensor(dst, dst, wts.unsqueeze(1).broadcast_to([P, CH, 4]), ALU.mult))
            step(nc.vector.tensor_reduce(tmp4, dst, AX.X, ALU.max))
            step(nc.vector.tensor_tensor(dst, dst, bc3(tmp4, 4), ALU.is_equal))

        def moe_dve(dve, step, L):
            bge = par[:, PC["bge"] + 20 * L:PC["bge"] + 20 * L + 20]
            dve.wait_ge(S("m_logits"), L + 1)
            step(nc.vector.tensor_tensor(lg, bank[4][:, 0:80].rearrange("p (t n) -> p t n", n=20),
                                         bge.unsqueeze(1).broadcast_to([P, CH, 20]), ALU.add))
            step(nc.vector.tensor_reduce(gmax, gl, AX.X, ALU.max))
            nc.vector.tensor_tensor(sh, gl, bc3(gmax, 4), ALU.subtract).then_inc(S("m_shift"), 1)
            first_only(step, oh, gl, gmax)
            t4 = tmp64.rearrange("p t (g i) -> p t g i", g=4)
            step(nc.vector.tensor_tensor(t4, el, oh.unsqueeze(3).broadcast_to([P, CH, NG, EG]), ALU.mult))
            step(nc.vector.tensor_reduce(ing, t4.rearrange("p t g i -> p t i g"), AX.X, ALU.add))
            step(nc.vector.tensor_reduce(m1, ing, AX.X, ALU.max))
            first_only(step, oh1, ing, m1)
            step(nc.vector.scalar_tensor_tensor(out=wt, in0=oh1, scalar=-1e30, in1=ing, op0=ALU.mult, op1=ALU.add))
            step(nc.vector.tensor_reduce(m2, wt, AX.X, ALU.max))
            first_only(step, oh2, wt, m2)
            nc.vector.tensor_tensor(e2, m2, m1, ALU.subtract).then_inc(S("m_shift"), 1)
            for dst, o in ((sel1, oh1), (sel2, oh2)):
                step(nc.vector.tensor_tensor(dst, oh.unsqueeze(3).broadcast_to([P, CH, NG, EG]),
                                             o.unsqueeze(2).broadcast_to([P, CH, NG, EG]), ALU.mult))
            s1, s2 = (a.rearrange("p t g i -> p t (g i)") for a in (sel1, sel2))
            step(nc.vector.tensor_tensor(sel, s1, s2, ALU.add))
            step(nc.vector.memset(pre[:, 0, :], 0.0))
            for t in range(1, CH):
                step(nc.vector.tensor_tensor(pre[:, t, :], pre[:, t - 1, :], sel[:, t - 1, :], ALU.add))
            nc.vector.tensor_tensor(tot, pre[:, 3, :], sel[:, 3, :], ALU.add).then_inc(S("m_sel"), 1)
            dve.wait_ge(S("m_exp"), L + 1)
            step(nc.vector.tensor_reduce(gsum, sh, AX.X, ALU.add))
            step(nc.vector.tensor_scalar(gate1, e2, 1.0, None, ALU.add))
            step(nc.vector.tensor_tensor(gate1, gate1, gsum, ALU.mult))
            step(nc.vector.reciprocal(gate1, gate1))
            step(nc.vector.tensor_tensor(gate2, gate1, e2, ALU.mult))
            dve.wait_ge(S("m_ranks"), L + 1)
            cnt = bank[5][:, 64:80]
            step(nc.vector.tensor_scalar(nblk, cnt, 0.0, None, ALU.is_gt))
            for b in range(1, CH):
                step(nc.vector.scalar_tensor_tensor(out=nblk, in0=cnt, scalar=float(P * b), in1=nblk, op0=ALU.is_gt, op1=ALU.add))
            step(nc.vector.tensor_tensor_scan(incl_b, ones[:, 0:NE], nblk, 0.0, ALU.mult, ALU.add))
            step(nc.vector.tensor_tensor(rowbase, incl_b, nblk, ALU.subtract))
            step(nc.vector.tensor_scalar(rowbase, rowbase, float(P), None, ALU.mult))
            step(nc.vector.tensor_tensor(tmp64, bank[5][:, 0:64].rearrange("p (t e) -> p t e", e=NE),
                                         rowbase.unsqueeze(1).broadcast_to([P, CH, NE]), ALU.add))
            step(nc.vector.tensor_tensor(pre, tmp64, s1, ALU.mult))
            step(nc.vector.tensor_reduce(row12[:, 0:4], pre, AX.X, ALU.add))
            step(nc.vector.tensor_tensor(pre, tmp64, s2, ALU.mult))
            step(nc.vector.tensor_reduce(row12[:, 4:8], pre, AX.X, ALU.add))
            nc.vector.tensor_copy(rows_i, row12).then_inc(S("m_plan"), 1)
            step(nc.vector.tensor_tensor(cmp, incl_b.unsqueeze(1).broadcast_to([P, ITEMS, NE]),
                                         iota.unsqueeze(2).broadcast_to([P, ITEMS, NE]), ALU.is_le))
            step(nc.vector.tensor_reduce(emapf, cmp, AX.X, ALU.add))
            step(nc.vector.tensor_scalar(emapf, emapf, float(NE - 1), None, ALU.min))
            step(nc.vector.tensor_copy(emap_i, emapf))
            step(nc.vector.tensor_scalar(cmp[:, :, 0], iota, incl_b[:, NE - 1:NE], None, ALU.is_lt))
            step(nc.vector.tensor_reduce(pairs_f[:, 0:1], cmp[:, 0:ITEMS:2, 0], AX.X, ALU.add))
            nc.vector.tensor_copy(smalli[:, 8 + ITEMS + L:9 + ITEMS + L], pairs_f[:, 0:1]).then_inc(S("m_plan"), 1)
            dve.wait_ge(S("m_plan"), 2 * L + 2)
            turns, before = item_turns(dve, L)
            base = 2 * before
            for t in range(CH):
                dve.wait_ge(S("m_tok_ready"), CH * L + t + 1)
                nc.vector.tensor_copy(htok[:, t, 0:T], bank[2 * (t % 2)][:, :]).then_inc(S("m_tok0"), 1)
            with dve.Fori(0, turns) as i:
                for u in range(2):
                    n = 2 * i + (base + u)
                    dve.wait_ge(S("m_xt_ready"), n + 1)
                    nc.vector.tensor_copy(xgT[u][:, 0:4, :], chunks(bank[0][:, :])).then_inc(S("m_xt0"), 1)
                for u in range(2):
                    n = 2 * i + (base + u)
                    dve.wait_ge(S("m_silu"), n + 1)
                    nc.vector.tensor_tensor(hid[u], hs[u], bank[2 + u][:, FF:2 * FF], ALU.mult).then_inc(S("m_hid"), 1)
                for u in range(2):
                    n = 2 * i + (base + u)
                    dve.wait_ge(S("m_ht_ready"), n + 1)
                    nc.vector.tensor_copy(hidT[u], bank[4 + u][:, 0:256].rearrange("p (a n) -> p a n", a=2)).then_inc(
                        S("m_ht"), 1)
                for u in range(2):
                    n = 2 * i + (base + u)
                    dve.wait_ge(S("m_y_ready"), n + 3)
                    dve.wait_ge(S(f"m_y_sent{u}"), (i + before + 1) * 16)
                    nc.vector.tensor_copy(ysb[u][:, 0, :], bank[6][:, :]).then_inc(S("m_y0"), 1)
            for t in range(CH):
                dve.wait_ge(S("m_got"), 128 * (L + 1))
                step(nc.vector.tensor_scalar(y1[:, t, :], y1[:, t, :], gate1[:, t:t + 1], None, ALU.mult))
                nc.vector.scalar_tensor_tensor(out=y1[:, t, :], in0=y2[:, t, :], scalar=gate2[:, t:t + 1], in1=y1[:, t, :],
                                               op0=ALU.mult, op1=ALU.add).then_inc(S("m_mix"), 1)
            for k in range(DT):
                dve.wait_ge(S("m_back"), DT * L + k + 1)
                nc.vector.tensor_tensor(xT[:, k, :], xT[:, k, :], bank[k % 4][:, :], ALU.add).then_inc(S("m_added"), 1)
            dve.wait_ge(S("m_added"), DT * (L + 1))

        def moe_act(act, step, L):
            act.wait_ge(S("m_shift"), 2 * L + 1)
            step(nc.scalar.activation(sh, sh, ACT.Exp))
            act.wait_ge(S("m_shift"), 2 * L + 2)
            nc.scalar.activation(e2, e2, ACT.Exp).then_inc(S("m_exp"), 1)
            for t in range(CH):
                act.wait_ge(S("m_tok_ready"), CH * L + t + 1)
                nc.scalar.activation(htok[:, t, T:2 * T], bank[2 * (t % 2) + 1][:, :], ACT.Copy).then_inc(S("m_tok1"), 1)
            act.wait_ge(S("m_plan"), 2 * L + 2)
            turns, before = item_turns(act, L)
            base = 2 * before
            with act.Fori(0, turns) as i:
                for u in range(2):
                    n = 2 * i + (base + u)
                    act.wait_ge(S("m_xt_ready"), n + 1)
                    nc.scalar.activation(xgT[u][:, 4:8, :], chunks(bank[1][:, :]), ACT.Copy).then_inc(S("m_xt1"), 1)
                for u in range(2):
                    n = 2 * i + (base + u)
                    act.wait_ge(S("m_h"), n + 3)
                    nc.scalar.activation(hs[u], bank[2 + u][:, 0:FF], ACT.Silu).then_inc(S("m_silu"), 1)
                for u in range(2):
                    n = 2 * i + (base + u)
                    act.wait_ge(S("m_y_ready"), n + 3)
                    act.wait_ge(S(f"m_y_sent{u}"), (i + before + 1) * 16)
                    nc.scalar.activation(ysb[u][:, 1, :], bank[7][:, :], ACT.Copy).then_inc(S("m_y1"), 1)
                    act.wait_ge(S("m_y0"), n + 1)
                    act.wait_ge(S("m_y1"), n + 1)
                    dst = rows_d[bass.ds(i * (2 * P) + u * P, P), :]
                    act.dma_start(dst, ysb[u].rearrange("p a n -> p (a n)")).then_inc(S(f"m_y_sent{u}"), 16)
            for u in range(2):
                act.wait_ge(S(f"m_y_sent{u}"), (turns + before + 1) * 16)
            act.sem_inc(S("m_rows_sent"), 1)

        def moe_pe(pe, L):
            wge = par[:, PC["wge"] + 160 * L:PC["wge"] + 160 * L + 160].rearrange("p (k n) -> p k n", k=DT)
            for t in range(CH):
                for k in range(DT):
                    mm = nc.tensor.matmul(bank[4][:, 20 * t:20 * t + 20], chunks(hT[:, k, :])[:, t, :], wge[:, k, :],
                                          start=(k == 0), stop=(k == DT - 1))
            mm.then_inc(S("m_logits"), 1)
            for t in range(CH):
                if t >= 2:
                    pe.wait_ge(S("m_tok0"), CH * L + t - 1)
                    pe.wait_ge(S("m_tok1"), CH * L + t - 1)
                for k in range(DT):
                    mm = nc.tensor.transpose(bank[2 * (t % 2) + k // 4][:, (k % 4) * P:(k % 4) * P + P], chunks(hT[:, k, :])[:, t, :],
                                             ident)
                mm.then_inc(S("m_tok_ready"), 1)
                if t == 1:
                    pe.wait_ge(S("m_sel"), L + 1)
                    sl = sel.rearrange("p t e -> p (t e)")
                    nc.tensor.matmul(bank[5][:, 0:64], strict, sl, start=True, stop=False)
                    nc.tensor.matmul(bank[5][:, 0:64], ones, pre.rearrange("p t e -> p (t e)"), start=False, stop=True)
                    nc.tensor.matmul(bank[5][:, 64:80], ones, tot, start=True, stop=True).then_inc(S("m_ranks"), 1)
            pe.wait_ge(S("m_plan"), 2 * L + 2)
            turns, before = item_turns(pe, L)
            base = 2 * before
            pe.wait_ge(S("m_tok0"), CH * (L + 1))
            pe.wait_ge(S("m_tok1"), CH * (L + 1))
            with pe.Fori(0, turns) as i:
                for u in range(2):
                    n = 2 * i + (base + u)
                    pe.wait_ge(S(f"m_x{u}"), (i + before + 1) * 16)
                    if u == 1:
                        pe.wait_ge(S("m_xt0"), n)
                        pe.wait_ge(S("m_xt1"), n)
                    for k in range(DT):
                        mm = nc.tensor.transpose(bank[k // 4][:, (k % 4) * P:(k % 4) * P + P], xg[u][:, k * P:k * P + P], ident)
                    mm.then_inc(S("m_xt_ready"), 1)
                for u in range(2):
                    n = 2 * i + (base + u)
                    pe.wait_ge(S("m_xt0"), n + 1)
                    pe.wait_ge(S("m_xt1"), n + 1)
                    pe.wait_ge(S(f"m_w13_{u}"), (i + before + 1) * 16)
                    for k in range(DT):
                        mm = nc.tensor.matmul(bank[2 + u][:, :], xgT[u][:, k, :], w13[u][:, k, :], start=(k == 0), stop=(k == DT - 1))
                    mm.then_inc(S("m_h"), 1)
                for u in range(2):
                    n = 2 * i + (base + u)
                    pe.wait_ge(S("m_hid"), n + 1)
                    for a in range(2):
                        mm = nc.tensor.transpose(bank[4 + u][:, a * P:a * P + P], hid[u][:, a * P:a * P + P], ident)
                    mm.then_inc(S("m_ht_ready"), 1)
                for u in range(2):
                    n = 2 * i + (base + u)
                    pe.wait_ge(S("m_ht"), n + 1)
                    pe.wait_ge(S(f"m_w2_{u}"), (i + before + 1) * 16)
                    if u == 1:
                        pe.wait_ge(S("m_y0"), n)
                        pe.wait_ge(S("m_y1"), n)
                    for half in range(2):
                        for a in range(2):
                            mm = nc.tensor.matmul(bank[6 + half][:, :], hidT[u][:, a, :], w2e[u][:, a, half * T:half * T + T],
                                                  start=(a == 0), stop=(a == 1))
                    mm.then_inc(S("m_y_ready"), 1)
                pe.wait_ge(S("m_y0"), 2 * i + (base + 2))
                pe.wait_ge(S("m_y1"), 2 * i + (base + 2))
            pe.sem_inc(S("m_items_done"), 1)
            for k in range(DT):
                if k >= 4:
                    pe.wait_ge(S("m_added"), DT * L + k - 3)
                for t in range(CH):
                    if k == 0:
                        pe.wait_ge(S("m_mix"), CH * L + t + 1)
                    mm = nc.tensor.transpose(bank[k % 4][:, t * P:t * P + P], y1[:, t, k * P:k * P + P], ident)
                mm.then_inc(S("m_back"), 1)

        def moe_pool(pool, L):
            pool.wait_ge(S("m_plan"), 2 * L + 1)
            if L == 0:
                pool.wait_ge(S("rows_zeroed"), 16 * ITEMS)
            for t in range(CH):
                pool.wait_ge(S("m_tok0"), CH * L + t + 1)
                pool.wait_ge(S("m_tok1"), CH * L + t + 1)
                for j in range(2):
                    pool.indirect_dma_start(rows_d[:, :], bass.IndirectOffsetOnAxis(ap=rows_i[:, 4 * j + t:4 * j + t + 1], axis=0),
                                            htok[:, t, :], None).then_inc(S("m_spread"), 16)
            pool.wait_ge(S("m_rows_sent"), L + 1)
            for t in range(CH):
                for j, y in enumerate((y1, y2)):
                    pool.indirect_dma_start(y[:, t, :], None, rows_d[:, :],
                                            bass.IndirectOffsetOnAxis(ap=rows_i[:, 4 * j + t:4 * j + t + 1], axis=0)).then_inc(
                        S("m_got"), 16)
            pool.wait_ge(S("m_got"), 128 * (L + 1))

        def moe_sync(sp, L):
            sp.wait_ge(S("m_plan"), 2 * L + 2)
            sp.wait_ge(S("m_spread"), 16 * 8 * (L + 1))
            turns, before = item_turns(sp, L)
            base = 2 * before
            with sp.Fori(0, turns) as i:
                for u in range(2):
                    n = 2 * i + (base + u)
                    e = sp.value_load(emap_i[0:1, bass.ds(2 * i + u, 1)], min_val=0, max_val=NE - 1)
                    sp.wait_ge(S("m_h"), n + 1)
                    sp.dma_start(xg[u], rows_d[bass.ds(i * (2 * P) + u * P, P), :]).then_inc(S(f"m_x{u}"), 16)
                    sp.dma_start(ring[:, 3 * u:3 * u + 2, :].rearrange("p a n -> p (a n)"),
                                 moe13[bass.ds(e * P + L * NE * P, P), :]).then_inc(S(f"m_w13_{u}"), 16)
                    sp.wait_ge(S("m_y_ready"), n + 1)
                    sp.dma_start(ring[:, 3 * u + 2, :], moe2[bass.ds(e * P + L * NE * P, P), :]).then_inc(S(f"m_w2_{u}"), 16)
            sp.wait_ge(S("m_items_done"), L + 1)

        N_IN, N_XA = 15, 4
        first_xa = [B_XA0, B_XA1]

        @block.sync
        def _(sp):
            sp.dma_start(con[:, :], con_d).then_inc(S("inputs_in"), 16)
            sp.dma_start(xT[:, :, :], x_d.rearrange("(k p) t -> p k t", p=P)).then_inc(S("inputs_in"), 16)
            sp.dma_start(par[:, :], par_d).then_inc(S("inputs_in"), 16)
            sp.dma_start(memT[:, :, :], mem_d.rearrange("(k p) t -> p k t", p=P)).then_inc(S("inputs_in"), 16)

            def load(i, b):
                if not (isinstance(i, int) and b < RING):
                    sp.wait_ge(S("tile_ready1"), b + RING * i - RING + 1)
                src = wst[bass.ds((b + RING * i) * P, P), :] if not isinstance(i, int) else wst[(b + RING * i) * P:(b + RING * i + 1) * P, :]
                sp.dma_start(ring[:, b % RING, :], src).then_inc(S(f"weights{b % RING}"), 16)

            for b in range(RING):
                load(0, b)
            each_block(sp, RING, B_CIN - RING, load)
            moe_sync(sp, 0)
            each_block(sp, B_CIN, NBLK - B_CIN, load)
            moe_sync(sp, 1)
            for t in range(DT):
                sp.wait_ge(S("norm_done"), DT * 8 + t + 1)
                sp.dma_start(out_d[t * P:t * P + P, :], hT[:, t, :]).then_inc(S("out_sent"), 16)
            sp.wait_ge(S("out_sent"), 16 * DT)

        @block.scalar
        def _(act):
            step = Line(act, "act_order")
            act.sem_inc(S("m_y_sent0"), 16)
            act.sem_inc(S("m_y_sent1"), 16)
            act.wait_ge(S("inputs_in"), 64)
            norm_act(act, step, 0, xT, T)
            drain_copies("act", act, B_IN, N_IN, 0, proj, 0, T)
            act.wait_ge(S("rows_zeroed"), 16 * ITEMS)
            delta_act(act, step)
            rwkv_act(act, step)
            for L in range(2):
                if L == 1:
                    act.wait_ge(S("m_added"), DT)
                    norm_act(act, step, 4, xT, T)
                    drain_copies("act", act, B_CIN, 16, 0, proj, 0, T)
                    hgrn_act(act, step)
                act.wait_ge(S("b_done") if L == 0 else S("c_done"), BT if L == 0 else CHEADS)
                norm_act(act, step, 4 * L + 1, memT, M)
                fx = first_xa[L]
                drain_copies("act", act, fx, 4, 0, proj, 0, M)
                drain_copies("act", act, fx + 4, 4, 0, proj, 8, 256)
                norm_act(act, step, 4 * L + 2, xT, T)
                drain_copies("act", act, fx + 8, 4, 0, proj, 16, T)
                act.wait_ge(S("tile_free1"), 2 + fx + 12)
                xattn_act(act, step, L)
                act.wait_ge(S("tile_free0"), 2 + fx + 16)
                act.wait_ge(S("tile_free1"), 2 + fx + 16)
                norm_act(act, step, 4 * L + 3, xT, T)
                moe_act(act, step, L)
            act.wait_ge(S("m_added"), 2 * DT)
            norm_act(act, step, 8, xT, T)

        @block.tensor
        def _(pe):
            pe.sem_inc(S("m_h"), 2)
            pe.sem_inc(S("m_y_ready"), 2)
            pe.wait_ge(S("inputs_in"), 64)
            norm_pe(pe, 0, T)
            pe.wait_ge(S("norm_done"), DT)
            project_pe(pe, B_IN, N_IN, hT, T)
            delta_pe(pe)
            rwkv_pe(pe)
            for L in range(2):
                if L == 1:
                    norm_pe(pe, 4, T)
                    pe.wait_ge(S("norm_done"), DT * 5)
                    project_pe(pe, B_CIN, 16, hT, T)
                    pe.wait_ge(S("tile_free0"), 2 + B_COUT)
                    pe.wait_ge(S("tile_free1"), 2 + B_COUT)
                    hgrn_pe(pe)
                    pe.wait_ge(S("c_done"), CHEADS)
                project_pe(pe, B_AOUT if L == 0 else B_COUT, 4, hT, T)
                norm_pe(pe, 4 * L + 1, M)
                pe.wait_ge(S("norm_done"), DT * (4 * L + 2))
                fx = first_xa[L]
                project_pe(pe, fx, 4, memn, M)
                project_pe(pe, fx + 4, 4, memn, M, tokens_out=True)
                norm_pe(pe, 4 * L + 2, T)
                pe.wait_ge(S("norm_done"), DT * (4 * L + 3))
                project_pe(pe, fx + 8, 4, hT, T)
                xattn_pe(pe, L)
                project_pe(pe, fx + 12, 4, hT, T)
                norm_pe(pe, 4 * L + 3, T)
                pe.wait_ge(S("norm_done"), DT * (4 * L + 4))
                moe_pe(pe, L)
            norm_pe(pe, 8, T)

        @block.vector
        def _(dve):
            step = Line(dve, "dve_order")
            dve.sem_inc(S("tile_free0"), 2)
            dve.sem_inc(S("tile_free1"), 2)
            dve.wait_ge(S("inputs_in"), 64)
            norm_dve(dve, 0, xT, hT, T, gains("mix", 0))
            drain_copies("dve", dve, B_IN, N_IN, 1, proj, 0, T)
            delta_dve(dve, step)
            rwkv_dve(dve, step)
            for L in range(2):
                if L == 1:
                    norm_dve(dve, 4, xT, hT, T, gains("mix", 1))
                    drain_copies("dve", dve, B_CIN, 16, 1, proj, 0, T)
                    hgrn_dve(dve, step)
                drain_residual(dve, B_AOUT if L == 0 else B_COUT)
                norm_dve(dve, 4 * L + 1, memT, memn, M, gains("mem", L))
                fx = first_xa[L]
                drain_copies("dve", dve, fx, 4, 1, proj, 0, M)
                drain_copies("dve", dve, fx + 4, 4, 1, proj, 8, 256)
                norm_dve(dve, 4 * L + 2, xT, hT, T, gains("xat", L))
                drain_copies("dve", dve, fx + 8, 4, 1, proj, 16, T)
                xattn_dve(dve, step, L)
                drain_residual(dve, fx + 12)
                norm_dve(dve, 4 * L + 3, xT, hT, T, gains("ffn", L))
                moe_dve(dve, step, L)
            norm_dve(dve, 8, xT, hT, T, gains("fin"))

        @block.gpsimd
        def _(pool):
            zero = work[:, 12:14, :].rearrange("p a n -> p (a n)")
            nc.gpsimd.memset(zero, 0.0).then_inc(S("zero_set"), 1)
            pool.wait_ge(S("zero_set"), 1)
            for i in range(ITEMS):
                pool.dma_start(rows_d[i * P:i * P + P, :], zero).then_inc(S("rows_zeroed"), 16)
            pool.wait_ge(S("inputs_in"), 64)
            for r in range(2):
                inv_pool(pool, r, a_bufs(r))
            for q in range(BT):
                inv_pool(pool, 2 + q, b_inv)
            moe_pool(pool, 0)
            hgrn_pool(pool)
            moe_pool(pool, 1)


def constants():
    c = np.zeros((P, NCONST), np.float32)
    i = np.arange(P)
    c[:, C_ID:C_ID + P] = np.eye(P)
    c[:, C_ONE:C_ONE + P] = 1
    c[:, C_BLK:C_BLK + P] = i[:, None] // 64 == i[None, :] // 64
    c[:, C_INC:C_INC + P] = i[:, None] <= i[None, :]
    c[:, C_STR:C_STR + P] = i[:, None] < i[None, :]
    for n, s in enumerate(LEVELS):
        same = i[:, None] // (2 * s) == i[None, :] // (2 * s)
        c[:, C_LVL + n * P:C_LVL + n * P + P] = same & (i[:, None] // s % 2 == 0) & (i[None, :] // s % 2 == 1)
    c[:, C_RST:C_RST + T] = np.arange(T) % P != 0
    for h in range(8):
        c[h, C_SEL + h * P:C_SEL + h * P + P] = 1
    c[:, C_IOTA:C_IOTA + ITEMS] = np.arange(ITEMS)
    c[:, C_WTS:C_WTS + 4] = [4, 3, 2, 1]
    c[:, C_EPS] = 1e-6
    c[:, C_EPS + 1] = 64e-5
    return c


def columns(v):
    v = np.asarray(v).reshape(-1, P)
    return v.T


def blocks(w):
    k, n = w.shape
    return np.asarray(w).reshape(DT, P, n // 256, 256).transpose(2, 1, 0, 3).reshape(n // 256, P, BLK)


def pack(i):
    f = {k: np.asarray(v) for k, v in i.items()}
    par = np.zeros((P, NPAR), np.float32)

    def put(name, a):
        par[:a.shape[0], PC[name]:PC[name] + a.shape[1]] = a

    for n, k in (("mix", "norm_mix"), ("xat", "norm_xattn"), ("mem", "norm_mem"), ("ffn", "norm_ffn"), ("fin", "norm_final"),
                 ("mu", "ab_shift_mu"), ("w0", "ab_w0"), ("a0", "ab_a0"), ("kk", "ab_k_k"), ("ka", "ab_k_a"), ("rk", "ab_r_k"),
                 ("lnw", "ab_ln_w"), ("lnb", "ab_ln_b"), ("lb", "c_lb_param"), ("onA", "ab_onorm"), ("onC", "c_onorm")):
        put(n, columns(f[k]))
    put("conv", f["ab_conv"][0].reshape(4, 12, P).transpose(2, 1, 0).reshape(P, 48))
    put("alog", f["ab_a_log"].reshape(4, 1))
    put("dt", f["ab_dt_bias"].reshape(4, 1))
    put("w2a2", np.concatenate([f["ab_w2"][0], f["ab_a2"][0]], axis=0))
    put("g2", f["ab_g2"][0])
    w_in = f["ab_w_in"][0]
    put("wdb", w_in[:, 2048:2056].reshape(DT, P, 8).transpose(1, 0, 2).reshape(P, 64))
    for L in range(2):
        wge = np.concatenate([f["moe_w_group"][L], f["moe_w_expert"][L]], axis=1)
        par[:, PC["wge"] + 160 * L:PC["wge"] + 160 * L + 160] = wge.reshape(DT, P, 20).transpose(1, 0, 2).reshape(P, 160)
        par[:, PC["bge"] + 20 * L:PC["bge"] + 20 * L + 20] = np.concatenate([f["moe_b_group"][L], f["moe_b_expert"][L]])
    wst = [blocks(w_in[:, :2048]), blocks(w_in[:, 2056:]), blocks(f["ab_w_out"][0])]
    for L in range(2):
        if L:
            wst += [blocks(f["c_w_in"][0]), blocks(f["c_w_out"][0])]
        wst += [blocks(f["xa_wkv"][L]), blocks(f["xa_wq"][L]), blocks(f["xa_wo"][L])]
    wst = np.concatenate(wst).reshape(NBLK * P, BLK)
    w13 = np.stack([f["moe_w1"], f["moe_w3"]], axis=3)
    w13 = w13.reshape(2, NE, DT, P, 2 * FF).transpose(0, 1, 3, 2, 4).reshape(2 * NE * P, 2 * BLK)
    w2 = f["moe_w2"].reshape(2, NE, 2, P, D).transpose(0, 1, 3, 2, 4).reshape(2 * NE * P, BLK)
    c = np.ascontiguousarray
    return {"wst": c(wst), "moe13": c(w13), "moe2": c(w2), "par": par, "con": constants(), "x": c(f["x"][0].T),
            "mem": c(f["mem"][0].T)}


def program(nc, arrays):
    ins = {n: nc.dram_tensor(f"in_{n}", a.shape, F32, kind="ExternalInput").ap() for n, a in arrays.items()}
    out = nc.dram_tensor("out_x", (D, T), F32, kind="ExternalOutput").ap()
    rows = nc.dram_tensor("sorted_rows", (ITEMS * P, D), F32, kind="Internal").ap()
    build(nc, ins["wst"], ins["moe13"], ins["moe2"], ins["par"], ins["con"], ins["x"], ins["mem"], out, rows)


def kernel(**inputs):
    import concourse.bacc as bacc
    from concourse.bass_utils import run_bass_kernel_spmd

    arrays = pack(inputs)
    nc = bacc.Bacc("TRN2", target_bir_lowering=False, num_devices=1)
    program(nc, arrays)
    r = run_bass_kernel_spmd(nc, [{f"in_{n}": a for n, a in arrays.items()}], core_ids=[0])
    return np.ascontiguousarray(r.results[0]["out_x"].T)[None]
```

```python
from contextlib import ExitStack

import numpy as np
import concourse.bass as bass
from concourse import mybir

F32 = mybir.dt.float32
I32 = mybir.dt.int32
ALU = mybir.AluOpType
ACT = mybir.ActivationFunctionType
AX = mybir.AxisListType

P = 128
D = 1024
T = 512
M = 256
DT = D // P
CH = T // P
AH = 4
BT = 4
CHEADS = 8
XH = 4
NE, NG, EG = 16, 4, 4
FF = 256
ITEMS = 24
BLK = 2048
RING = 2
LEVELS = [1, 2, 4, 8, 16, 32, 64]

C_ID, C_ONE, C_BLK, C_INC, C_STR = 0, P, 2 * P, 3 * P, 4 * P
C_LVL = 5 * P
C_RST = C_LVL + 7 * P
C_SEL = C_RST + T
C_IOTA = C_SEL + 8 * P
C_WTS = C_IOTA + ITEMS
C_EPS = C_WTS + 4
NCONST = C_EPS + 4

_names = [("mix", 16), ("xat", 16), ("mem", 16), ("ffn", 16), ("fin", 8), ("conv", 48), ("alog", 1),
          ("dt", 1), ("onA", 1), ("onC", 1), ("mu", 14), ("w0", 4), ("a0", 4), ("kk", 4), ("ka", 4),
          ("rk", 4), ("lnw", 4), ("lnb", 4), ("lb", 16), ("w2a2", 512), ("g2", 512), ("wge", 320),
          ("wdb", 64), ("bge", 40)]
PC, NPAR = {}, 0
for _n, _w in _names:
    PC[_n] = NPAR
    NPAR += _w

B_IN, B_AOUT, B_XA0, B_CIN = 0, 15, 19, 35
B_COUT, B_XA1 = 51, 55
NBLK = 71


def build(nc, wst, moe13, moe2, par_d, con_d, x_d, mem_d, out_d, rows_d):
    ctx = ExitStack()
    with ctx:
        def sb(name, shape, dt=F32):
            return ctx.enter_context(nc.sbuf_tensor(name, shape, dt))

        sems = {}

        def S(name):
            if name not in sems:
                sems[name] = ctx.enter_context(nc.semaphore(name))
            return sems[name]

        con = sb("con", [P, NCONST])
        par = sb("par", [P, NPAR])
        xT = sb("xT", [P, DT, T])
        hT = sb("hT", [P, DT, T])
        gates = sb("gates", [P, BT, T])
        ryz = sb("ryz", [P, 4, P])
        proj = sb("proj", [P, 32, T])
        ring = sb("ring", [P, 6, BLK])
        work = sb("work", [P, 14, T])
        small = sb("small", [P, 1024])
        smalli = sb("smalli", [P, 64], I32)
        bank = [ctx.enter_context(nc.psum_tensor(f"bank{i}", [P, T], F32)) for i in range(8)]
        extra = ring[:, RING:6, :].rearrange("p a (b n) -> p (a b) n", n=T)

        ident = con[:, C_ID:C_ID + P]
        ones = con[:, C_ONE:C_ONE + P]
        bones = con[:, C_BLK:C_BLK + P]
        incl = con[:, C_INC:C_INC + P]
        strict = con[:, C_STR:C_STR + P]
        lvl = [con[:, C_LVL + P * i:C_LVL + P * (i + 1)] for i in range(7)]
        reset = con[:, C_RST:C_RST + T]
        sel8 = [con[0:8, C_SEL + P * i:C_SEL + P * (i + 1)] for i in range(8)]
        eps6 = con[:, C_EPS:C_EPS + 1]
        epsg = con[:, C_EPS + 1:C_EPS + 2]

        def pc(name, i=0, rows=P):
            return par[0:rows, PC[name] + i:PC[name] + i + 1]

        def chunks(ap):
            return ap.rearrange("p (c n) -> p c n", n=P)

        def over4(ap):
            return ap.unsqueeze(1).broadcast_to([P, CH, P])

        block = ctx.enter_context(nc.Block())

        class Line:

            def __init__(self, eng, name):
                self.eng, self.sem, self.n = eng, S(name), 0

            def __call__(self, ins):
                self.n += 1
                ins.then_inc(self.sem, 1)
                self.eng.wait_ge(self.sem, self.n)

        NORMS = {"mix0": 0, "mem0": 1, "xat0": 2, "ffn0": 3, "mix1": 4, "mem1": 5, "xat1": 6, "ffn1": 7, "fin": 8}

        def sq_of(n):
            return work[:, 0:8, 0:n]

        def norm_act(act, step, k, src, n):
            if k > 0:
                act.wait_ge(S("norm_summed"), k)
            for t in range(DT):
                nc.scalar.activation(work[:, t, 0:n], src[:, t, 0:n], ACT.Square).then_inc(S("norm_squared"), 1)
            act.wait_ge(S("norm_summed"), k + 1)
            step(nc.scalar.activation(work[:, 8, 0:n], bank[7][:, 0:n], ACT.Ln, bias=eps6, scale=1.0 / D))
            nc.scalar.activation(work[:, 9, 0:n], work[:, 8, 0:n], ACT.Exp, scale=-0.5).then_inc(S("norm_rstd"), 1)

        def norm_pe(pe, k, n):
            for t in range(DT):
                pe.wait_ge(S("norm_squared"), DT * k + t + 1)
                mm = nc.tensor.matmul(bank[7][:, 0:n], ones, work[:, t, 0:n], start=(t == 0), stop=(t == DT - 1))
            mm.then_inc(S("norm_summed"), 1)

        def norm_dve(dve, k, src, dst, n, gain):
            dve.wait_ge(S("norm_rstd"), k + 1)
            for t in range(DT):
                nc.vector.scalar_tensor_tensor(
                    out=dst[:, t, 0:n], in0=src[:, t, 0:n], scalar=gain[:, t:t + 1], in1=work[:, 9, 0:n],
                    op0=ALU.mult, op1=ALU.mult).then_inc(S("norm_done"), 1)
            dve.wait_ge(S("norm_done"), DT * (k + 1))

        def gains(name, layer=0):
            return par[:, PC[name] + DT * layer:PC[name] + DT * layer + DT]

        def each_block(eng, first, count, body):
            turns = count // RING
            if turns > 1:
                with eng.Fori(0, turns) as i:
                    for s in range(RING):
                        body(i, first + s)
            else:
                turns = 0
            for b in range(first + turns * RING, first + count):
                body(0, b)

        def project_pe(pe, first, count, src, n, tokens_out=False):
            def body(i, b):
                w = ring[:, b % RING, :].rearrange("p (k n) -> p k n", k=DT)
                pe.wait_ge(S(f"weights{b % RING}"), (b // RING + 1 + i) * 16)
                for h in range(2):
                    bk = bank[(2 * b + h) % 4]
                    pe.wait_ge(S(f"tile_free{h}"), b + RING * i + 1)
                    for k in range(DT):
                        if tokens_out:
                            mm = nc.tensor.matmul(bk[:, 0:256], src[:, k, h * P:h * P + P], w[:, k, :],
                                                  start=(k == 0), stop=(k == DT - 1))
                        else:
                            mm = nc.tensor.matmul(bk[:, 0:n], w[:, k, h * P:h * P + P], src[:, k, 0:n],
                                                  start=(k == 0), stop=(k == DT - 1))
                    mm.then_inc(S(f"tile_ready{h}"), 1)
            each_block(pe, first, count, body)

        def drain(eng, first, count, halves, write):
            def body(i, b):
                for h in halves:
                    eng.wait_ge(S(f"tile_ready{h}"), b + RING * i + 1)
                    write(h, i, b, bank[(2 * b + h) % 4]).then_inc(S(f"tile_free{h}"), 1)
            each_block(eng, first, count, body)

        def tile_at(buf, base, i, b, h, first):
            n = base + 2 * (b - first) + h
            if isinstance(i, int):
                return buf[:, n + 2 * RING * i, :]
            return buf[:, bass.ds(i * (2 * RING) + n, 1), :].rearrange("p a n -> p (a n)")

        def drain_copies(act_or_dve, eng, first, count, half, buf, base, n):
            def write(h, i, b, bk):
                dst = tile_at(buf, base, i, b, h, first)[:, 0:n]
                if act_or_dve == "act":
                    return nc.scalar.activation(dst, bk[:, 0:n], ACT.Copy)
                return nc.vector.tensor_copy(dst, bk[:, 0:n])
            drain(eng, first, count, [half], write)

        def drain_residual(dve, first):
            def write(h, i, b, bk):
                dst = tile_at(xT, 0, i, b, h, first)
                return nc.vector.tensor_tensor(dst, dst, bk[:, :], ALU.add)
            drain(dve, first, 4, [0, 1], write)
            dve.wait_ge(S("tile_free1"), 2 + first + 4)

        inv_rounds = {"n": 0}

        def inv_pe(pe, r, bufs, between=None):
            for li in range(7):
                for g, (MT, Tt, TT, X, Cm) in enumerate(bufs):
                    if li == 0:
                        pe.wait_ge(S(f"inv_tt{g}"), 7 * r + 1)
                        for c in range(CH):
                            mm = nc.tensor.transpose(bank[g][:, c * P:c * P + P], chunks(TT)[:, c, :], ident)
                        mm.then_inc(S(f"inv_t_ready{g}"), 1)
                        continue
                    pe.wait_ge(S(f"inv_c{g}"), 7 * r + li + 1)
                    pe.wait_ge(S(f"inv_t{g}"), 6 * r + li)
                    for c in range(CH):
                        mm = nc.tensor.matmul(bank[g][:, c * P:c * P + P], chunks(Cm)[:, c, :], chunks(Tt)[:, c, :],
                                              start=True, stop=True)
                    mm.then_inc(S(f"inv_x_ready{g}"), 1)
                if between and li:
                    between(2 * li - 2)
                for g, (MT, Tt, TT, X, Cm) in enumerate(bufs):
                    if li == 0:
                        continue
                    pe.wait_ge(S(f"inv_x{g}"), 6 * r + li)
                    pe.wait_ge(S(f"inv_tt{g}"), 7 * r + li)
                    if li < 6:
                        for c in range(CH):
                            mm = nc.tensor.matmul(bank[2 + g][:, c * P:c * P + P], chunks(TT)[:, c, :], chunks(X)[:, c, :],
                                                  start=True, stop=True)
                    for c in range(CH):
                        mm = nc.tensor.matmul(bank[4 + g][:, c * P:c * P + P], chunks(X)[:, c, :], chunks(TT)[:, c, :],
                                              start=True, stop=True)
                    mm.then_inc(S(f"inv_tct_ready{g}"), 1)
                if between and li:
                    between(2 * li - 1)

        def inv_act(act, r, bufs, between=None):
            for li in range(1, 7):
                for g, (MT, Tt, TT, X, Cm) in enumerate(bufs):
                    act.wait_ge(S(f"inv_x_ready{g}"), 6 * r + li)
                    nc.scalar.activation(X, bank[g][:, :], ACT.Copy).then_inc(S(f"inv_x{g}"), 1)
                if between:
                    between(2 * li - 2)
                    between(2 * li - 1)

        def inv_pool(pool, r, bufs):
            for li in range(7):
                for g, (MT, Tt, TT, X, Cm) in enumerate(bufs):
                    pool.wait_ge(S(f"inv_mt{g}"), r + 1)
                    if li == 1:
                        pool.wait_ge(S(f"inv_tt{g}"), 7 * r + 1)
                    if li > 1:
                        pool.wait_ge(S(f"inv_x_ready{g}"), 6 * r + li - 1)
                    nc.gpsimd.tensor_tensor(chunks(Cm), chunks(MT), over4(lvl[li]), ALU.mult).then_inc(S(f"inv_c{g}"), 1)

        def inv_dve(dve, r, bufs, between=None):
            for g, (MT, Tt, TT, X, Cm) in enumerate(bufs):
                dve.wait_ge(S(f"inv_c{g}"), 7 * r + 1)
                nc.vector.tensor_tensor(chunks(TT), over4(ident), chunks(Cm), ALU.subtract).then_inc(S(f"inv_tt{g}"), 1)
            for g, (MT, Tt, TT, X, Cm) in enumerate(bufs):
                dve.wait_ge(S(f"inv_t_ready{g}"), r + 1)
                nc.vector.tensor_copy(Tt, bank[g][:, :]).then_inc(S(f"inv_t{g}"), 1)
            for li in range(1, 7):
                if between:
                    between(2 * li - 2)
                for g, (MT, Tt, TT, X, Cm) in enumerate(bufs):
                    dve.wait_ge(S(f"inv_tct_ready{g}"), 6 * r + li)
                    if li < 6:
                        dve.wait_ge(S(f"inv_t{g}"), 6 * r + li)
                        nc.vector.tensor_tensor(Tt, Tt, bank[2 + g][:, :], ALU.subtract).then_inc(S(f"inv_t{g}"), 1)
                    dve.wait_ge(S(f"inv_tt{g}"), 7 * r + li)
                    nc.vector.tensor_tensor(TT, TT, bank[4 + g][:, :], ALU.subtract).then_inc(S(f"inv_tt{g}"), 1)
                if between:
                    between(2 * li - 1)
            for g in range(2):
                dve.wait_ge(S(f"inv_tt{g}"), 7 * r + 7)

        W = [work[:, i, :] for i in range(14)]
        X = [extra[:, i, :] for i in range(16)]
        beta8, g8 = W[12][0:8, :], W[13][0:8, :]
        cols = small[:, 16:80].rearrange("p (a c h) -> p a c h", a=2, c=CH)
        glast = small[:, 80:96].rearrange("p (h c) -> p h c", h=AH)
        e_glast = small[:, 96:112].rearrange("p (h c) -> p h c", h=AH)
        e_rest = small[:, 112:128].rearrange("p (h c) -> p h c", h=AH)
        e_col = small[:, 128:144].rearrange("p (h c) -> p h c", h=AH)
        nbeta_e = small[:, 144:160].rearrange("p (h c) -> p h c", h=AH)
        a_neg = small[0:8, 0:1]
        PT = X[0:4]
        TTa = X[4:8]
        ktok = W[8:12]
        state = proj[:, 30, :]
        N_A, N_IN = 8, 15

        def a_bufs(r):
            return [(hT[:, 4 * g, :], hT[:, 4 * g + 1, :], TTa[2 * r + g], hT[:, 4 * g + 2, :], hT[:, 4 * g + 3, :])
                    for g in range(2)]

        def pair(i):
            return [j for j in (2 * i, 2 * i + 1) if 0 <= i < 4]

        def delta_prep_dve(dve, step):
            dve.wait_ge(S("tile_free0"), 2 + N_A)
            dve.wait_ge(S("tile_free1"), 2 + N_A)
            for i in range(N_IN - N_A):
                for j in (2 * i, 2 * i + 1):
                    if j >= 12:
                        continue
                    cv, p = W[j % 2], proj[:, j, :]
                    if j >= 2:
                        dve.wait_ge(S("a_silu"), j - 1)
                    step(nc.vector.tensor_scalar(cv, p, pc("conv", 4 * j + 3), None, ALU.mult))
                    for s in range(1, 4):
                        ins = nc.vector.scalar_tensor_tensor(out=cv[:, s:T], in0=p[:, 0:T - s], scalar=pc("conv", 4 * j + 3 - s),
                                                             in1=cv[:, s:T], op0=ALU.mult, op1=ALU.add)
                        if s < 3:
                            step(ins)
                    ins.then_inc(S("a_conv"), 1)
                for j in pair(i - 2):
                    p = proj[:, j, :]
                    dve.wait_ge(S("head_rstd"), j + 1)
                    nc.vector.scalar_tensor_tensor(out=p, in0=p, scalar=(P ** -0.5 if j < 4 else 1.0), in1=W[6 + j % 2],
                                                   op0=ALU.mult, op1=ALU.mult).then_inc(S("a_unit"), 1)
                if i == 1:
                    dve.wait_ge(S("a_softplus"), 1)
                    z, l = W[9][0:8, :], W[11][0:8, :]
                    step(nc.vector.tensor_scalar(z, z, 0.0, None, ALU.max))
                    step(nc.vector.tensor_tensor(z, z, l, ALU.add))
                    step(nc.vector.tensor_scalar(z, z, a_neg, -1.0, ALU.mult, ALU.mult))
                    nc.vector.tensor_tensor_scan(g8, reset[0:8, :], z, 0.0, ALU.mult, ALU.add).then_inc(S("a_decay"), 1)
                drain_copies("dve", dve, N_A + i, 1, 1, proj, 2 * (N_A + i), T)
            dve.wait_ge(S("a_unit"), 8)
            dve.wait_ge(S("a_cols"), 1)
            step(nc.vector.tensor_copy(small[:, 16:80], bank[7][:, 0:64]))

        def delta_prep_act(act, step):
            act.wait_ge(S("tile_free0"), 2 + N_A)
            act.wait_ge(S("tile_free1"), 2 + N_A)
            act.wait_ge(S("rows_zeroed"), 16 * ITEMS)
            act.wait_ge(S("a_db"), 1)
            step(nc.scalar.activation(beta8, bank[6][0:8, :], ACT.Sigmoid))
            step(nc.scalar.activation(W[9][0:8, :], bank[6][0:8, :], ACT.Identity, bias=pc("dt", 0, 8)))
            step(nc.scalar.activation(W[10][0:8, :], W[9][0:8, :], ACT.Abs))
            step(nc.scalar.activation(W[10][0:8, :], W[10][0:8, :], ACT.Exp, scale=-1.0))
            step(nc.scalar.activation(W[11][0:8, :], W[10][0:8, :], ACT.Ln, bias=con[0:8, C_ONE:C_ONE + 1]))
            nc.scalar.activation(a_neg, pc("alog", 0, 8), ACT.Exp).then_inc(S("a_softplus"), 1)
            for i in range(N_IN - N_A):
                for j in (2 * i, 2 * i + 1):
                    if j < 12:
                        act.wait_ge(S("a_conv"), j + 1)
                        nc.scalar.activation(proj[:, j, :], W[j % 2], ACT.Silu).then_inc(S("a_silu"), 1)
                if i == 6:
                    for h in range(AH):
                        step(nc.scalar.activation(proj[:, 12 + h, :], proj[:, 12 + h, :], ACT.Silu))
                for j in pair(i - 1):
                    if j >= 2:
                        act.wait_ge(S("head_summed"), j - 1)
                    act.wait_ge(S("a_silu"), j + 1)
                    nc.scalar.activation(W[2 + j % 2], proj[:, j, :], ACT.Square).then_inc(S("head_squared"), 1)
                for j in pair(i - 2):
                    act.wait_ge(S("head_summed"), j + 1)
                    if j >= 2:
                        act.wait_ge(S("a_unit"), j - 1)
                    step(nc.scalar.activation(W[4], bank[4 + j % 2][:, :], ACT.Ln, bias=eps6))
                    nc.scalar.activation(W[6 + j % 2], W[4], ACT.Exp, scale=-0.5).then_inc(S("head_rstd"), 1)
                    act.wait_ge(S("head_rstd"), j + 1)
                drain_copies("act", act, N_A + i, 1, 0, proj, 2 * (N_A + i), T)

        def delta_prep_pe(pe):
            wdb = par[:, PC["wdb"]:PC["wdb"] + 64].rearrange("p (k n) -> p k n", k=DT)
            for k in range(DT):
                mm = nc.tensor.matmul(bank[6][0:8, :], wdb[:, k, :], hT[:, k, :], start=(k == 0), stop=(k == DT - 1))
            mm.then_inc(S("a_db"), 1)
            for i in range(N_IN - N_A):
                project_pe(pe, N_A + i, 1, hT, T)
                for j in pair(i - 1):
                    pe.wait_ge(S("head_squared"), j + 1)
                    if j >= 2:
                        pe.wait_ge(S("head_rstd"), j - 1)
                    nc.tensor.matmul(bank[4 + j % 2][:, :], ones, W[2 + j % 2], start=True, stop=True).then_inc(S("head_summed"), 1)
                if i == 4:
                    pe.wait_ge(S("a_decay"), 1)
                    for a, rows in enumerate((g8, beta8)):
                        for c in range(CH):
                            o = a * 32 + c * 8
                            mm = nc.tensor.transpose(bank[7][:, o:o + 8], rows[:, c * P:c * P + P], ident[0:8, 0:8])
                    mm.then_inc(S("a_cols"), 1)
            pe.wait_ge(S("a_unit"), 8)
            pe.wait_ge(S("head_rstd"), 8)

        def delta_round_dve(dve, step, r, between):
            for g in range(2):
                h = 2 * r + g
                dve.wait_ge(S("a_bcast"), h + 1)
                for c in range(CH):
                    nc.vector.tensor_scalar(chunks(W[g])[:, c, :], chunks(bank[4 + g][:, :])[:, c, :], cols[:, 0, c, h:h + 1],
                                            0.0, ALU.subtract, ALU.min).then_inc(S("a_diff"), 1)
                step(nc.vector.tensor_copy(glast[:, h, :], bank[4 + g][:, P - 1:T:P]))
                nc.vector.tensor_tensor(e_rest[:, h, :], glast[:, h, :], cols[:, 0, :, h], ALU.subtract).then_inc(S("a_diff"), 1)
                nc.vector.tensor_tensor(W[2 + g], proj[:, 4 + h, :], bank[6 + g][:, :], ALU.mult).then_inc(S("a_diff"), 1)
            for g in range(2):
                h = 2 * r + g
                dve.wait_ge(S("a_exps"), h + 1)
                step(nc.vector.tensor_tensor(chunks(W[6 + g]), chunks(W[g]), over4(incl), ALU.mult))
                dve.wait_ge(S("a_scores"), h + 1)
                nc.vector.tensor_tensor(a_bufs(r)[g][0], bank[g][:, :], W[g], ALU.mult).then_inc(S(f"inv_mt{g}"), 1)
                step(nc.vector.tensor_tensor(PT[h], bank[2 + g][:, :], W[6 + g], ALU.mult))
                step(nc.vector.tensor_tensor(proj[:, h, :], proj[:, h, :], W[4 + g], ALU.mult))
                step(nc.vector.scalar_tensor_tensor(out=nbeta_e[:, h, :], in0=e_col[:, h, :], scalar=-1.0,
                                                    in1=cols[:, 1, :, 4 + h], op0=ALU.mult, op1=ALU.mult))
            for g in range(2):
                h = 2 * r + g
                dve.wait_ge(S("a_turned"), h + 1)
                for c in range(CH):
                    nc.vector.tensor_scalar(chunks(ktok[h])[:, c, :], chunks(bank[4 + g][:, :])[:, c, :],
                                            e_rest[:, h, c:c + 1], None, ALU.mult)
                    ins = nc.vector.tensor_scalar(chunks(proj[:, 8 + h, :])[:, c, :], chunks(bank[6 + g][:, :])[:, c, :],
                                                  cols[:, 1, c, 4 + h:5 + h], None, ALU.mult)
                ins.then_inc(S("a_tok"), 1)
            dve.wait_ge(S("a_tok"), 2 * r + 2)
            inv_dve(dve, r, a_bufs(r), between)

        def delta_round_act(act, step, r):
            for g in range(2):
                h = 2 * r + g
                act.wait_ge(S("a_diff"), 6 * h + 6)
                step(nc.scalar.activation(W[4 + g], bank[4 + g][:, :], ACT.Exp))
                step(nc.scalar.activation(W[g], W[g], ACT.Exp))
                step(nc.scalar.activation(e_glast[:, h, :], glast[:, h, :], ACT.Exp))
                step(nc.scalar.activation(e_rest[:, h, :], e_rest[:, h, :], ACT.Exp))
                nc.scalar.activation(e_col[:, h, :], cols[:, 0, :, h], ACT.Exp).then_inc(S("a_exps"), 1)
            inv_act(act, r, a_bufs(r))

        def delta_round_pe(pe, r):
            for g in range(2):
                h = 2 * r + g
                if r == 0 and g == 1:
                    pe.wait_ge(S("a_diff"), 5)
                if r > 0:
                    pe.wait_ge(S("a_tok"), 2 * r)
                    pe.wait_ge(S(f"inv_tt{g}"), 7 * r)
                nc.tensor.matmul(bank[4 + g][:, :], sel8[h], g8, start=True, stop=True)
                nc.tensor.matmul(bank[6 + g][:, :], sel8[4 + h], beta8, start=True, stop=True).then_inc(S("a_bcast"), 1)
            for g in range(2):
                h = 2 * r + g
                pe.wait_ge(S("a_diff"), 6 * h + 6)
                for c in range(CH):
                    k = chunks(proj[:, 4 + h, :])[:, c, :]
                    nc.tensor.matmul(bank[g][:, c * P:c * P + P], k, chunks(W[2 + g])[:, c, :], start=True, stop=True)
                    mm = nc.tensor.matmul(bank[2 + g][:, c * P:c * P + P], k, chunks(proj[:, h, :])[:, c, :],
                                          start=True, stop=True)
                mm.then_inc(S("a_scores"), 1)
            for g in range(2):
                h = 2 * r + g
                pe.wait_ge(S("a_exps"), h + 1)
                for c in range(CH):
                    nc.tensor.transpose(bank[4 + g][:, c * P:c * P + P], chunks(proj[:, 4 + h, :])[:, c, :], ident)
                    mm = nc.tensor.transpose(bank[6 + g][:, c * P:c * P + P], chunks(proj[:, 8 + h, :])[:, c, :], ident)
                mm.then_inc(S("a_turned"), 1)
            pe.wait_ge(S("a_tok"), 2 * r + 2)
            inv_pe(pe, r, a_bufs(r))

        def delta_chunk_dve(dve, step, c):
            if c > 0:
                dve.wait_ge(S("a_ks"), c)
                for h in range(AH):
                    nc.vector.scalar_tensor_tensor(
                        out=W[c % 2][:, h * P:h * P + P], in0=bank[0][:, h * P:h * P + P], scalar=nbeta_e[:, h, c:c + 1],
                        in1=chunks(proj[:, 8 + h, :])[:, c, :], op0=ALU.mult, op1=ALU.add).then_inc(S("a_r"), 1)

        def delta_state_dve(dve, step, c):
            if c == CH - 1:
                return
            dve.wait_ge(S("a_out"), c + 1)
            if c == 0:
                nc.vector.tensor_copy(state, bank[3][:, :]).then_inc(S("a_state"), 1)
            else:
                for h in range(AH):
                    sl = state[:, h * P:h * P + P]
                    ins = nc.vector.scalar_tensor_tensor(out=sl, in0=sl, scalar=e_glast[:, h, c:c + 1],
                                                         in1=bank[3][:, h * P:h * P + P], op0=ALU.mult, op1=ALU.add)
                    if h < AH - 1:
                        step(ins)
                ins.then_inc(S("a_state"), 1)
            dve.wait_ge(S("a_state"), c + 1)

        def delta_chunk_act(act, step, c):
            act.wait_ge(S("a_v"), c + 1)
            nc.scalar.activation(W[2 + c % 2], bank[1][:, :], ACT.Copy).then_inc(S("a_vnew"), 1)

        def delta_out_act(act, step, c):
            act.wait_ge(S("a_out"), c + 1)
            nc.scalar.activation(hT[:, 0:4, c * P:c * P + P], chunks(bank[2][:, :]), ACT.Copy).then_inc(S("a_o"), 1)

        def delta_chunk_pe(pe, c):
            if c > 0:
                pe.wait_ge(S("a_state"), c)
                for h in range(AH):
                    mm = nc.tensor.matmul(bank[0][:, h * P:h * P + P], chunks(proj[:, 4 + h, :])[:, c, :],
                                          state[:, h * P:h * P + P], start=True, stop=True)
                mm.then_inc(S("a_ks"), 1)
                pe.wait_ge(S("a_r"), AH * c)
            for h in range(AH):
                r_h = W[c % 2][:, h * P:h * P + P] if c > 0 else chunks(proj[:, 8 + h, :])[:, 0, :]
                mm = nc.tensor.matmul(bank[1][:, h * P:h * P + P], chunks(TTa[h])[:, c, :], r_h, start=True, stop=True)
            mm.then_inc(S("a_v"), 1)

        def delta_out_pe(pe, c):
            pe.wait_ge(S("a_vnew"), c + 1)
            if c > 0:
                pe.wait_ge(S("a_o"), c)
            for h in range(AH):
                v = W[2 + c % 2][:, h * P:h * P + P]
                mm = nc.tensor.matmul(bank[3][:, h * P:h * P + P], chunks(ktok[h])[:, c, :], v, start=True, stop=True)
            for h in range(AH):
                v = W[2 + c % 2][:, h * P:h * P + P]
                if c > 0:
                    nc.tensor.matmul(bank[2][:, h * P:h * P + P], state[:, h * P:h * P + P], chunks(proj[:, h, :])[:, c, :],
                                     start=True, stop=False)
                mm = nc.tensor.matmul(bank[2][:, h * P:h * P + P], v, chunks(PT[h])[:, c, :], start=(c == 0), stop=True)
            mm.then_inc(S("a_out"), 1)

        def delta_norm_dve(dve, step, n):
            h = n - 2
            if 0 <= h < AH:
                o = hT[:, h, :]
                dve.wait_ge(S("head_rstd"), h + 1 + 12)
                step(nc.vector.scalar_tensor_tensor(out=o, in0=o, scalar=pc("onA"), in1=B_RS[h % 2], op0=ALU.mult, op1=ALU.mult))
                nc.vector.tensor_tensor(o, o, proj[:, 12 + h, :], ALU.mult).then_inc(S("a_done"), 1)

        def delta_norm_act(act, step, n):
            if n < AH:
                if n >= 2:
                    act.wait_ge(S("head_summed"), n - 1 + 12)
                nc.scalar.activation(B_SQ[n % 2], hT[:, n, :], ACT.Square).then_inc(S("head_squared"), 1)
            h = n - 1
            if 0 <= h < AH:
                act.wait_ge(S("head_summed"), h + 1 + 12)
                if h >= 2:
                    act.wait_ge(S("a_done"), h - 1)
                step(nc.scalar.activation(K_LN, bank[4 + h % 2][:, :], ACT.Ln, bias=eps6, scale=1.0 / P))
                nc.scalar.activation(B_RS[h % 2], K_LN, ACT.Exp, scale=-0.5).then_inc(S("head_rstd"), 1)
                act.wait_ge(S("head_rstd"), h + 1 + 12)

        def delta_norm_pe(pe, n):
            h = n - 1
            if 0 <= h < AH:
                pe.wait_ge(S("head_squared"), h + 1 + 12)
                if h >= 2:
                    pe.wait_ge(S("head_rstd"), h - 1 + 12)
                nc.tensor.matmul(bank[4 + h % 2][:, :], ones, B_SQ[h % 2], start=True, stop=True).then_inc(S("head_summed"), 1)

        E_HALF = float(np.exp(-0.5))
        Gc, Bc, KKc = X[8:12], X[12:16], W[4:8]
        GATE = [gates[:, q, :] for q in range(BT)]
        TH, SGL, B_T0, B_T1 = hT[:, 4, :], hT[:, 5, :], hT[:, 6, :], hT[:, 7, :]
        K_SQ, K_LN, K_RN = W[12], W[13], proj[:, 31, :]
        KR = [proj[:, i:i + 2, :].rearrange("p a n -> p (a n)").rearrange("p (c x n) -> p c x n", c=CH, x=2)
              for i in (0, 2, 12)]
        KM, BM, E1, E3 = proj[:, 4, :], proj[:, 5, :], proj[:, 6, :], proj[:, 7, :]
        VT, KMT, BMT = [proj[:, 8, :], proj[:, 9, :]], [proj[:, 10, :], proj[:, 11, :]], [proj[:, 28, :], proj[:, 29, :]]
        Rb, Yb, Zb, Zt = (ryz[:, i, :] for i in range(4))
        egm = [small[:, 160 + 8 * i:164 + 8 * i] for i in range(3)]
        egc = [small[:, 164 + 8 * i:168 + 8 * i] for i in range(3)]
        omka, engm = small[:, 184:188], small[:, 188:192]
        sc_bufs = [[W[i] for i in (0, 1, 2, 3, 8, 9)], [W[10], W[11], W[12], W[13], proj[:, 30, :], proj[:, 31, :]]]
        B_SQ, B_RS, B_LN = [X[4], X[5]], [X[6], X[7]], E1
        RK, BV = [proj[:, 12, :], proj[:, 13, :]], [proj[:, 14, :], proj[:, 15, :]]

        def b_inv(q):
            t = [hT[:, 4 + i, :] if i >= q else (Gc[0], Bc[0], Gc[1])[i] for i in range(4)]
            return [(X[4], X[5], X[2 * (q % 2)], X[6], X[7]), (t[0], t[1], X[2 * (q % 2) + 1], t[2], t[3])]

        def b_scores(q, g):
            return sc_bufs[q % 2][3 * g:3 * g + 3]

        def mid(q):
            return Gc[q][:, 63:T:P]

        def lerp_dve(dve, step, n):
            j = ([12, 13] + list(range(12)))[n]
            p, d = proj[:, 16 + j, :], X[8 + n % 2]
            step(nc.vector.tensor_tensor(d[:, 1:T], p[:, 0:T - 1], p[:, 1:T], ALU.subtract))
            step(nc.vector.tensor_scalar(d[:, 0:1], p[:, 0:1], -1.0, None, ALU.mult))
            nc.vector.scalar_tensor_tensor(out=p, in0=d, scalar=pc("mu", j), in1=p, op0=ALU.mult,
                                           op1=ALU.add).then_inc(S("b_lerp"), 1)
            dve.wait_ge(S("b_lerp"), n + 1)

        def keys_dve(dve, step, q):
            k, kk, g, b = proj[:, 20 + q, :], KKc[q], Gc[q], Bc[q]
            nc.vector.tensor_scalar(kk, k, pc("kk", q), None, ALU.mult).then_inc(S("b_kraw"), 1)
            dve.wait_ge(S("b_rates"), q + 1)
            step(nc.vector.tensor_scalar(B_T0, g, -E_HALF, None, ALU.mult))
            step(nc.vector.tensor_tensor_scan(g, reset, B_T0, 0.0, ALU.mult, ALU.add))
            step(nc.vector.tensor_scalar(B_T1, b, pc("ka", q), omka[:, q:q + 1], ALU.mult, ALU.add))
            dve.wait_ge(S("b_kraw"), q + 1)
            step(nc.vector.tensor_tensor(k, k, B_T1, ALU.mult))

        def unit_keys_dve(dve, step, q):
            dve.wait_ge(S("head_rstd"), q + 1 + 8)
            nc.vector.tensor_tensor(KKc[q], KKc[q], K_RN, ALU.mult).then_inc(S("b_kk"), 1)
            dve.wait_ge(S("b_kk"), q + 1)
            step(nc.vector.tensor_tensor(Bc[q], Bc[q], KKc[q], ALU.mult))

        def keys_act(act, step, q):
            act.wait_ge(S("b_low"), q + 1)
            step(nc.scalar.activation(Gc[q], bank[4][:, :], ACT.Sigmoid, bias=pc("w0", q)))
            step(nc.scalar.activation(Bc[q], bank[5][:, :], ACT.Sigmoid, bias=pc("a0", q)))
            nc.scalar.activation(GATE[q], bank[6][:, :], ACT.Copy).then_inc(S("b_rates"), 1)
            act.wait_ge(S("b_kraw"), q + 1)
            nc.scalar.activation(K_SQ, KKc[q], ACT.Square).then_inc(S("head_squared"), 1)
            act.wait_ge(S("head_summed"), q + 1 + 8)
            step(nc.scalar.activation(K_LN, bank[7][:, :], ACT.Ln, bias=eps6))
            if q > 0:
                act.wait_ge(S("b_kk"), q)
            nc.scalar.activation(K_RN, K_LN, ACT.Exp, scale=-0.5).then_inc(S("head_rstd"), 1)
            act.wait_ge(S("head_rstd"), q + 1 + 8)

        def low_pe(pe, q):
            w2 = par[0:64, PC["w2a2"]:PC["w2a2"] + 512]
            a2 = par[64:128, PC["w2a2"]:PC["w2a2"] + 512]
            g2w = par[:, PC["g2"]:PC["g2"] + 512]
            if q > 0:
                pe.wait_ge(S("b_rates"), q)
            nc.tensor.matmul(bank[4][:, :], w2[:, q * P:q * P + P], TH[0:64, :], start=True, stop=True)
            nc.tensor.matmul(bank[5][:, :], a2[:, q * P:q * P + P], proj[64:128, 28, :], start=True, stop=True)
            nc.tensor.matmul(bank[6][:, :], g2w[:, q * P:q * P + P], SGL, start=True, stop=True).then_inc(S("b_low"), 1)

        def key_sums_pe(pe, q):
            pe.wait_ge(S("head_squared"), q + 1 + 8)
            if q > 0:
                pe.wait_ge(S("head_rstd"), q + 8)
            nc.tensor.matmul(bank[7][:, :], bones, K_SQ, start=True, stop=True).then_inc(S("head_summed"), 1)

        def scale_dve(dve, step, q, part):
            kr = KR[q % 3]
            if part == 0:
                nc.vector.tensor_tensor(chunks(E3), chunks(Gc[q]), mid(q).unsqueeze(2).broadcast_to([P, CH, P]),
                                        ALU.subtract).then_inc(S("b_diff"), 1)
            elif part == 1:
                dve.wait_ge(S("b_exps"), q + 1)
                step(nc.vector.tensor_tensor(kr[:, :, 1, :], chunks(proj[:, 16 + q, :]), chunks(E1), ALU.mult))
            elif part == 2:
                step(nc.vector.tensor_tensor(kr[:, :, 0, 1:P], chunks(KKc[q])[:, :, 1:P], chunks(E1)[:, :, 0:P - 1], ALU.mult))
                step(nc.vector.tensor_tensor(kr[:, :, 0, 0], KKc[q][:, 0:T:P], engm, ALU.mult))
            elif part == 3:
                step(nc.vector.tensor_tensor(KM, proj[:, 20 + q, :], E3, ALU.mult))
            elif part == 4:
                nc.vector.tensor_tensor(BM, Bc[q], E3, ALU.mult).then_inc(S("b_scaled"), 1)
                dve.wait_ge(S("b_scaled"), q + 1)

        def scale_act(act, step, q):
            act.wait_ge(S("b_diff"), q + 1)
            step(nc.scalar.activation(E1, E3, ACT.Exp))
            step(nc.scalar.activation(E3, E3, ACT.Exp, scale=-1.0))
            step(nc.scalar.activation(egc[q % 3], E1[:, P - 1:T:P], ACT.Copy))
            step(nc.scalar.activation(egm[q % 3], mid(q), ACT.Exp))
            nc.scalar.activation(engm, mid(q), ACT.Exp, scale=-1.0).then_inc(S("b_exps"), 1)

        def scores_pe(pe, q):
            pe.wait_ge(S("b_scaled"), q + 1)
            if q >= 2:
                pe.wait_ge(S("b_o"), CH * (q - 1))
            for g in range(2):
                sl = slice(64 * g, 64 * g + 64)
                for c in range(CH):
                    o = slice((c % 2) * 256, (c % 2) * 256 + 256)
                    kr = KR[q % 3][sl, c, :, :].rearrange("p x n -> p (x n)")
                    nc.tensor.matmul(bank[4 * g + c // 2][:, o], chunks(BM)[sl, c, :], kr, start=True, stop=True)
                    mm = nc.tensor.matmul(bank[4 * g + 2 + c // 2][:, o], chunks(KM)[sl, c, :], kr, start=True, stop=True)
                mm.then_inc(S("b_scores"), 1)
            pe.wait_ge(S("inv_mt1"), 2 + q + 1)
            for n, src in enumerate((proj[:, 24 + q, :], KM, BM)):
                for c in range(CH):
                    mm = nc.tensor.transpose(bank[4 + n][:, c * P:c * P + P], chunks(src)[:, c, :], ident)
            mm.then_inc(S("b_turned"), 1)
            pe.wait_ge(S("b_tok"), q + 1)

        def scores_dve(dve, step, q):
            m_i = incl.unsqueeze(1).broadcast_to([P, 2, P])
            m_s = strict.unsqueeze(1).broadcast_to([P, 2, P])
            for g in range(2):
                strict_v, with_y, with_v = b_scores(q, g)
                dve.wait_ge(S("b_scores"), 2 * q + g + 1)
                for cc in range(2):
                    by, bv = bank[4 * g + cc][:, :], bank[4 * g + 2 + cc][:, :]
                    by = by.rearrange("p (c x n) -> p c x n", c=2, x=2)
                    bv = bv.rearrange("p (c x n) -> p c x n", c=2, x=2)
                    two = slice(2 * cc, 2 * cc + 2)
                    step(nc.vector.tensor_tensor(chunks(with_y)[:, two, :], by[:, :, 1, :], m_i, ALU.mult))
                    step(nc.vector.tensor_tensor(chunks(strict_v)[:, two, :], bv[:, :, 0, :], m_s, ALU.mult))
                    step(nc.vector.tensor_tensor(chunks(with_v)[:, two, :], bv[:, :, 1, :], m_i, ALU.mult))
                    ins = nc.vector.tensor_copy(chunks(b_inv(q)[g][0])[:, two, :], by[:, :, 0, :])
                    if cc == 0:
                        step(ins)
                ins.then_inc(S(f"inv_mt{g}"), 1)
                dve.wait_ge(S(f"inv_mt{g}"), 2 + q + 1)

        def turned_act(act, step, q):
            act.wait_ge(S("b_turned"), q + 1)
            step(nc.scalar.activation(VT[q % 2], bank[4][:, :], ACT.Copy))
            step(nc.scalar.activation(KMT[q % 2], bank[5][:, :], ACT.Copy))
            nc.scalar.activation(BMT[q % 2], bank[6][:, :], ACT.Copy).then_inc(S("b_tok"), 1)

        def slot_pe(pe, q, k):
            if q < 0:
                return
            c, part = divmod(k, 3)
            n = CH * q + c
            kr = KR[q % 3]
            vt, kmt, bmt = VT[q % 2], KMT[q % 2], BMT[q % 2]
            if part == 0:
                if n > 0:
                    pe.wait_ge(S("b_o"), n)
                if c > 0:
                    pe.wait_ge(S("b_state"), (CH - 1) * q + c)
                    nc.tensor.matmul(bank[6][:, 0:P], kr[:, c, 0, :], Zb, start=True, stop=True)
                for g in range(2):
                    hs_ = slice(64 * g, 64 * g + 64)
                    mm = nc.tensor.matmul(bank[6][:, hs_], chunks(b_scores(q, g)[0])[:, c, :], chunks(vt)[:, c, hs_],
                                          start=(c == 0), stop=True, skip_group_check=True)
                mm.then_inc(S("b_r"), 1)
            elif part == 1:
                pe.wait_ge(S("b_rset"), n + 1)
                if c > 0:
                    pe.wait_ge(S("b_state"), (CH - 1) * q + c)
                for g in range(2):
                    hs_ = slice(64 * g, 64 * g + 64)
                    mm = nc.tensor.matmul(bank[7][:, hs_], chunks(b_inv(q)[g][2])[:, c, :], Rb[:, hs_], start=True, stop=True)
                mm.then_inc(S("b_y"), 1)
            else:
                pe.wait_ge(S("b_yset"), n + 1)
                nc.tensor.matmul(bank[7][:, 0:P], chunks(kmt)[:, c, :], chunks(vt)[:, c, :], start=True, stop=False)
                nc.tensor.matmul(bank[7][:, 0:P], chunks(bmt)[:, c, :], Yb, start=False, stop=True)
                if c > 0:
                    nc.tensor.matmul(bank[6][:, 0:P], Zb, kr[:, c, 1, :], start=True, stop=True)
                for g in range(2):
                    hs_ = slice(64 * g, 64 * g + 64)
                    _, wy, wv = b_scores(q, g)
                    nc.tensor.matmul(bank[6][hs_, 0:P], chunks(vt)[:, c, hs_], chunks(wv)[:, c, :], start=(c == 0), stop=(c > 0),
                                     skip_group_check=True)
                    mm = nc.tensor.matmul(bank[6][hs_, 0:P], Yb[:, hs_], chunks(wy)[:, c, :], start=False, stop=True,
                                          skip_group_check=True)
                mm.then_inc(S("b_out"), 1)

        def slot_dve(dve, step, q, k):
            if q < 0:
                return
            c, part = divmod(k, 3)
            n = CH * q + c
            if part == 0:
                dve.wait_ge(S("b_r"), n + 1)
                nc.vector.tensor_copy(Rb, bank[6][:, 0:P]).then_inc(S("b_rset"), 1)
            elif part == 1:
                dve.wait_ge(S("b_y"), n + 1)
                nc.vector.tensor_scalar(Yb, bank[7][:, 0:P], -1.0, None, ALU.mult).then_inc(S("b_yset"), 1)
            elif c < CH - 1:
                dve.wait_ge(S("b_out"), n + 1)
                step(nc.vector.tensor_tensor(Zt, bank[7][:, 0:P], bones, ALU.mult))
                if c > 0:
                    step(nc.vector.tensor_tensor(Zt, Zt, Zb, ALU.add))
                nc.vector.tensor_scalar(Zb, Zt, egc[q % 3][:, c:c + 1], egm[q % 3][:, c + 1:c + 2], ALU.mult,
                                        ALU.mult).then_inc(S("b_state"), 1)
                dve.wait_ge(S("b_state"), (CH - 1) * q + c + 1)

        def slot_act(act, q, k):
            c, part = divmod(k, 3)
            if q >= 0 and part == 2:
                act.wait_ge(S("b_out"), CH * q + c + 1)
                nc.scalar.activation(hT[:, 4 + q, c * P:c * P + P], bank[6][:, 0:P], ACT.Copy).then_inc(S("b_o"), 1)

        def rwkv_norm_dve(dve, step):
            for n in range(BT + 1):
                if n < BT:
                    o = hT[:, 4 + n, :]
                    if n >= 2:
                        dve.wait_ge(S("b_bonus"), n - 1)
                    nc.vector.scalar_tensor_tensor(out=RK[n % 2], in0=proj[:, 16 + n, :], scalar=pc("rk", n),
                                                   in1=proj[:, 20 + n, :], op0=ALU.mult, op1=ALU.mult).then_inc(S("b_rk"), 1)
                    dve.wait_ge(S("b_mean"), n + 1)
                    nc.vector.scalar_tensor_tensor(out=o, in0=bank[n % 2][:, :], scalar=-1.0 / 64, in1=o, op0=ALU.mult,
                                                   op1=ALU.add).then_inc(S("b_centred"), 1)
                q = n - 1
                if q >= 0:
                    o = hT[:, 4 + q, :]
                    dve.wait_ge(S("b_bonus"), q + 1)
                    step(nc.vector.tensor_tensor(BV[q % 2], bank[2 + q % 2][:, :], proj[:, 24 + q, :], ALU.mult))
                    dve.wait_ge(S("head_rstd"), q + 1 + 16)
                    step(nc.vector.scalar_tensor_tensor(out=o, in0=o, scalar=pc("lnw", q), in1=B_RS[q % 2], op0=ALU.mult,
                                                        op1=ALU.mult))
                    step(nc.vector.scalar_tensor_tensor(out=o, in0=o, scalar=pc("lnb", q), in1=BV[q % 2], op0=ALU.add,
                                                        op1=ALU.add))
                    nc.vector.tensor_tensor(o, o, GATE[q], ALU.mult).then_inc(S("b_done"), 1)
            dve.wait_ge(S("b_done"), BT)

        def rwkv_norm_act(act, step):
            for q in range(BT):
                act.wait_ge(S("b_centred"), q + 1)
                nc.scalar.activation(B_SQ[q % 2], hT[:, 4 + q, :], ACT.Square).then_inc(S("head_squared"), 1)
                act.wait_ge(S("head_summed"), q + 1 + 16)
                step(nc.scalar.activation(B_LN, bank[4 + q % 2][:, :], ACT.Ln, bias=epsg, scale=1.0 / 64))
                if q >= 2:
                    act.wait_ge(S("b_done"), q - 1)
                nc.scalar.activation(B_RS[q % 2], B_LN, ACT.Exp, scale=-0.5).then_inc(S("head_rstd"), 1)
                act.wait_ge(S("head_rstd"), q + 1 + 16)

        def rwkv_norm_pe(pe):
            def mean(q):
                if q >= 2:
                    pe.wait_ge(S("b_centred"), q - 1)
                nc.tensor.matmul(bank[q % 2][:, :], bones, hT[:, 4 + q, :], start=True, stop=True).then_inc(S("b_mean"), 1)

            pe.wait_ge(S("b_o"), CH * BT)
            mean(0)
            for q in range(BT):
                if q + 1 < BT:
                    mean(q + 1)
                pe.wait_ge(S("b_rk"), q + 1)
                if q >= 2:
                    pe.wait_ge(S("b_done"), q - 1)
                nc.tensor.matmul(bank[2 + q % 2][:, :], bones, RK[q % 2], start=True, stop=True).then_inc(S("b_bonus"), 1)
                pe.wait_ge(S("head_squared"), q + 1 + 16)
                if q >= 2:
                    pe.wait_ge(S("head_rstd"), q - 1 + 16)
                nc.tensor.matmul(bank[4 + q % 2][:, :], bones, B_SQ[q % 2], start=True, stop=True).then_inc(S("head_summed"), 1)
            pe.wait_ge(S("b_done"), BT)

        def mixer0_dve(dve, step):
            delta_prep_dve(dve, step)
            dve.wait_ge(S("tile_free0"), 2 + N_IN)
            dve.wait_ge(S("tile_free1"), 2 + N_IN)
            step(nc.vector.tensor_scalar(omka, par[:, PC["ka"]:PC["ka"] + 4], -1.0, 1.0, ALU.mult, ALU.add))
            for r in range(2):
                delta_round_dve(dve, step, r, lambda k: lerp_dve(dve, step, 7 * r + k // 2) if k % 2 == 0 else
                                (lerp_dve(dve, step, 7 * r + 6) if k == 11 else None))
            for c in range(CH):
                delta_chunk_dve(dve, step, c)
                keys_dve(dve, step, c)
                delta_state_dve(dve, step, c)
                unit_keys_dve(dve, step, c)
            for n in range(AH + 2):
                delta_norm_dve(dve, step, n)
                if n < 5:
                    scale_dve(dve, step, 0, n)
            dve.wait_ge(S("a_done"), AH)
            for q in range(BT):
                scores_dve(dve, step, q)

                def between(k):
                    slot_dve(dve, step, q - 1, k)
                    if k % 2 == 0 and k < 10 and q + 1 < BT:
                        scale_dve(dve, step, q + 1, k // 2)
                inv_dve(dve, 2 + q, b_inv(q), between)
            for k in range(12):
                slot_dve(dve, step, BT - 1, k)
            rwkv_norm_dve(dve, step)

        def mixer0_act(act, step):
            delta_prep_act(act, step)
            for r in range(2):
                delta_round_act(act, step, r)
            act.wait_ge(S("b_lerp"), 14)
            step(nc.scalar.activation(TH[0:64, :], proj[0:64, 28, :], ACT.Tanh))
            nc.scalar.activation(SGL, proj[:, 29, :], ACT.Sigmoid).then_inc(S("b_lora"), 1)
            for c in range(CH):
                delta_chunk_act(act, step, c)
                keys_act(act, step, c)
                delta_out_act(act, step, c)
            act.wait_ge(S("a_o"), CH)
            for n in range(AH + 1):
                delta_norm_act(act, step, n)
                if n == 0:
                    scale_act(act, step, 0)
            for q in range(BT):
                turned_act(act, step, q)

                def between(k):
                    if k == 0 and q + 1 < BT:
                        scale_act(act, step, q + 1)
                    slot_act(act, q - 1, k)
                inv_act(act, 2 + q, b_inv(q), between)
            for k in range(12):
                slot_act(act, BT - 1, k)
            act.wait_ge(S("b_o"), CH * BT)
            rwkv_norm_act(act, step)

        def mixer0_pe(pe):
            delta_prep_pe(pe)
            for r in range(2):
                delta_round_pe(pe, r)
            for g in range(2):
                pe.wait_ge(S(f"inv_tt{g}"), 14)
            pe.wait_ge(S("b_lora"), 1)
            low_pe(pe, 0)
            for c in range(CH):
                delta_chunk_pe(pe, c)
                key_sums_pe(pe, c)
                delta_out_pe(pe, c)
                if c + 1 < CH:
                    low_pe(pe, c + 1)
            pe.wait_ge(S("b_rates"), BT)
            pe.wait_ge(S("head_rstd"), 12)
            for n in range(AH + 1):
                delta_norm_pe(pe, n)
            pe.wait_ge(S("a_done"), AH)
            pe.wait_ge(S("a_o"), CH)
            for q in range(BT):
                scores_pe(pe, q)
                inv_pe(pe, 2 + q, b_inv(q), lambda k: slot_pe(pe, q - 1, k))
                for g in range(2):
                    pe.wait_ge(S(f"inv_tt{g}"), 7 * (3 + q))
            for k in range(12):
                slot_pe(pe, BT - 1, k)
            rwkv_norm_pe(pe)

        Dt, Et, Qs, Ks = W[0:3], W[3:6], W[6:9], X[0:3]
        ACC, KD, KDT, VTc = X[3:5], W[9:11], [X[5]] * 2, [X[6]] * 2
        St = [X[7]] * 2
        sqt, lnt, rst = W[11], W[12], W[13]
        UN = 8
        UNITS = UN * CHEADS
        sbk = [bank[0], bank[1], bank[7]]

        def ended(u, after):
            h, r = divmod(u - after + 1, UN)
            return [h - 1] if r == 0 and 1 <= h <= CHEADS else []

        def halves(ap, s):
            return ap.rearrange("p (b x s) -> p b x s", x=2, s=s)

        def middle(ap, s):
            return halves(ap, s)[:, :, 0, s - 1:s].broadcast_to([P, T // (2 * s), s])

        lbv, oml = small[:, 200:208], small[:, 208:216]
        eC = small[:, 216:224].rearrange("p (a c) -> p a c", a=2)

        def hgrn_dve(dve, step):
            nc.vector.tensor_tensor(small[:, 192:200], par[:, PC["lb"]:PC["lb"] + 8], par[:, PC["lb"] + 8:PC["lb"] + 16],
                                    ALU.subtract).then_inc(S("c_lb"), 1)
            dve.wait_ge(S("tile_free0"), 2 + B_COUT)
            dve.wait_ge(S("tile_free1"), 2 + B_COUT)
            for h in range(CHEADS):
                f, k = proj[:, 8 + h, :], hT[:, h, :]
                dve.wait_ge(S("c_sig"), h + 1)
                step(nc.vector.tensor_scalar(k, k, oml[:, h:h + 1], None, ALU.mult))
                nc.vector.tensor_scalar(f, f, oml[:, h:h + 1], lbv[:, h:h + 1], ALU.mult, ALU.add).then_inc(S("c_f"), 1)
            for h in range(CHEADS):
                dve.wait_ge(S("c_ln"), h + 1)
                step(nc.vector.tensor_tensor_scan(proj[:, 8 + h, :], reset, W[h], 0.0, ALU.mult, ALU.add))

            def spread(u):
                h, li = divmod(u, UN)
                if li == 7:
                    return
                n, s = 7 * h + li, LEVELS[li]
                g = proj[:, 8 + h, :]
                if n >= 3:
                    dve.wait_ge(S("c_e"), n - 2)
                nc.vector.tensor_tensor(halves(Dt[n % 3], s)[:, :, 1, :], halves(g, s)[:, :, 1, :], middle(g, s), ALU.subtract)
                nc.vector.tensor_tensor(halves(Dt[n % 3], s)[:, :, 0, :], middle(g, s), halves(g, s)[:, :, 0, :],
                                        ALU.subtract).then_inc(S("c_d"), 1)

            def queries(u):
                h, li = divmod(u, UN)
                if li == 7:
                    return
                n, s = 7 * h + li, LEVELS[li]
                dve.wait_ge(S("c_e"), n + 1)
                if n >= 3:
                    dve.wait_ge(S("c_s"), u - 2 - (1 if li < 3 and h > 0 else 0))
                nc.vector.tensor_tensor(halves(Qs[n % 3], s)[:, :, 1, :], halves(proj[:, h, :], s)[:, :, 1, :],
                                        halves(Et[n % 3], s)[:, :, 1, :], ALU.mult).then_inc(S("c_q"), 1)

            def gather(u):
                h, li = divmod(u, UN)
                acc = chunks(ACC[h % 2])
                if li == 0:
                    if h >= 2:
                        dve.wait_ge(S("c_o"), h - 1)
                    step(nc.vector.memset(ACC[h % 2], 0.0))
                dve.wait_ge(S("c_s"), u + 1)
                m = lvl[li] if li < 7 else ident
                nc.vector.copy_predicated(acc, over4(m).bitcast(I32), chunks(sbk[u % 3][:, :])).then_inc(S("c_acc"), 1)
                dve.wait_ge(S("c_acc"), u + 1)

            def rest(h):
                g = proj[:, 8 + h, :]
                last = chunks(g)[:, :, P - 1:P].broadcast_to([P, CH, P])
                if h >= 2:
                    dve.wait_ge(S("c_turned"), h - 1)
                nc.vector.tensor_tensor(chunks(KD[h % 2]), last, chunks(g), ALU.subtract).then_inc(S("c_rest"), 1)

            def decayed_q(h):
                dve.wait_ge(S("c_tail_e"), h + 1)
                nc.vector.tensor_tensor(proj[:, h, :], proj[:, h, :], proj[:, 8 + h, :], ALU.mult).then_inc(S("c_qg"), 1)

            def states(h):
                dve.wait_ge(S("c_incr"), h + 1)
                if h >= 1:
                    dve.wait_ge(S("c_o"), h)
                st = chunks(St[h % 2])
                step(nc.vector.tensor_copy(st[:, 1, :], bank[4][:, 0:P]))
                step(nc.vector.scalar_tensor_tensor(out=st[:, 2, :], in0=st[:, 1, :], scalar=eC[:, h % 2, 1:2],
                                                    in1=bank[4][:, P:2 * P], op0=ALU.mult, op1=ALU.add))
                nc.vector.scalar_tensor_tensor(out=st[:, 3, :], in0=st[:, 2, :], scalar=eC[:, h % 2, 2:3],
                                               in1=bank[4][:, 2 * P:3 * P], op0=ALU.mult, op1=ALU.add).then_inc(S("c_state"), 1)

            def close(h):
                o = hT[:, h, :]
                dve.wait_ge(S("head_rstd"), h + 1 + 20)
                step(nc.vector.scalar_tensor_tensor(out=o, in0=o, scalar=pc("onC"), in1=rst, op0=ALU.mult, op1=ALU.mult))
                nc.vector.tensor_tensor(o, o, proj[:, 24 + h, :], ALU.mult).then_inc(S("c_done"), 1)

            spread(0)
            spread(1)
            for u in range(UNITS + 12):
                if u + 2 < UNITS:
                    spread(u + 2)
                if u < UNITS:
                    queries(u)
                if 0 <= u - 2 < UNITS:
                    gather(u - 2)
                for h in ended(u, 1):
                    rest(h)
                for h in ended(u, 3):
                    decayed_q(h)
                for h in ended(u, 6):
                    states(h)
                for h in ended(u, 11):
                    close(h)
            dve.wait_ge(S("c_done"), CHEADS)

        def hgrn_act(act, step):
            act.wait_ge(S("c_lb"), 1)
            step(nc.scalar.activation(lbv, small[:, 192:200], ACT.Sigmoid, scale=-1.0))
            step(nc.scalar.activation(oml, small[:, 192:200], ACT.Sigmoid))
            act.wait_ge(S("tile_free0"), 2 + B_COUT)
            act.wait_ge(S("tile_free1"), 2 + B_COUT)
            for h in range(CHEADS):
                nc.scalar.activation(hT[:, h, :], proj[:, 8 + h, :], ACT.Sigmoid, scale=-1.0).then_inc(S("c_sigk"), 1)
                act.wait_ge(S("c_sigk"), h + 1)
                nc.scalar.activation(proj[:, 8 + h, :], proj[:, 8 + h, :], ACT.Sigmoid).then_inc(S("c_sig"), 1)
            for h in range(CHEADS):
                step(nc.scalar.activation(proj[:, h, :], proj[:, h, :], ACT.Silu))
                nc.scalar.activation(proj[:, 24 + h, :], proj[:, 24 + h, :], ACT.Silu).then_inc(S("c_silu"), 1)
            act.wait_ge(S("c_silu"), CHEADS)
            for h in range(CHEADS):
                act.wait_ge(S("c_f"), h + 1)
                nc.scalar.activation(W[h], proj[:, 8 + h, :], ACT.Ln).then_inc(S("c_ln"), 1)

            def exps(u):
                h, li = divmod(u, UN)
                if li == 7:
                    return
                n = 7 * h + li
                act.wait_ge(S("c_d"), n + 1)
                if n >= 3:
                    act.wait_ge(S("c_q"), n - 2)
                    act.wait_ge(S("c_k"), n - 2)
                nc.scalar.activation(Et[n % 3], Dt[n % 3], ACT.Exp).then_inc(S("c_e"), 1)

            exps(0)
            exps(1)
            for u in range(UNITS + 12):
                if u + 2 < UNITS:
                    exps(u + 2)
                for h in ended(u, 2):
                    act.wait_ge(S("c_rest"), h + 1)
                    step(nc.scalar.activation(KD[h % 2], KD[h % 2], ACT.Exp))
                    if h >= 2:
                        act.wait_ge(S("c_state"), h - 1)
                    step(nc.scalar.activation(eC[:, h % 2, :], proj[:, 8 + h, P - 1:T:P], ACT.Exp))
                    nc.scalar.activation(proj[:, 8 + h, :], proj[:, 8 + h, :], ACT.Exp).then_inc(S("c_tail_e"), 1)
                for h in ended(u, 4):
                    act.wait_ge(S("c_turned"), h + 1)
                    if h >= 1:
                        act.wait_ge(S("c_o"), h)
                    step(nc.scalar.activation(KDT[h % 2], bank[2][:, :], ACT.Copy))
                    nc.scalar.activation(VTc[h % 2], bank[3][:, :], ACT.Copy).then_inc(S("c_tok"), 1)
                for h in ended(u, 8):
                    act.wait_ge(S("c_o"), h + 1)
                    nc.scalar.activation(hT[:, h, :], bank[5][:, :], ACT.Copy).then_inc(S("c_oset"), 1)
                    act.wait_ge(S("c_oset"), h + 1)
                    nc.scalar.activation(sqt, hT[:, h, :], ACT.Square).then_inc(S("head_squared"), 1)
                for h in ended(u, 10):
                    act.wait_ge(S("head_summed"), h + 1 + 20)
                    step(nc.scalar.activation(lnt, bank[6][:, :], ACT.Ln, bias=eps6, scale=1.0 / P))
                    if h > 0:
                        act.wait_ge(S("c_done"), h)
                    nc.scalar.activation(rst, lnt, ACT.Exp, scale=-0.5).then_inc(S("head_rstd"), 1)

        def hgrn_pool(pool):
            for u in range(UNITS + 12):
                h, li = divmod(u, UN)
                if u < UNITS and li < 7:
                    n, s = 7 * h + li, LEVELS[li]
                    pool.wait_ge(S("c_e"), n + 1)
                    if n >= 3:
                        pool.wait_ge(S("c_s"), u - 2 - (1 if li < 3 and h > 0 else 0))
                    nc.gpsimd.tensor_tensor(halves(Ks[n % 3], s)[:, :, 0, :], halves(hT[:, h, :], s)[:, :, 0, :],
                                            halves(Et[n % 3], s)[:, :, 0, :], ALU.mult).then_inc(S("c_k"), 1)
                for h in ended(u, 3):
                    pool.wait_ge(S("c_tail_e"), h + 1)
                    nc.gpsimd.tensor_tensor(KD[h % 2], KD[h % 2], hT[:, h, :], ALU.mult).then_inc(S("c_kd"), 1)

        def hgrn_pe(pe):
            pe.wait_ge(S("c_silu"), CHEADS)
            pe.wait_ge(S("c_f"), CHEADS)
            for u in range(UNITS + 12):
                if u < UNITS:
                    h, li = divmod(u, UN)
                    if u >= 3:
                        pe.wait_ge(S("c_acc"), u - 2)
                    n = 7 * h + li
                    k, q = hT[:, h, :], proj[:, h, :]
                    if li < 7:
                        pe.wait_ge(S("c_q"), n + 1)
                        pe.wait_ge(S("c_k"), n + 1)
                        k, q = Ks[n % 3], Qs[n % 3]
                    for c in range(CH):
                        mm = nc.tensor.matmul(sbk[u % 3][:, c * P:c * P + P], chunks(k)[:, c, :], chunks(q)[:, c, :],
                                              start=True, stop=True)
                    mm.then_inc(S("c_s"), 1)
                for h in ended(u, 3):
                    if h > 0:
                        pe.wait_ge(S("c_tok"), h)
                    for c in range(CH):
                        nc.tensor.transpose(bank[3][:, c * P:c * P + P], chunks(proj[:, 16 + h, :])[:, c, :], ident)
                    pe.wait_ge(S("c_kd"), h + 1)
                    for c in range(CH):
                        mm = nc.tensor.transpose(bank[2][:, c * P:c * P + P], chunks(KD[h % 2])[:, c, :], ident)
                    mm.then_inc(S("c_turned"), 1)
                for h in ended(u, 5):
                    pe.wait_ge(S("c_tok"), h + 1)
                    if h > 0:
                        pe.wait_ge(S("c_state"), h)
                    for c in range(CH - 1):
                        mm = nc.tensor.matmul(bank[4][:, c * P:c * P + P], chunks(KDT[h % 2])[:, c, :], chunks(VTc[h % 2])[:, c, :],
                                              start=True, stop=True)
                    mm.then_inc(S("c_incr"), 1)
                for h in ended(u, 7):
                    pe.wait_ge(S("c_state"), h + 1)
                    pe.wait_ge(S("c_qg"), h + 1)
                    pe.wait_ge(S("c_acc"), UN * (h + 1))
                    if h > 0:
                        pe.wait_ge(S("c_oset"), h)
                    for c in range(CH):
                        if c > 0:
                            nc.tensor.matmul(bank[5][:, c * P:c * P + P], chunks(St[h % 2])[:, c, :], chunks(proj[:, h, :])[:, c, :],
                                             start=True, stop=False)
                        mm = nc.tensor.matmul(bank[5][:, c * P:c * P + P], chunks(VTc[h % 2])[:, c, :],
                                              chunks(ACC[h % 2])[:, c, :], start=(c == 0), stop=True)
                    mm.then_inc(S("c_o"), 1)
                for h in ended(u, 9):
                    pe.wait_ge(S("head_squared"), h + 1 + 20)
                    if h > 0:
                        pe.wait_ge(S("head_rstd"), h + 20)
                    nc.tensor.matmul(bank[6][:, :], ones, sqt, start=True, stop=True).then_inc(S("head_summed"), 1)

        memn = proj[:, 24:32, :]
        PX = [work[:, 2 * i:2 * i + 2, :].rearrange("p a (t n) -> p (a t) n", n=M) for i in range(2)]
        PXT = W[4:6]
        mx = small[:, 224:232].rearrange("p (a t) -> p a t", a=2)
        sm = small[:, 232:240].rearrange("p (a t) -> p a t", a=2)
        XSC = (D // XH) ** -0.5

        def sbank(x):
            return [bank[4 + 2 * (x % 2) + i][:, :].rearrange("p (t n) -> p t n", n=M) for i in range(2)]

        def xattn_dve(dve, step, L):
            for x in range(XH):
                n = XH * L + x
                dve.wait_ge(S("x_scores"), n + 1)
                if x >= 1:
                    dve.wait_ge(S("x_probs"), n)
                for i in range(2):
                    step(nc.vector.tensor_reduce(mx[:, x % 2, 2 * i:2 * i + 2], sbank(x)[i], AX.X, ALU.max))
                nc.vector.tensor_scalar(mx[:, x % 2, :], mx[:, x % 2, :], -XSC, None, ALU.mult).then_inc(S("x_max"), 1)
                dve.wait_ge(S("x_exp"), n + 1)
                step(nc.vector.reciprocal(sm[:, x % 2, :], sm[:, x % 2, :]))
                for t in range(CH):
                    ins = nc.vector.tensor_scalar(PX[x % 2][:, t, :], PX[x % 2][:, t, :], sm[:, x % 2, t:t + 1], None, ALU.mult)
                ins.then_inc(S("x_probs"), 1)
                dve.wait_ge(S("x_turned"), n + 1)
                step(nc.vector.tensor_copy(PXT[0], bank[0][:, :]))
                nc.vector.tensor_copy(PXT[1], bank[1][:, :]).then_inc(S("x_pt"), 1)

        def xattn_act(act, step, L):
            def out(x):
                act.wait_ge(S("x_out"), XH * L + x + 1)
                step(nc.scalar.activation(hT[:, 2 * x, :], bank[2][:, :], ACT.Copy))
                nc.scalar.activation(hT[:, 2 * x + 1, :], bank[3][:, :], ACT.Copy).then_inc(S("x_o"), 1)

            for x in range(XH):
                n = XH * L + x
                act.wait_ge(S("x_max"), n + 1)
                if x >= 2:
                    act.wait_ge(S("x_turned"), n - 1)
                for t in range(CH):
                    ins = nc.scalar.activation(PX[x % 2][:, t, :], sbank(x)[t // 2][:, t % 2, :], ACT.Exp, bias=mx[:, x % 2, t:t + 1],
                                               scale=XSC, accum_out=sm[:, x % 2, t:t + 1])
                    if t < CH - 1:
                        step(ins)
                ins.then_inc(S("x_exp"), 1)
                if x > 0:
                    out(x - 1)
            out(XH - 1)

        def xattn_pe(pe, L):
            first = B_XA0 if L == 0 else B_XA1
            pe.wait_ge(S("tile_free0"), 2 + first + 12)
            pe.wait_ge(S("tile_free1"), 2 + first + 12)

            def scores(x):
                if x >= 2:
                    pe.wait_ge(S("x_exp"), XH * L + x - 1)
                for t in range(CH):
                    for d in range(2):
                        mm = nc.tensor.matmul(sbank(x)[t // 2][:, t % 2, :], chunks(proj[:, 16 + 2 * x + d, :])[:, t, :],
                                              proj[:, 2 * x + d, 0:M], start=(d == 0), stop=(d == 1))
                mm.then_inc(S("x_scores"), 1)

            scores(0)
            for x in range(XH):
                n = XH * L + x
                if x + 1 < XH:
                    scores(x + 1)
                pe.wait_ge(S("x_probs"), n + 1)
                if x > 0:
                    pe.wait_ge(S("x_pt"), n)
                for m in range(2):
                    for t in range(CH):
                        mm = nc.tensor.transpose(bank[m][:, t * P:t * P + P], PX[x % 2][:, t, m * P:m * P + P], ident)
                mm.then_inc(S("x_turned"), 1)
                pe.wait_ge(S("x_pt"), n + 1)
                if x > 0:
                    pe.wait_ge(S("x_o"), n)
                for d in range(2):
                    for m in range(2):
                        mm = nc.tensor.matmul(bank[2 + d][:, :], proj[:, 8 + 2 * x + m, d * P:d * P + P], PXT[m],
                                              start=(m == 0), stop=(m == 1))
                mm.then_inc(S("x_out"), 1)
            pe.wait_ge(S("x_o"), XH * (L + 1))

        htok = proj[:, 0:8, :].rearrange("p (t a) n -> p t (a n)", a=2)
        y1 = htok
        y2 = proj[:, 8:16, :].rearrange("p (t a) n -> p t (a n)", a=2)
        xg = [proj[:, 8 + 2 * i:10 + 2 * i, :].rearrange("p a n -> p (a n)") for i in range(2)]
        xgT = [proj[:, 12 + 2 * i:14 + 2 * i, :].rearrange("p a (b n) -> p (a b) n", n=P) for i in range(2)]
        ysb = [proj[:, 16 + 2 * i:18 + 2 * i, :] for i in range(2)]
        hs = [W[i][:, 0:FF] for i in range(2)]
        hid = [W[2 + i][:, 0:FF] for i in range(2)]
        hidT = [W[4 + i][:, 0:FF].rearrange("p (a n) -> p a n", a=2) for i in range(2)]
        w13 = [ring[:, 3 * i:3 * i + 2, :].rearrange("p a n -> p (a n)").rearrange("p (k n) -> p k n", k=DT) for i in range(2)]
        w2e = [ring[:, 3 * i + 2, :].rearrange("p (k n) -> p k n", k=2) for i in range(2)]

        def sm3(o, *dims):
            n = int(np.prod(dims))
            names = ["a", "b", "c"][:len(dims)]
            pat = f"p ({' '.join(names)}) -> p {' '.join(names)}"
            return small[:, o:o + n].rearrange(pat, **dict(zip(names, dims)))

        lg = sm3(256, CH, 20)
        gl, el = lg[:, :, 0:4], lg[:, :, 4:20].rearrange("p t (g i) -> p t g i", g=4)
        oh = sm3(336, CH, NG)
        oh1, oh2 = sm3(352, CH, EG), sm3(368, CH, EG)
        ing, sh = sm3(384, CH, EG), sm3(400, CH, NG)
        wt = sm3(416, CH, 4)
        gmax, gsum, m1, m2 = (small[:, 432 + 4 * i:436 + 4 * i] for i in range(4))
        gate1, gate2, e2, tmp4 = (small[:, 448 + 4 * i:452 + 4 * i] for i in range(4))
        sel1, sel2, sel = sm3(464, CH, NG, EG), sm3(528, CH, NG, EG), sm3(592, CH, NE)
        pre = sm3(656, CH, NE)
        tot = small[:, 720:736]
        nblk, incl_b = small[:, 736:752], small[:, 752:768]
        tmp64 = sm3(768, CH, NE)
        row12 = small[:, 832:840]
        rowbase = small[:, 840:856]
        emapf = small[:, 856:856 + ITEMS]
        rows_i = smalli[:, 0:8]
        emap_i = smalli[:, 8:8 + ITEMS]
        pairs_i = smalli[0:1, 8 + ITEMS:10 + ITEMS]
        pairs_f = small[:, 880:888]

        def item_turns(eng, L):
            def load(l):
                return eng.value_load(pairs_i[:, l:l + 1], min_val=2, max_val=ITEMS // 2)
            return load(L), (load(0) if L else 0)
        cmp = W[6][:, 0:ITEMS * NE].rearrange("p (i e) -> p i e", e=NE)
        wts = con[:, C_WTS:C_WTS + 4]
        iota = con[:, C_IOTA:C_IOTA + ITEMS]

        def bc3(ap, n):
            return ap.unsqueeze(2).broadcast_to([P, CH, n])

        def first_only(step, dst, src, m):
            step(nc.vector.tensor_tensor(dst, src, bc3(m, 4), ALU.is_equal))
            step(nc.vector.tensor_tensor(dst, dst, wts.unsqueeze(1).broadcast_to([P, CH, 4]), ALU.mult))
            step(nc.vector.tensor_reduce(tmp4, dst, AX.X, ALU.max))
            step(nc.vector.tensor_tensor(dst, dst, bc3(tmp4, 4), ALU.is_equal))

        def moe_dve(dve, step, L):
            bge = par[:, PC["bge"] + 20 * L:PC["bge"] + 20 * L + 20]
            dve.wait_ge(S("m_logits"), L + 1)
            step(nc.vector.tensor_tensor(lg, bank[4][:, 0:80].rearrange("p (t n) -> p t n", n=20),
                                         bge.unsqueeze(1).broadcast_to([P, CH, 20]), ALU.add))
            step(nc.vector.tensor_reduce(gmax, gl, AX.X, ALU.max))
            nc.vector.tensor_tensor(sh, gl, bc3(gmax, 4), ALU.subtract).then_inc(S("m_shift"), 1)
            first_only(step, oh, gl, gmax)
            t4 = tmp64.rearrange("p t (g i) -> p t g i", g=4)
            step(nc.vector.tensor_tensor(t4, el, oh.unsqueeze(3).broadcast_to([P, CH, NG, EG]), ALU.mult))
            step(nc.vector.tensor_reduce(ing, t4.rearrange("p t g i -> p t i g"), AX.X, ALU.add))
            step(nc.vector.tensor_reduce(m1, ing, AX.X, ALU.max))
            first_only(step, oh1, ing, m1)
            step(nc.vector.scalar_tensor_tensor(out=wt, in0=oh1, scalar=-1e30, in1=ing, op0=ALU.mult, op1=ALU.add))
            step(nc.vector.tensor_reduce(m2, wt, AX.X, ALU.max))
            first_only(step, oh2, wt, m2)
            nc.vector.tensor_tensor(e2, m2, m1, ALU.subtract).then_inc(S("m_shift"), 1)
            for dst, o in ((sel1, oh1), (sel2, oh2)):
                step(nc.vector.tensor_tensor(dst, oh.unsqueeze(3).broadcast_to([P, CH, NG, EG]),
                                             o.unsqueeze(2).broadcast_to([P, CH, NG, EG]), ALU.mult))
            s1, s2 = (a.rearrange("p t g i -> p t (g i)") for a in (sel1, sel2))
            step(nc.vector.tensor_tensor(sel, s1, s2, ALU.add))
            step(nc.vector.memset(pre[:, 0, :], 0.0))
            for t in range(1, CH):
                step(nc.vector.tensor_tensor(pre[:, t, :], pre[:, t - 1, :], sel[:, t - 1, :], ALU.add))
            nc.vector.tensor_tensor(tot, pre[:, 3, :], sel[:, 3, :], ALU.add).then_inc(S("m_sel"), 1)
            dve.wait_ge(S("m_exp"), L + 1)
            step(nc.vector.tensor_reduce(gsum, sh, AX.X, ALU.add))
            step(nc.vector.tensor_scalar(gate1, e2, 1.0, None, ALU.add))
            step(nc.vector.tensor_tensor(gate1, gate1, gsum, ALU.mult))
            step(nc.vector.reciprocal(gate1, gate1))
            step(nc.vector.tensor_tensor(gate2, gate1, e2, ALU.mult))
            dve.wait_ge(S("m_ranks"), L + 1)
            cnt = bank[5][:, 64:80]
            step(nc.vector.tensor_scalar(nblk, cnt, 0.0, None, ALU.is_gt))
            for b in range(1, CH):
                step(nc.vector.scalar_tensor_tensor(out=nblk, in0=cnt, scalar=float(P * b), in1=nblk, op0=ALU.is_gt, op1=ALU.add))
            step(nc.vector.tensor_tensor_scan(incl_b, ones[:, 0:NE], nblk, 0.0, ALU.mult, ALU.add))
            step(nc.vector.tensor_tensor(rowbase, incl_b, nblk, ALU.subtract))
            step(nc.vector.tensor_scalar(rowbase, rowbase, float(P), None, ALU.mult))
            step(nc.vector.tensor_tensor(tmp64, bank[5][:, 0:64].rearrange("p (t e) -> p t e", e=NE),
                                         rowbase.unsqueeze(1).broadcast_to([P, CH, NE]), ALU.add))
            step(nc.vector.tensor_tensor(pre, tmp64, s1, ALU.mult))
            step(nc.vector.tensor_reduce(row12[:, 0:4], pre, AX.X, ALU.add))
            step(nc.vector.tensor_tensor(pre, tmp64, s2, ALU.mult))
            step(nc.vector.tensor_reduce(row12[:, 4:8], pre, AX.X, ALU.add))
            nc.vector.tensor_copy(rows_i, row12).then_inc(S("m_plan"), 1)
            step(nc.vector.tensor_tensor(cmp, incl_b.unsqueeze(1).broadcast_to([P, ITEMS, NE]),
                                         iota.unsqueeze(2).broadcast_to([P, ITEMS, NE]), ALU.is_le))
            step(nc.vector.tensor_reduce(emapf, cmp, AX.X, ALU.add))
            step(nc.vector.tensor_scalar(emapf, emapf, float(NE - 1), None, ALU.min))
            step(nc.vector.tensor_copy(emap_i, emapf))
            step(nc.vector.tensor_scalar(cmp[:, :, 0], iota, incl_b[:, NE - 1:NE], None, ALU.is_lt))
            step(nc.vector.tensor_reduce(pairs_f[:, 0:1], cmp[:, 0:ITEMS:2, 0], AX.X, ALU.add))
            nc.vector.tensor_copy(smalli[:, 8 + ITEMS + L:9 + ITEMS + L], pairs_f[:, 0:1]).then_inc(S("m_plan"), 1)
            dve.wait_ge(S("m_plan"), 2 * L + 2)
            turns, before = item_turns(dve, L)
            base = 2 * before
            for t in range(CH):
                dve.wait_ge(S("m_tok_ready"), CH * L + t + 1)
                nc.vector.tensor_copy(htok[:, t, 0:T], bank[2 * (t % 2)][:, :]).then_inc(S("m_tok0"), 1)
            with dve.Fori(0, turns) as i:
                for u in range(2):
                    n = 2 * i + (base + u)
                    dve.wait_ge(S("m_xt_ready"), n + 1)
                    nc.vector.tensor_copy(xgT[u][:, 0:4, :], chunks(bank[0][:, :])).then_inc(S("m_xt0"), 1)
                for u in range(2):
                    n = 2 * i + (base + u)
                    dve.wait_ge(S("m_silu"), n + 1)
                    nc.vector.tensor_tensor(hid[u], hs[u], bank[2 + u][:, FF:2 * FF], ALU.mult).then_inc(S("m_hid"), 1)
                for u in range(2):
                    n = 2 * i + (base + u)
                    dve.wait_ge(S("m_ht_ready"), n + 1)
                    nc.vector.tensor_copy(hidT[u], bank[4 + u][:, 0:256].rearrange("p (a n) -> p a n", a=2)).then_inc(
                        S("m_ht"), 1)
                for u in range(2):
                    n = 2 * i + (base + u)
                    dve.wait_ge(S("m_y_ready"), n + 3)
                    dve.wait_ge(S(f"m_y_sent{u}"), (i + before + 1) * 16)
                    nc.vector.tensor_copy(ysb[u][:, 0, :], bank[6][:, :]).then_inc(S("m_y0"), 1)
            for t in range(CH):
                dve.wait_ge(S("m_got"), 128 * (L + 1))
                step(nc.vector.tensor_scalar(y1[:, t, :], y1[:, t, :], gate1[:, t:t + 1], None, ALU.mult))
                nc.vector.scalar_tensor_tensor(out=y1[:, t, :], in0=y2[:, t, :], scalar=gate2[:, t:t + 1], in1=y1[:, t, :],
                                               op0=ALU.mult, op1=ALU.add).then_inc(S("m_mix"), 1)
            for k in range(DT):
                dve.wait_ge(S("m_back"), DT * L + k + 1)
                nc.vector.tensor_tensor(xT[:, k, :], xT[:, k, :], bank[k % 4][:, :], ALU.add).then_inc(S("m_added"), 1)
            dve.wait_ge(S("m_added"), DT * (L + 1))

        def moe_act(act, step, L):
            act.wait_ge(S("m_shift"), 2 * L + 1)
            step(nc.scalar.activation(sh, sh, ACT.Exp))
            act.wait_ge(S("m_shift"), 2 * L + 2)
            nc.scalar.activation(e2, e2, ACT.Exp).then_inc(S("m_exp"), 1)
            for t in range(CH):
                act.wait_ge(S("m_tok_ready"), CH * L + t + 1)
                nc.scalar.activation(htok[:, t, T:2 * T], bank[2 * (t % 2) + 1][:, :], ACT.Copy).then_inc(S("m_tok1"), 1)
            act.wait_ge(S("m_plan"), 2 * L + 2)
            turns, before = item_turns(act, L)
            base = 2 * before
            with act.Fori(0, turns) as i:
                for u in range(2):
                    n = 2 * i + (base + u)
                    act.wait_ge(S("m_xt_ready"), n + 1)
                    nc.scalar.activation(xgT[u][:, 4:8, :], chunks(bank[1][:, :]), ACT.Copy).then_inc(S("m_xt1"), 1)
                for u in range(2):
                    n = 2 * i + (base + u)
                    act.wait_ge(S("m_h"), n + 3)
                    nc.scalar.activation(hs[u], bank[2 + u][:, 0:FF], ACT.Silu).then_inc(S("m_silu"), 1)
                for u in range(2):
                    n = 2 * i + (base + u)
                    act.wait_ge(S("m_y_ready"), n + 3)
                    act.wait_ge(S(f"m_y_sent{u}"), (i + before + 1) * 16)
                    nc.scalar.activation(ysb[u][:, 1, :], bank[7][:, :], ACT.Copy).then_inc(S("m_y1"), 1)
                    act.wait_ge(S("m_y0"), n + 1)
                    act.wait_ge(S("m_y1"), n + 1)
                    dst = rows_d[bass.ds(i * (2 * P) + u * P, P), :]
                    act.dma_start(dst, ysb[u].rearrange("p a n -> p (a n)")).then_inc(S(f"m_y_sent{u}"), 16)
            for u in range(2):
                act.wait_ge(S(f"m_y_sent{u}"), (turns + before + 1) * 16)
            act.sem_inc(S("m_rows_sent"), 1)

        def moe_pe(pe, L):
            wge = par[:, PC["wge"] + 160 * L:PC["wge"] + 160 * L + 160].rearrange("p (k n) -> p k n", k=DT)
            for t in range(CH):
                for k in range(DT):
                    mm = nc.tensor.matmul(bank[4][:, 20 * t:20 * t + 20], chunks(hT[:, k, :])[:, t, :], wge[:, k, :],
                                          start=(k == 0), stop=(k == DT - 1))
            mm.then_inc(S("m_logits"), 1)
            for t in range(CH):
                if t >= 2:
                    pe.wait_ge(S("m_tok0"), CH * L + t - 1)
                    pe.wait_ge(S("m_tok1"), CH * L + t - 1)
                for k in range(DT):
                    mm = nc.tensor.transpose(bank[2 * (t % 2) + k // 4][:, (k % 4) * P:(k % 4) * P + P], chunks(hT[:, k, :])[:, t, :],
                                             ident)
                mm.then_inc(S("m_tok_ready"), 1)
                if t == 1:
                    pe.wait_ge(S("m_sel"), L + 1)
                    sl = sel.rearrange("p t e -> p (t e)")
                    nc.tensor.matmul(bank[5][:, 0:64], strict, sl, start=True, stop=False)
                    nc.tensor.matmul(bank[5][:, 0:64], ones, pre.rearrange("p t e -> p (t e)"), start=False, stop=True)
                    nc.tensor.matmul(bank[5][:, 64:80], ones, tot, start=True, stop=True).then_inc(S("m_ranks"), 1)
            pe.wait_ge(S("m_plan"), 2 * L + 2)
            turns, before = item_turns(pe, L)
            base = 2 * before
            pe.wait_ge(S("m_tok0"), CH * (L + 1))
            pe.wait_ge(S("m_tok1"), CH * (L + 1))
            with pe.Fori(0, turns) as i:
                for u in range(2):
                    n = 2 * i + (base + u)
                    pe.wait_ge(S(f"m_x{u}"), (i + before + 1) * 16)
                    if u == 1:
                        pe.wait_ge(S("m_xt0"), n)
                        pe.wait_ge(S("m_xt1"), n)
                    for k in range(DT):
                        mm = nc.tensor.transpose(bank[k // 4][:, (k % 4) * P:(k % 4) * P + P], xg[u][:, k * P:k * P + P], ident)
                    mm.then_inc(S("m_xt_ready"), 1)
                for u in range(2):
                    n = 2 * i + (base + u)
                    pe.wait_ge(S("m_xt0"), n + 1)
                    pe.wait_ge(S("m_xt1"), n + 1)
                    pe.wait_ge(S(f"m_w13_{u}"), (i + before + 1) * 16)
                    for k in range(DT):
                        mm = nc.tensor.matmul(bank[2 + u][:, :], xgT[u][:, k, :], w13[u][:, k, :], start=(k == 0), stop=(k == DT - 1))
                    mm.then_inc(S("m_h"), 1)
                for u in range(2):
                    n = 2 * i + (base + u)
                    pe.wait_ge(S("m_hid"), n + 1)
                    for a in range(2):
                        mm = nc.tensor.transpose(bank[4 + u][:, a * P:a * P + P], hid[u][:, a * P:a * P + P], ident)
                    mm.then_inc(S("m_ht_ready"), 1)
                for u in range(2):
                    n = 2 * i + (base + u)
                    pe.wait_ge(S("m_ht"), n + 1)
                    pe.wait_ge(S(f"m_w2_{u}"), (i + before + 1) * 16)
                    if u == 1:
                        pe.wait_ge(S("m_y0"), n)
                        pe.wait_ge(S("m_y1"), n)
                    for half in range(2):
                        for a in range(2):
                            mm = nc.tensor.matmul(bank[6 + half][:, :], hidT[u][:, a, :], w2e[u][:, a, half * T:half * T + T],
                                                  start=(a == 0), stop=(a == 1))
                    mm.then_inc(S("m_y_ready"), 1)
                pe.wait_ge(S("m_y0"), 2 * i + (base + 2))
                pe.wait_ge(S("m_y1"), 2 * i + (base + 2))
            pe.sem_inc(S("m_items_done"), 1)
            for k in range(DT):
                if k >= 4:
                    pe.wait_ge(S("m_added"), DT * L + k - 3)
                for t in range(CH):
                    if k == 0:
                        pe.wait_ge(S("m_mix"), CH * L + t + 1)
                    mm = nc.tensor.transpose(bank[k % 4][:, t * P:t * P + P], y1[:, t, k * P:k * P + P], ident)
                mm.then_inc(S("m_back"), 1)

        def moe_pool(pool, L):
            pool.wait_ge(S("m_plan"), 2 * L + 1)
            if L == 0:
                pool.wait_ge(S("rows_zeroed"), 16 * ITEMS)
            for t in range(CH):
                pool.wait_ge(S("m_tok0"), CH * L + t + 1)
                pool.wait_ge(S("m_tok1"), CH * L + t + 1)
                for j in range(2):
                    pool.indirect_dma_start(rows_d[:, :], bass.IndirectOffsetOnAxis(ap=rows_i[:, 4 * j + t:4 * j + t + 1], axis=0),
                                            htok[:, t, :], None).then_inc(S("m_spread"), 16)
            pool.wait_ge(S("m_rows_sent"), L + 1)
            for t in range(CH):
                for j, y in enumerate((y1, y2)):
                    pool.indirect_dma_start(y[:, t, :], None, rows_d[:, :],
                                            bass.IndirectOffsetOnAxis(ap=rows_i[:, 4 * j + t:4 * j + t + 1], axis=0)).then_inc(
                        S("m_got"), 16)
            pool.wait_ge(S("m_got"), 128 * (L + 1))

        def moe_sync(sp, L):
            sp.wait_ge(S("m_plan"), 2 * L + 2)
            sp.wait_ge(S("m_spread"), 16 * 8 * (L + 1))
            turns, before = item_turns(sp, L)
            base = 2 * before
            with sp.Fori(0, turns) as i:
                for u in range(2):
                    n = 2 * i + (base + u)
                    e = sp.value_load(emap_i[0:1, bass.ds(2 * i + u, 1)], min_val=0, max_val=NE - 1)
                    sp.wait_ge(S("m_h"), n + 1)
                    sp.dma_start(xg[u], rows_d[bass.ds(i * (2 * P) + u * P, P), :]).then_inc(S(f"m_x{u}"), 16)
                    sp.dma_start(ring[:, 3 * u:3 * u + 2, :].rearrange("p a n -> p (a n)"),
                                 moe13[bass.ds(e * P + L * NE * P, P), :]).then_inc(S(f"m_w13_{u}"), 16)
                    sp.wait_ge(S("m_y_ready"), n + 1)
                    sp.dma_start(ring[:, 3 * u + 2, :], moe2[bass.ds(e * P + L * NE * P, P), :]).then_inc(S(f"m_w2_{u}"), 16)
            sp.wait_ge(S("m_items_done"), L + 1)

        first_xa = [B_XA0, B_XA1]

        @block.sync
        def _(sp):
            sp.dma_start(con[:, :], con_d).then_inc(S("inputs_in"), 16)
            sp.dma_start(xT[:, :, :], x_d.rearrange("(k p) t -> p k t", p=P)).then_inc(S("inputs_in"), 16)
            sp.dma_start(par[:, :], par_d).then_inc(S("inputs_in"), 16)

            def load(i, b):
                if not (isinstance(i, int) and b < RING):
                    sp.wait_ge(S("tile_ready1"), b + RING * i - RING + 1)
                src = wst[bass.ds((b + RING * i) * P, P), :] if not isinstance(i, int) else wst[(b + RING * i) * P:(b + RING * i + 1) * P, :]
                sp.dma_start(ring[:, b % RING, :], src).then_inc(S(f"weights{b % RING}"), 16)

            for b in range(RING):
                load(0, b)
            def load_mem(done, n):
                sp.wait_ge(S(done), n)
                sp.dma_start(memn[:, :, 0:M], mem_d.rearrange("(k p) t -> p k t", p=P)).then_inc(S("mem_in"), 16)

            each_block(sp, RING, B_XA0 - RING, load)
            load_mem("b_done", BT)
            each_block(sp, B_XA0, B_CIN - B_XA0, load)
            moe_sync(sp, 0)
            each_block(sp, B_CIN, B_XA1 - B_CIN, load)
            load_mem("c_done", CHEADS)
            each_block(sp, B_XA1, NBLK - B_XA1, load)
            moe_sync(sp, 1)
            for t in range(DT):
                sp.wait_ge(S("norm_done"), DT * 8 + t + 1)
                sp.dma_start(out_d[t * P:t * P + P, :], hT[:, t, :]).then_inc(S("out_sent"), 16)
            sp.wait_ge(S("out_sent"), 16 * DT)

        @block.scalar
        def _(act):
            step = Line(act, "act_order")
            act.sem_inc(S("m_y_sent0"), 16)
            act.sem_inc(S("m_y_sent1"), 16)
            act.wait_ge(S("inputs_in"), 48)
            norm_act(act, step, 0, xT, T)
            drain_copies("act", act, B_IN, N_A, 0, proj, 0, T)
            mixer0_act(act, step)
            for L in range(2):
                if L == 1:
                    act.wait_ge(S("m_added"), DT)
                    norm_act(act, step, 4, xT, T)
                    drain_copies("act", act, B_CIN, 16, 0, proj, 0, T)
                    hgrn_act(act, step)
                act.wait_ge(S("b_done") if L == 0 else S("c_done"), BT if L == 0 else CHEADS)
                act.wait_ge(S("mem_in"), 16 * (L + 1))
                norm_act(act, step, 4 * L + 1, memn, M)
                fx = first_xa[L]
                drain_copies("act", act, fx, 4, 0, proj, 0, M)
                drain_copies("act", act, fx + 4, 4, 0, proj, 8, 256)
                norm_act(act, step, 4 * L + 2, xT, T)
                drain_copies("act", act, fx + 8, 4, 0, proj, 16, T)
                act.wait_ge(S("tile_free1"), 2 + fx + 12)
                xattn_act(act, step, L)
                act.wait_ge(S("tile_free0"), 2 + fx + 16)
                act.wait_ge(S("tile_free1"), 2 + fx + 16)
                norm_act(act, step, 4 * L + 3, xT, T)
                moe_act(act, step, L)
            act.wait_ge(S("m_added"), 2 * DT)
            norm_act(act, step, 8, xT, T)

        @block.tensor
        def _(pe):
            pe.sem_inc(S("m_h"), 2)
            pe.sem_inc(S("m_y_ready"), 2)
            pe.wait_ge(S("inputs_in"), 48)
            norm_pe(pe, 0, T)
            pe.wait_ge(S("norm_done"), DT)
            project_pe(pe, B_IN, N_A, hT, T)
            mixer0_pe(pe)
            for L in range(2):
                if L == 1:
                    norm_pe(pe, 4, T)
                    pe.wait_ge(S("norm_done"), DT * 5)
                    project_pe(pe, B_CIN, 16, hT, T)
                    pe.wait_ge(S("tile_free0"), 2 + B_COUT)
                    pe.wait_ge(S("tile_free1"), 2 + B_COUT)
                    hgrn_pe(pe)
                    pe.wait_ge(S("c_done"), CHEADS)
                project_pe(pe, B_AOUT if L == 0 else B_COUT, 4, hT, T)
                norm_pe(pe, 4 * L + 1, M)
                pe.wait_ge(S("norm_done"), DT * (4 * L + 2))
                fx = first_xa[L]
                project_pe(pe, fx, 4, memn, M)
                project_pe(pe, fx + 4, 4, memn, M, tokens_out=True)
                norm_pe(pe, 4 * L + 2, T)
                pe.wait_ge(S("norm_done"), DT * (4 * L + 3))
                project_pe(pe, fx + 8, 4, hT, T)
                xattn_pe(pe, L)
                project_pe(pe, fx + 12, 4, hT, T)
                norm_pe(pe, 4 * L + 3, T)
                pe.wait_ge(S("norm_done"), DT * (4 * L + 4))
                moe_pe(pe, L)
            norm_pe(pe, 8, T)

        @block.vector
        def _(dve):
            step = Line(dve, "dve_order")
            dve.sem_inc(S("tile_free0"), 2)
            dve.sem_inc(S("tile_free1"), 2)
            dve.wait_ge(S("inputs_in"), 48)
            norm_dve(dve, 0, xT, hT, T, gains("mix", 0))
            drain_copies("dve", dve, B_IN, N_A, 1, proj, 0, T)
            mixer0_dve(dve, step)
            for L in range(2):
                if L == 1:
                    norm_dve(dve, 4, xT, hT, T, gains("mix", 1))
                    drain_copies("dve", dve, B_CIN, 16, 1, proj, 0, T)
                    hgrn_dve(dve, step)
                drain_residual(dve, B_AOUT if L == 0 else B_COUT)
                norm_dve(dve, 4 * L + 1, memn, memn, M, gains("mem", L))
                fx = first_xa[L]
                drain_copies("dve", dve, fx, 4, 1, proj, 0, M)
                drain_copies("dve", dve, fx + 4, 4, 1, proj, 8, 256)
                norm_dve(dve, 4 * L + 2, xT, hT, T, gains("xat", L))
                drain_copies("dve", dve, fx + 8, 4, 1, proj, 16, T)
                xattn_dve(dve, step, L)
                drain_residual(dve, fx + 12)
                norm_dve(dve, 4 * L + 3, xT, hT, T, gains("ffn", L))
                moe_dve(dve, step, L)
            norm_dve(dve, 8, xT, hT, T, gains("fin"))

        @block.gpsimd
        def _(pool):
            zero = work[:, 12:14, :].rearrange("p a n -> p (a n)")
            nc.gpsimd.memset(zero, 0.0).then_inc(S("zero_set"), 1)
            pool.wait_ge(S("zero_set"), 1)
            for i in range(ITEMS):
                pool.dma_start(rows_d[i * P:i * P + P, :], zero).then_inc(S("rows_zeroed"), 16)
            pool.wait_ge(S("inputs_in"), 48)
            for r in range(2):
                inv_pool(pool, r, a_bufs(r))
            for q in range(BT):
                inv_pool(pool, 2 + q, b_inv(q))
            moe_pool(pool, 0)
            hgrn_pool(pool)
            moe_pool(pool, 1)


def constants():
    c = np.zeros((P, NCONST), np.float32)
    i = np.arange(P)
    c[:, C_ID:C_ID + P] = np.eye(P)
    c[:, C_ONE:C_ONE + P] = 1
    c[:, C_BLK:C_BLK + P] = i[:, None] // 64 == i[None, :] // 64
    c[:, C_INC:C_INC + P] = i[:, None] <= i[None, :]
    c[:, C_STR:C_STR + P] = i[:, None] < i[None, :]
    for n, s in enumerate(LEVELS):
        same = i[:, None] // (2 * s) == i[None, :] // (2 * s)
        c[:, C_LVL + n * P:C_LVL + n * P + P] = same & (i[:, None] // s % 2 == 0) & (i[None, :] // s % 2 == 1)
    c[:, C_RST:C_RST + T] = np.arange(T) % P != 0
    for h in range(8):
        c[h, C_SEL + h * P:C_SEL + h * P + P] = 1
    c[:, C_IOTA:C_IOTA + ITEMS] = np.arange(ITEMS)
    c[:, C_WTS:C_WTS + 4] = [4, 3, 2, 1]
    c[:, C_EPS] = 1e-6
    c[:, C_EPS + 1] = 64e-5
    return c


def columns(v):
    v = np.asarray(v).reshape(-1, P)
    return v.T


def blocks(w):
    k, n = w.shape
    return np.asarray(w).reshape(DT, P, n // 256, 256).transpose(2, 1, 0, 3).reshape(n // 256, P, BLK)


def pack(i):
    f = {k: np.asarray(v) for k, v in i.items()}
    par = np.zeros((P, NPAR), np.float32)

    def put(name, a):
        par[:a.shape[0], PC[name]:PC[name] + a.shape[1]] = a

    for n, k in (("mix", "norm_mix"), ("xat", "norm_xattn"), ("mem", "norm_mem"), ("ffn", "norm_ffn"), ("fin", "norm_final"),
                 ("mu", "ab_shift_mu"), ("w0", "ab_w0"), ("a0", "ab_a0"), ("kk", "ab_k_k"), ("ka", "ab_k_a"), ("rk", "ab_r_k"),
                 ("lnw", "ab_ln_w"), ("lnb", "ab_ln_b"), ("lb", "c_lb_param"), ("onA", "ab_onorm"), ("onC", "c_onorm")):
        put(n, columns(f[k]))
    put("conv", f["ab_conv"][0].reshape(4, 12, P).transpose(2, 1, 0).reshape(P, 48))
    put("alog", f["ab_a_log"].reshape(4, 1))
    put("dt", f["ab_dt_bias"].reshape(4, 1))
    put("w2a2", np.concatenate([f["ab_w2"][0], f["ab_a2"][0]], axis=0))
    put("g2", f["ab_g2"][0])
    w_in = f["ab_w_in"][0]
    put("wdb", w_in[:, 2048:2056].reshape(DT, P, 8).transpose(1, 0, 2).reshape(P, 64))
    for L in range(2):
        wge = np.concatenate([f["moe_w_group"][L], f["moe_w_expert"][L]], axis=1)
        par[:, PC["wge"] + 160 * L:PC["wge"] + 160 * L + 160] = wge.reshape(DT, P, 20).transpose(1, 0, 2).reshape(P, 160)
        par[:, PC["bge"] + 20 * L:PC["bge"] + 20 * L + 20] = np.concatenate([f["moe_b_group"][L], f["moe_b_expert"][L]])
    wst = [blocks(w_in[:, :2048]), blocks(w_in[:, 2056:]), blocks(f["ab_w_out"][0])]
    for L in range(2):
        if L:
            wst += [blocks(f["c_w_in"][0]), blocks(f["c_w_out"][0])]
        wst += [blocks(f["xa_wkv"][L]), blocks(f["xa_wq"][L]), blocks(f["xa_wo"][L])]
    wst = np.concatenate(wst).reshape(NBLK * P, BLK)
    w13 = np.stack([f["moe_w1"], f["moe_w3"]], axis=3)
    w13 = w13.reshape(2, NE, DT, P, 2 * FF).transpose(0, 1, 3, 2, 4).reshape(2 * NE * P, 2 * BLK)
    w2 = f["moe_w2"].reshape(2, NE, 2, P, D).transpose(0, 1, 3, 2, 4).reshape(2 * NE * P, BLK)
    c = np.ascontiguousarray
    return {"wst": c(wst), "moe13": c(w13), "moe2": c(w2), "par": par, "con": constants(), "x": c(f["x"][0].T),
            "mem": c(f["mem"][0].T)}


def program(nc, arrays):
    ins = {n: nc.dram_tensor(f"in_{n}", a.shape, F32, kind="ExternalInput").ap() for n, a in arrays.items()}
    out = nc.dram_tensor("out_x", (D, T), F32, kind="ExternalOutput").ap()
    rows = nc.dram_tensor("sorted_rows", (ITEMS * P, D), F32, kind="Internal").ap()
    build(nc, ins["wst"], ins["moe13"], ins["moe2"], ins["par"], ins["con"], ins["x"], ins["mem"], out, rows)


def kernel(**inputs):
    import concourse.bacc as bacc
    from concourse.bass_utils import run_bass_kernel_spmd

    arrays = pack(inputs)
    nc = bacc.Bacc("TRN2", target_bir_lowering=False, num_devices=1)
    program(nc, arrays)
    r = run_bass_kernel_spmd(nc, [{f"in_{n}": a for n, a in arrays.items()}], core_ids=[0])
    return np.ascontiguousarray(r.results[0]["out_x"].T)[None]
```

```python
from contextlib import ExitStack

import numpy as np
import concourse.bass as bass
from concourse import mybir

F32 = mybir.dt.float32
F32R = mybir.dt.float32r
I32 = mybir.dt.int32
ALU = mybir.AluOpType
ACT = mybir.ActivationFunctionType
AX = mybir.AxisListType

P = 128
D = 1024
T = 512
M = 256
DT = D // P
CH = T // P
AH = 4
BT = 4
CHEADS = 8
XH = 4
NE, NG, EG = 16, 4, 4
FF = 256
ITEMS = 24
BLK = 2048
RING = 2
LEVELS = [1, 2, 4, 8, 16, 32, 64]

C_ID, C_ONE, C_BLK, C_INC, C_STR = 0, P, 2 * P, 3 * P, 4 * P
C_LVL = 5 * P
C_RST = C_LVL + 7 * P
C_SEL = C_RST + T
C_IOTA = C_SEL + 8 * P
C_WTS = C_IOTA + ITEMS
C_EPS = C_WTS + 4
NCONST = C_EPS + 4

_names = [("mix", 16), ("xat", 16), ("mem", 16), ("ffn", 16), ("fin", 8), ("conv", 48), ("alog", 1),
          ("dt", 1), ("onA", 1), ("onC", 1), ("mu", 14), ("w0", 4), ("a0", 4), ("kk", 4), ("ka", 4),
          ("rk", 4), ("lnw", 4), ("lnb", 4), ("lb", 16), ("w2a2", 512), ("g2", 512), ("wge", 320),
          ("wdb", 64), ("bge", 40)]
PC, NPAR = {}, 0
for _n, _w in _names:
    PC[_n] = NPAR
    NPAR += _w

B_IN, B_AOUT, B_XA0, B_CIN = 0, 15, 19, 35
B_COUT, B_XA1 = 51, 55
NBLK = 71
SPLIT = [(B_IN, 15), (B_XA0 + 8, 8), (B_CIN, 16), (B_XA1 + 8, 8)]
BEFORE = {b: sum(n for f, n in SPLIT if f < first) + b - first for first, count in SPLIT for b in range(first, first + count)}


def build(nc, wst, moe13, moe2, par_d, con_d, x_d, mem_d, out_d, rows_d):
    ctx = ExitStack()
    with ctx:
        def sb(name, shape, dt=F32):
            return ctx.enter_context(nc.sbuf_tensor(name, shape, dt))

        sems = {}

        def S(name):
            if name not in sems:
                sems[name] = ctx.enter_context(nc.semaphore(name))
            return sems[name]

        def placed(name, shape, dt=F32):
            at = nc.sbuf_base
            return sb(name, shape, dt), at

        def over(name, shape, at):
            return nc.alloc_sbuf_tensor_at(name, shape, F32R, offset=at)

        xT = sb("xT", [P, DT, T])
        hT, at_h = placed("hT", [P, DT, T])
        gates, at_gates = placed("gates", [P, BT, T])
        proj = sb("proj", [P, 32, T])
        ring, at_ring = placed("ring", [P, 6, BLK])
        work, at_work = placed("work", [P, 14, T])
        ryz = sb("ryz", [P, 4, P])
        con = sb("con", [P, NCONST])
        par = sb("par", [P, NPAR])
        small = sb("small", [P, 1024])
        smalli = sb("smalli", [P, 64], I32)
        bank = [ctx.enter_context(nc.psum_tensor(f"bank{i}", [P, T], F32)) for i in range(8)]
        w_hi = [over(f"w_hi{i}", [P, BLK], at_ring + 4 * BLK * (RING + i)) for i in range(2)]
        w_lo = [over("w_lo0", [P, BLK], at_work + 4 * T * 10), over("w_lo1", [P, BLK], at_gates)]
        x_hi = over("x_hi", [P, DT, T], at_ring + 4 * BLK * (RING + 2))
        x_lo = over("x_lo", [P, DT, T], at_h)
        extra = ring[:, RING:6, :].rearrange("p a (b n) -> p (a b) n", n=T)

        ident = con[:, C_ID:C_ID + P]
        ones = con[:, C_ONE:C_ONE + P]
        bones = con[:, C_BLK:C_BLK + P]
        incl = con[:, C_INC:C_INC + P]
        strict = con[:, C_STR:C_STR + P]
        lvl = [con[:, C_LVL + P * i:C_LVL + P * (i + 1)] for i in range(7)]
        reset = con[:, C_RST:C_RST + T]
        sel8 = [con[0:8, C_SEL + P * i:C_SEL + P * (i + 1)] for i in range(8)]
        eps6 = con[:, C_EPS:C_EPS + 1]
        epsg = con[:, C_EPS + 1:C_EPS + 2]

        def pc(name, i=0, rows=P):
            return par[0:rows, PC[name] + i:PC[name] + i + 1]

        def chunks(ap):
            return ap.rearrange("p (c n) -> p c n", n=P)

        def over4(ap):
            return ap.unsqueeze(1).broadcast_to([P, CH, P])

        block = ctx.enter_context(nc.Block())

        class Line:

            def __init__(self, eng, name):
                self.eng, self.sem, self.n = eng, S(name), 0

            def __call__(self, ins):
                self.n += 1
                ins.then_inc(self.sem, 1)
                self.eng.wait_ge(self.sem, self.n)

        NORMS = {"mix0": 0, "mem0": 1, "xat0": 2, "ffn0": 3, "mix1": 4, "mem1": 5, "xat1": 6, "ffn1": 7, "fin": 8}

        def sq_of(n):
            return work[:, 0:8, 0:n]

        def norm_act(act, step, k, src, n, ready=None):
            square_act(act, k, src, n, ready)
            rstd_act(act, step, k, n)

        def square_act(act, k, src, n, ready=None):
            if k > 0:
                act.wait_ge(S("norm_summed"), k)
            for t in range(DT):
                if ready:
                    ready(t)
                nc.scalar.activation(work[:, t, 0:n], src[:, t, 0:n], ACT.Square).then_inc(S("norm_squared"), 1)

        def rstd_act(act, step, k, n):
            act.wait_ge(S("norm_summed"), k + 1)
            if k == 0:
                act.wait_ge(S("con_in"), 16)
                act.wait_ge(S("par_in"), 16)
            step(nc.scalar.activation(work[:, 8, 0:n], bank[7][:, 0:n], ACT.Ln, bias=eps6, scale=1.0 / D))
            nc.scalar.activation(work[:, 9, 0:n], work[:, 8, 0:n], ACT.Exp, scale=-0.5).then_inc(S("norm_rstd"), 1)

        def norm_pe(pe, k, n, tiles=range(DT)):
            for t in tiles:
                pe.wait_ge(S("norm_squared"), DT * k + t + 1)
                mm = nc.tensor.matmul(bank[7][:, 0:n], ones, work[:, t, 0:n], start=(t == 0), stop=(t == DT - 1))
            if t == DT - 1:
                mm.then_inc(S("norm_summed"), 1)

        def norm_dve(dve, k, src, dst, n, gain):
            dve.wait_ge(S("norm_rstd"), k + 1)
            for t in range(DT):
                nc.vector.scalar_tensor_tensor(
                    out=dst[:, t, 0:n], in0=src[:, t, 0:n], scalar=gain[:, t:t + 1], in1=work[:, 9, 0:n],
                    op0=ALU.mult, op1=ALU.mult).then_inc(S("norm_done"), 1)
            dve.wait_ge(S("norm_done"), DT * (k + 1))

        def gains(name, layer=0):
            return par[:, PC[name] + DT * layer:PC[name] + DT * layer + DT]

        def each_block(eng, first, count, body):
            turns = count // RING
            if turns > 1:
                with eng.Fori(0, turns) as i:
                    for s in range(RING):
                        body(i, first + s)
            else:
                turns = 0
            for b in range(first + turns * RING, first + count):
                body(0, b)

        def project_pe(pe, first, count, src, n, tokens_out=False):
            def body(i, b):
                w = ring[:, b % RING, :].rearrange("p (k n) -> p k n", k=DT)
                pe.wait_ge(S(f"weights{b % RING}"), (b // RING + 1 + i) * 16)
                for h in range(2):
                    bk = bank[(2 * b + h) % 4]
                    pe.wait_ge(S(f"tile_free{h}"), b + RING * i + 1)
                    for k in range(DT):
                        if tokens_out:
                            mm = nc.tensor.matmul(bk[:, 0:256], src[:, k, h * P:h * P + P], w[:, k, :],
                                                  start=(k == 0), stop=(k == DT - 1))
                        else:
                            mm = nc.tensor.matmul(bk[:, 0:n], w[:, k, h * P:h * P + P], src[:, k, 0:n],
                                                  start=(k == 0), stop=(k == DT - 1))
                    mm.then_inc(S(f"tile_ready{h}"), 1)
            each_block(pe, first, count, body)

        def split_weights_dve(dve, first, low=True):
            high_part(dve, 0, first)
            if low:
                s = first % RING
                dve.wait_ge(S("w_high"), BEFORE[first] + 1)
                nc.vector.tensor_tensor(w_lo[s][:, :], ring[:, s, :], w_hi[s][:, :], ALU.subtract).then_inc(S("w_split"), 1)
                dve.wait_ge(S("w_split"), BEFORE[first] + 1)
            high_part(dve, 0, first + 1)

        def high_part(dve, i, b):
            dve.wait_ge(S(f"weights{b % RING}"), (b // RING + 1 + i) * 16)
            nc.vector.tensor_copy(w_hi[b % RING][:, :], ring[:, b % RING, :]).then_inc(S("w_high"), 1)

        def split_weights_pool(pool, first, count):
            def body(i, b):
                pool.wait_ge(S("w_high"), BEFORE[b] + RING * i + 1)
                nc.gpsimd.tensor_tensor(w_lo[b % RING][:, :], ring[:, b % RING, :], w_hi[b % RING][:, :],
                                        ALU.subtract).then_inc(S("w_split"), 1)
            each_block(pool, first, count, body)

        def split_stream_act(act, k, norm):
            for t in range(DT):
                act.wait_ge(S("norm_done"), DT * norm + t + 1)
                nc.scalar.activation(x_hi[:, t, :], hT[:, t, :], ACT.Copy).then_inc(S("x_high"), 1)

        def split_stream_pool(pool, k):
            for t in range(DT):
                pool.wait_ge(S("x_high"), DT * k + t + 1)
                if k == 0:
                    pool.wait_ge(S("a_db"), t + 1)
                nc.gpsimd.tensor_tensor(x_lo[:, t, :], hT[:, t, :], x_hi[:, t, :], ALU.subtract).then_inc(S("x_split"), 1)

        def project_split_pe(pe, first, count, k):
            def body(i, b):
                wh, wl = (a[b % RING][:, :].rearrange("p (k n) -> p k n", k=DT) for a in (w_hi, w_lo))
                pe.wait_ge(S("w_split"), BEFORE[b] + RING * i + 1)
                for h in range(2):
                    bk = bank[(2 * b + h) % 4]
                    pe.wait_ge(S(f"tile_free{h}"), b + RING * i + 1)
                    for t in range(DT):
                        if h == 0:
                            pe.wait_ge(S("x_split"), DT * k + t + 1)
                        sl = slice(h * P, h * P + P)
                        nc.tensor.matmul(bk[:, :], wh[:, t, sl], x_hi[:, t, :], start=(t == 0), stop=False)
                        nc.tensor.matmul(bk[:, :], wh[:, t, sl], x_lo[:, t, :], start=False, stop=False)
                        mm = nc.tensor.matmul(bk[:, :], wl[:, t, sl], x_hi[:, t, :], start=False, stop=(t == DT - 1))
                    mm.then_inc(S(f"tile_ready{h}"), 1)
            each_block(pe, first, count, body)

        def drain(eng, first, count, halves, write):
            last = max([f + n for f, n in SPLIT if f <= first < f + n] + [0])

            def body(i, b):
                for h in halves:
                    eng.wait_ge(S(f"tile_ready{h}"), b + RING * i + 1)
                    write(h, i, b, bank[(2 * b + h) % 4]).then_inc(S(f"tile_free{h}"), 1)

            def body_and_high(i, b):
                body(i, b)
                high_part(eng, i, b + 2)

            ahead = max(0, min(count, last - 2 - first)) if 1 in halves else 0
            if ahead:
                each_block(eng, first, ahead, body_and_high)
            each_block(eng, first + ahead, count - ahead, body)

        def tile_at(buf, base, i, b, h, first):
            n = base + 2 * (b - first) + h
            if isinstance(i, int):
                return buf[:, n + 2 * RING * i, :]
            return buf[:, bass.ds(i * (2 * RING) + n, 1), :].rearrange("p a n -> p (a n)")

        def drain_copies(act_or_dve, eng, first, count, half, buf, base, n):
            def write(h, i, b, bk):
                dst = tile_at(buf, base, i, b, h, first)[:, 0:n]
                if act_or_dve == "act":
                    return nc.scalar.activation(dst, bk[:, 0:n], ACT.Copy)
                return nc.vector.tensor_copy(dst, bk[:, 0:n])
            drain(eng, first, count, [half], write)

        def drain_residual(dve, first, count=4, at=0):
            def write(h, i, b, bk):
                dst = tile_at(xT, at, i, b, h, first)
                return nc.vector.tensor_tensor(dst, dst, bk[:, :], ALU.add)
            drain(dve, first, count, [0, 1], write)
            dve.wait_ge(S("tile_free1"), 2 + first + count)

        inv_rounds = {"n": 0}

        def inv_pe(pe, r, bufs, between=None):
            for li in range(7):
                for g, (MT, Tt, TT, X, Cm) in enumerate(bufs):
                    if li == 0:
                        pe.wait_ge(S(f"inv_tt{g}"), 7 * r + 1)
                        for c in range(CH):
                            mm = nc.tensor.transpose(bank[g][:, c * P:c * P + P], chunks(TT)[:, c, :], ident)
                        mm.then_inc(S(f"inv_t_ready{g}"), 1)
                        continue
                    pe.wait_ge(S(f"inv_c{g}"), 7 * r + li + 1)
                    pe.wait_ge(S(f"inv_t{g}"), 6 * r + li)
                    for c in range(CH):
                        mm = nc.tensor.matmul(bank[g][:, c * P:c * P + P], chunks(Cm)[:, c, :], chunks(Tt)[:, c, :],
                                              start=True, stop=True)
                    mm.then_inc(S(f"inv_x_ready{g}"), 1)
                if between and li:
                    between(2 * li - 2)
                for g, (MT, Tt, TT, X, Cm) in enumerate(bufs):
                    if li == 0:
                        continue
                    pe.wait_ge(S(f"inv_x{g}"), 6 * r + li)
                    pe.wait_ge(S(f"inv_tt{g}"), 7 * r + li)
                    if li < 6:
                        for c in range(CH):
                            mm = nc.tensor.matmul(bank[2 + g][:, c * P:c * P + P], chunks(TT)[:, c, :], chunks(X)[:, c, :],
                                                  start=True, stop=True)
                    for c in range(CH):
                        mm = nc.tensor.matmul(bank[4 + g][:, c * P:c * P + P], chunks(X)[:, c, :], chunks(TT)[:, c, :],
                                              start=True, stop=True)
                    mm.then_inc(S(f"inv_tct_ready{g}"), 1)
                if between and li:
                    between(2 * li - 1)

        def inv_act(act, r, bufs, between=None):
            for li in range(1, 7):
                for g, (MT, Tt, TT, X, Cm) in enumerate(bufs):
                    act.wait_ge(S(f"inv_x_ready{g}"), 6 * r + li)
                    nc.scalar.activation(X, bank[g][:, :], ACT.Copy).then_inc(S(f"inv_x{g}"), 1)
                if between:
                    between(2 * li - 2)
                    between(2 * li - 1)

        def inv_pool(pool, r, bufs):
            for li in range(7):
                for g, (MT, Tt, TT, X, Cm) in enumerate(bufs):
                    pool.wait_ge(S(f"inv_mt{g}"), r + 1)
                    if li == 1:
                        pool.wait_ge(S(f"inv_tt{g}"), 7 * r + 1)
                    if li > 1:
                        pool.wait_ge(S(f"inv_x_ready{g}"), 6 * r + li - 1)
                    nc.gpsimd.tensor_tensor(chunks(Cm), chunks(MT), over4(lvl[li]), ALU.mult).then_inc(S(f"inv_c{g}"), 1)

        def inv_dve(dve, r, bufs, between=None):
            for g, (MT, Tt, TT, X, Cm) in enumerate(bufs):
                dve.wait_ge(S(f"inv_c{g}"), 7 * r + 1)
                nc.vector.tensor_tensor(chunks(TT), over4(ident), chunks(Cm), ALU.subtract).then_inc(S(f"inv_tt{g}"), 1)
            for g, (MT, Tt, TT, X, Cm) in enumerate(bufs):
                dve.wait_ge(S(f"inv_t_ready{g}"), r + 1)
                nc.vector.tensor_copy(Tt, bank[g][:, :]).then_inc(S(f"inv_t{g}"), 1)
            for li in range(1, 7):
                if between:
                    between(2 * li - 2)
                for g, (MT, Tt, TT, X, Cm) in enumerate(bufs):
                    dve.wait_ge(S(f"inv_tct_ready{g}"), 6 * r + li)
                    if li < 6:
                        dve.wait_ge(S(f"inv_t{g}"), 6 * r + li)
                        nc.vector.tensor_tensor(Tt, Tt, bank[2 + g][:, :], ALU.subtract).then_inc(S(f"inv_t{g}"), 1)
                    dve.wait_ge(S(f"inv_tt{g}"), 7 * r + li)
                    nc.vector.tensor_tensor(TT, TT, bank[4 + g][:, :], ALU.subtract).then_inc(S(f"inv_tt{g}"), 1)
                if between:
                    between(2 * li - 1)
            for g in range(2):
                dve.wait_ge(S(f"inv_tt{g}"), 7 * r + 7)

        W = [work[:, i, :] for i in range(14)]
        X = [extra[:, i, :] for i in range(16)]
        beta8, g8 = proj[0:8, 30, :], proj[0:8, 31, :]
        z8, l8, t8 = W[5][0:8, :], W[8][0:8, :], ryz[:, :, :].rearrange("p a n -> p (a n)")[0:8, :]
        cols = small[:, 16:80].rearrange("p (a c h) -> p a c h", a=2, c=CH)
        glast = small[:, 80:96].rearrange("p (h c) -> p h c", h=AH)
        e_glast = small[:, 96:112].rearrange("p (h c) -> p h c", h=AH)
        e_rest = small[:, 112:128].rearrange("p (h c) -> p h c", h=AH)
        e_col = small[:, 128:144].rearrange("p (h c) -> p h c", h=AH)
        nbeta_e = small[:, 144:160].rearrange("p (h c) -> p h c", h=AH)
        a_neg = small[0:8, 0:1]
        PT = X[0:4]
        TTa = X[4:8]
        ktok = W[8:12]
        state = proj[:, 30, :]
        N_A, N_IN = 8, 15

        def a_bufs(r):
            return [(hT[:, 4 * g, :], hT[:, 4 * g + 1, :], TTa[2 * r + g], hT[:, 4 * g + 2, :], hT[:, 4 * g + 3, :])
                    for g in range(2)]

        def pair(i):
            return [j for j in (2 * i, 2 * i + 1) if 0 <= i < 4]

        def delta_prep_dve(dve, step):
            dve.wait_ge(S("tile_free0"), 2 + N_A)
            dve.wait_ge(S("tile_free1"), 2 + N_A)
            for i in range(N_IN - N_A):
                for j in (2 * i, 2 * i + 1):
                    if j >= 12:
                        continue
                    cv, p = W[j % 2], proj[:, j, :]
                    if j >= 2:
                        dve.wait_ge(S("a_silu"), j - 1)
                    step(nc.vector.tensor_scalar(cv, p, pc("conv", 4 * j + 3), None, ALU.mult))
                    for s in range(1, 4):
                        ins = nc.vector.scalar_tensor_tensor(out=cv[:, s:T], in0=p[:, 0:T - s], scalar=pc("conv", 4 * j + 3 - s),
                                                             in1=cv[:, s:T], op0=ALU.mult, op1=ALU.add)
                        if s < 3:
                            step(ins)
                    ins.then_inc(S("a_conv"), 1)
                for j in pair(i - 2):
                    p = proj[:, j, :]
                    dve.wait_ge(S("head_rstd"), j + 1)
                    nc.vector.scalar_tensor_tensor(out=p, in0=p, scalar=(P ** -0.5 if j < 4 else 1.0), in1=W[6 + j % 2],
                                                   op0=ALU.mult, op1=ALU.mult).then_inc(S("a_unit"), 1)
                if i == 1:
                    dve.wait_ge(S("a_softplus"), 1)
                    step(nc.vector.tensor_scalar(z8, z8, 0.0, None, ALU.max))
                    step(nc.vector.tensor_tensor(z8, z8, l8, ALU.add))
                    step(nc.vector.tensor_scalar(z8, z8, a_neg, -1.0, ALU.mult, ALU.mult))
                    nc.vector.tensor_tensor_scan(g8, reset[0:8, :], z8, 0.0, ALU.mult, ALU.add).then_inc(S("a_decay"), 1)
                drain_copies("dve", dve, N_A + i, 1, 1, proj, 2 * (N_A + i), T)
            dve.wait_ge(S("a_unit"), 8)
            dve.wait_ge(S("a_cols"), 1)
            step(nc.vector.tensor_copy(small[:, 16:80], bank[7][:, 0:64]))

        def delta_prep_act(act, step):
            act.wait_ge(S("tile_free0"), 2 + N_A)
            act.wait_ge(S("tile_free1"), 2 + N_A)
            act.wait_ge(S("a_db"), DT)
            step(nc.scalar.activation(beta8, bank[6][0:8, :], ACT.Sigmoid))
            step(nc.scalar.activation(z8, bank[6][0:8, :], ACT.Identity, bias=pc("dt", 0, 8)))
            step(nc.scalar.activation(t8, z8, ACT.Abs))
            step(nc.scalar.activation(t8, t8, ACT.Exp, scale=-1.0))
            step(nc.scalar.activation(l8, t8, ACT.Ln, bias=con[0:8, C_ONE:C_ONE + 1]))
            nc.scalar.activation(a_neg, pc("alog", 0, 8), ACT.Exp).then_inc(S("a_softplus"), 1)
            for i in range(N_IN - N_A):
                for j in (2 * i, 2 * i + 1):
                    if j < 12:
                        act.wait_ge(S("a_conv"), j + 1)
                        nc.scalar.activation(proj[:, j, :], W[j % 2], ACT.Silu).then_inc(S("a_silu"), 1)
                if i == 6:
                    for h in range(AH):
                        step(nc.scalar.activation(proj[:, 12 + h, :], proj[:, 12 + h, :], ACT.Silu))
                for j in pair(i - 1):
                    if j >= 2:
                        act.wait_ge(S("head_summed"), j - 1)
                    act.wait_ge(S("a_silu"), j + 1)
                    nc.scalar.activation(W[2 + j % 2], proj[:, j, :], ACT.Square).then_inc(S("head_squared"), 1)
                for j in pair(i - 2):
                    act.wait_ge(S("head_summed"), j + 1)
                    step(nc.scalar.activation(W[(4, 9)[j % 2]], bank[4 + j % 2][:, :], ACT.Ln, bias=eps6))
                for j in pair(i - 2):
                    if j >= 2:
                        act.wait_ge(S("a_unit"), j - 1)
                    nc.scalar.activation(W[6 + j % 2], W[(4, 9)[j % 2]], ACT.Exp, scale=-0.5).then_inc(S("head_rstd"), 1)
                    act.wait_ge(S("head_rstd"), j + 1)
                drain_copies("act", act, N_A + i, 1, 0, proj, 2 * (N_A + i), T)

        def rates_pe(pe):
            wdb = par[:, PC["wdb"]:PC["wdb"] + 64].rearrange("p (k n) -> p k n", k=DT)
            for k in range(DT):
                pe.wait_ge(S("norm_done"), k + 1)
                nc.tensor.matmul(bank[6][0:8, :], wdb[:, k, :], hT[:, k, :], start=(k == 0), stop=(k == DT - 1)).then_inc(
                    S("a_db"), 1)

        def delta_prep_pe(pe):
            for i in range(N_IN - N_A):
                project_split_pe(pe, N_A + i, 1, 0)
                for j in pair(i - 1):
                    pe.wait_ge(S("head_squared"), j + 1)
                    if j >= 2:
                        pe.wait_ge(S("head_rstd"), j - 1)
                    nc.tensor.matmul(bank[4 + j % 2][:, :], ones, W[2 + j % 2], start=True, stop=True).then_inc(S("head_summed"), 1)
                if i == 4:
                    pe.wait_ge(S("a_decay"), 1)
                    for a, rows in enumerate((g8, beta8)):
                        for c in range(CH):
                            o = a * 32 + c * 8
                            mm = nc.tensor.transpose(bank[7][:, o:o + 8], rows[:, c * P:c * P + P], ident[0:8, 0:8])
                    mm.then_inc(S("a_cols"), 1)
            pe.wait_ge(S("a_unit"), 8)
            pe.wait_ge(S("head_rstd"), 8)

        def delta_round_dve(dve, step, r, between):
            for g in range(2):
                h = 2 * r + g
                dve.wait_ge(S("a_bcast"), h + 1)
                for c in range(CH):
                    nc.vector.tensor_scalar(chunks(W[g])[:, c, :], chunks(bank[4 + g][:, :])[:, c, :], cols[:, 0, c, h:h + 1],
                                            0.0, ALU.subtract, ALU.min).then_inc(S("a_diff"), 1)
                step(nc.vector.tensor_copy(glast[:, h, :], bank[4 + g][:, P - 1:T:P]))
                nc.vector.tensor_tensor(e_rest[:, h, :], glast[:, h, :], cols[:, 0, :, h], ALU.subtract).then_inc(S("a_diff"), 1)
                nc.vector.tensor_tensor(W[2 + g], proj[:, 4 + h, :], bank[6 + g][:, :], ALU.mult).then_inc(S("a_diff"), 1)
            for g in range(2):
                h = 2 * r + g
                dve.wait_ge(S("a_exps"), h + 1)
                step(nc.vector.tensor_tensor(chunks(W[6 + g]), chunks(W[g]), over4(incl), ALU.mult))
                dve.wait_ge(S("a_scores"), h + 1)
                nc.vector.tensor_tensor(a_bufs(r)[g][0], bank[g][:, :], W[g], ALU.mult).then_inc(S(f"inv_mt{g}"), 1)
                step(nc.vector.tensor_tensor(PT[h], bank[2 + g][:, :], W[6 + g], ALU.mult))
                step(nc.vector.tensor_tensor(proj[:, h, :], proj[:, h, :], W[4 + g], ALU.mult))
                step(nc.vector.scalar_tensor_tensor(out=nbeta_e[:, h, :], in0=e_col[:, h, :], scalar=-1.0,
                                                    in1=cols[:, 1, :, 4 + h], op0=ALU.mult, op1=ALU.mult))
            for g in range(2):
                h = 2 * r + g
                dve.wait_ge(S("a_turned"), h + 1)
                for c in range(CH):
                    nc.vector.tensor_scalar(chunks(ktok[h])[:, c, :], chunks(bank[4 + g][:, :])[:, c, :],
                                            e_rest[:, h, c:c + 1], None, ALU.mult)
                    ins = nc.vector.tensor_scalar(chunks(proj[:, 8 + h, :])[:, c, :], chunks(bank[6 + g][:, :])[:, c, :],
                                                  cols[:, 1, c, 4 + h:5 + h], None, ALU.mult)
                ins.then_inc(S("a_tok"), 1)
            dve.wait_ge(S("a_tok"), 2 * r + 2)
            inv_dve(dve, r, a_bufs(r), between)

        def delta_round_act(act, step, r):
            for g in range(2):
                h = 2 * r + g
                act.wait_ge(S("a_diff"), 6 * h + 6)
                step(nc.scalar.activation(W[4 + g], bank[4 + g][:, :], ACT.Exp))
                step(nc.scalar.activation(W[g], W[g], ACT.Exp))
                step(nc.scalar.activation(e_glast[:, h, :], glast[:, h, :], ACT.Exp))
                step(nc.scalar.activation(e_rest[:, h, :], e_rest[:, h, :], ACT.Exp))
                nc.scalar.activation(e_col[:, h, :], cols[:, 0, :, h], ACT.Exp).then_inc(S("a_exps"), 1)
            inv_act(act, r, a_bufs(r))

        def delta_round_pe(pe, r):
            for g in range(2):
                h = 2 * r + g
                if r == 0 and g == 1:
                    pe.wait_ge(S("a_diff"), 5)
                if r > 0:
                    pe.wait_ge(S("a_tok"), 2 * r)
                    pe.wait_ge(S(f"inv_tt{g}"), 7 * r)
                nc.tensor.matmul(bank[4 + g][:, :], sel8[h], g8, start=True, stop=True)
                nc.tensor.matmul(bank[6 + g][:, :], sel8[4 + h], beta8, start=True, stop=True).then_inc(S("a_bcast"), 1)
            for g in range(2):
                h = 2 * r + g
                pe.wait_ge(S("a_diff"), 6 * h + 6)
                for c in range(CH):
                    k = chunks(proj[:, 4 + h, :])[:, c, :]
                    nc.tensor.matmul(bank[g][:, c * P:c * P + P], k, chunks(W[2 + g])[:, c, :], start=True, stop=True)
                    mm = nc.tensor.matmul(bank[2 + g][:, c * P:c * P + P], k, chunks(proj[:, h, :])[:, c, :],
                                          start=True, stop=True)
                mm.then_inc(S("a_scores"), 1)
            for g in range(2):
                h = 2 * r + g
                pe.wait_ge(S("a_exps"), h + 1)
                for c in range(CH):
                    nc.tensor.transpose(bank[4 + g][:, c * P:c * P + P], chunks(proj[:, 4 + h, :])[:, c, :], ident)
                    mm = nc.tensor.transpose(bank[6 + g][:, c * P:c * P + P], chunks(proj[:, 8 + h, :])[:, c, :], ident)
                mm.then_inc(S("a_turned"), 1)
            pe.wait_ge(S("a_tok"), 2 * r + 2)
            inv_pe(pe, r, a_bufs(r))

        def delta_chunk_dve(dve, step, c):
            if c > 0:
                dve.wait_ge(S("a_ks"), c)
                for h in range(AH):
                    nc.vector.scalar_tensor_tensor(
                        out=W[c % 2][:, h * P:h * P + P], in0=bank[0][:, h * P:h * P + P], scalar=nbeta_e[:, h, c:c + 1],
                        in1=chunks(proj[:, 8 + h, :])[:, c, :], op0=ALU.mult, op1=ALU.add).then_inc(S("a_r"), 1)

        def delta_state_dve(dve, step, c):
            if c == CH - 1:
                return
            dve.wait_ge(S("a_out"), c + 1)
            if c == 0:
                nc.vector.tensor_copy(state, bank[3][:, :]).then_inc(S("a_state"), 1)
            else:
                for h in range(AH):
                    sl = state[:, h * P:h * P + P]
                    ins = nc.vector.scalar_tensor_tensor(out=sl, in0=sl, scalar=e_glast[:, h, c:c + 1],
                                                         in1=bank[3][:, h * P:h * P + P], op0=ALU.mult, op1=ALU.add)
                    if h < AH - 1:
                        step(ins)
                ins.then_inc(S("a_state"), 1)
            dve.wait_ge(S("a_state"), c + 1)

        def delta_chunk_act(act, step, c):
            act.wait_ge(S("a_v"), c + 1)
            nc.scalar.activation(W[2 + c % 2], bank[1][:, :], ACT.Copy).then_inc(S("a_vnew"), 1)

        def delta_out_act(act, step, c):
            act.wait_ge(S("a_out"), c + 1)
            nc.scalar.activation(hT[:, 0:4, c * P:c * P + P], chunks(bank[2][:, :]), ACT.Copy).then_inc(S("a_o"), 1)

        def delta_chunk_pe(pe, c):
            if c > 0:
                pe.wait_ge(S("a_state"), c)
                for h in range(AH):
                    mm = nc.tensor.matmul(bank[0][:, h * P:h * P + P], chunks(proj[:, 4 + h, :])[:, c, :],
                                          state[:, h * P:h * P + P], start=True, stop=True)
                mm.then_inc(S("a_ks"), 1)
                pe.wait_ge(S("a_r"), AH * c)
            for h in range(AH):
                r_h = W[c % 2][:, h * P:h * P + P] if c > 0 else chunks(proj[:, 8 + h, :])[:, 0, :]
                mm = nc.tensor.matmul(bank[1][:, h * P:h * P + P], chunks(TTa[h])[:, c, :], r_h, start=True, stop=True)
            mm.then_inc(S("a_v"), 1)

        def delta_out_pe(pe, c):
            pe.wait_ge(S("a_vnew"), c + 1)
            if c > 0:
                pe.wait_ge(S("a_o"), c)
            for h in range(AH):
                v = W[2 + c % 2][:, h * P:h * P + P]
                mm = nc.tensor.matmul(bank[3][:, h * P:h * P + P], chunks(ktok[h])[:, c, :], v, start=True, stop=True)
            for h in range(AH):
                v = W[2 + c % 2][:, h * P:h * P + P]
                if c > 0:
                    nc.tensor.matmul(bank[2][:, h * P:h * P + P], state[:, h * P:h * P + P], chunks(proj[:, h, :])[:, c, :],
                                     start=True, stop=False)
                mm = nc.tensor.matmul(bank[2][:, h * P:h * P + P], v, chunks(PT[h])[:, c, :], start=(c == 0), stop=True)
            mm.then_inc(S("a_out"), 1)

        def delta_norm_dve(dve, step, h):
            o = hT[:, h, :]
            dve.wait_ge(S("head_rstd"), h + 1 + 12)
            step(nc.vector.scalar_tensor_tensor(out=o, in0=o, scalar=pc("onA"), in1=X[4 + h], op0=ALU.mult, op1=ALU.mult))
            nc.vector.tensor_tensor(o, o, proj[:, 12 + h, :], ALU.mult).then_inc(S("a_done"), 1)

        def delta_square_act(act):
            for h in range(AH):
                nc.scalar.activation(X[4 + h], hT[:, h, :], ACT.Square).then_inc(S("head_squared"), 1)

        def delta_norm_act(act, step):
            for h in range(AH):
                act.wait_ge(S("head_summed"), h + 1 + 12)
                step(nc.scalar.activation(X[h], bank[4 + h][:, :], ACT.Ln, bias=eps6, scale=1.0 / P))
            for h in range(AH):
                nc.scalar.activation(X[4 + h], X[h], ACT.Exp, scale=-0.5).then_inc(S("head_rstd"), 1)
            act.wait_ge(S("head_rstd"), AH + 12)

        def delta_norm_pe(pe):
            for h in range(AH):
                pe.wait_ge(S("head_squared"), h + 1 + 12)
                nc.tensor.matmul(bank[4 + h][:, :], ones, X[4 + h], start=True, stop=True).then_inc(S("head_summed"), 1)

        E_HALF = float(np.exp(-0.5))
        Gc, Bc, KKc = X[8:12], X[12:16], W[4:8]
        GATE = [gates[:, q, :] for q in range(BT)]
        TH, SGL, B_T0, B_T1 = hT[:, 4, :], hT[:, 5, :], hT[:, 6, :], hT[:, 7, :]
        K_SQ, K_LN, K_RN = W[12], W[13], proj[:, 31, :]
        KR = [proj[:, i:i + 2, :].rearrange("p a n -> p (a n)").rearrange("p (c x n) -> p c x n", c=CH, x=2)
              for i in (0, 2, 12)]
        KM, BM, E1, E3 = proj[:, 4, :], proj[:, 5, :], proj[:, 6, :], proj[:, 7, :]
        VT, KMT, BMT = [proj[:, 8, :], proj[:, 9, :]], [proj[:, 10, :], proj[:, 11, :]], [proj[:, 28, :], proj[:, 29, :]]
        Rb, Yb, Zb, Zt = (ryz[:, i, :] for i in range(4))
        egm = [small[:, 160 + 8 * i:164 + 8 * i] for i in range(3)]
        egc = [small[:, 164 + 8 * i:168 + 8 * i] for i in range(3)]
        omka, engm = small[:, 184:188], small[:, 188:192]
        sc_bufs = [[W[i] for i in (0, 1, 2, 3, 8, 9)], [W[10], W[11], W[12], W[13], proj[:, 30, :], proj[:, 31, :]]]
        B_SQ, B_RS, B_LN = [X[4], X[5]], [X[6], X[7]], E1
        RK, BV = [proj[:, 12, :], proj[:, 13, :]], [proj[:, 14, :], proj[:, 15, :]]

        def b_inv(q):
            t = [hT[:, 4 + i, :] if i >= q else (Gc[0], Bc[0], Gc[1])[i] for i in range(4)]
            return [(X[4], X[5], X[2 * (q % 2)], X[6], X[7]), (t[0], t[1], X[2 * (q % 2) + 1], t[2], t[3])]

        def b_scores(q, g):
            return sc_bufs[q % 2][3 * g:3 * g + 3]

        def mid(q):
            return Gc[q][:, 63:T:P]

        def lerp_dve(dve, step, n):
            j = ([12, 13] + list(range(12)))[n]
            p, d = proj[:, 16 + j, :], X[8 + n % 2]
            step(nc.vector.tensor_tensor(d[:, 1:T], p[:, 0:T - 1], p[:, 1:T], ALU.subtract))
            step(nc.vector.tensor_scalar(d[:, 0:1], p[:, 0:1], -1.0, None, ALU.mult))
            nc.vector.scalar_tensor_tensor(out=p, in0=d, scalar=pc("mu", j), in1=p, op0=ALU.mult,
                                           op1=ALU.add).then_inc(S("b_lerp"), 1)
            dve.wait_ge(S("b_lerp"), n + 1)

        def raw_keys_dve(q):
            nc.vector.tensor_scalar(KKc[q], proj[:, 20 + q, :], pc("kk", q), None, ALU.mult).then_inc(S("b_kraw"), 1)

        def keys_dve(dve, step, q):
            k, kk, g, b = proj[:, 20 + q, :], KKc[q], Gc[q], Bc[q]
            dve.wait_ge(S("b_rates"), q + 1)
            step(nc.vector.tensor_scalar(B_T0, g, -E_HALF, None, ALU.mult))
            step(nc.vector.tensor_tensor_scan(g, reset, B_T0, 0.0, ALU.mult, ALU.add))
            step(nc.vector.tensor_scalar(B_T1, b, pc("ka", q), omka[:, q:q + 1], ALU.mult, ALU.add))
            dve.wait_ge(S("b_kraw"), q + 1)
            step(nc.vector.tensor_tensor(k, k, B_T1, ALU.mult))

        def unit_keys_dve(dve, step, q):
            dve.wait_ge(S("head_rstd"), q + 1 + 8)
            nc.vector.tensor_tensor(KKc[q], KKc[q], K_RN, ALU.mult).then_inc(S("b_kk"), 1)
            dve.wait_ge(S("b_kk"), q + 1)
            step(nc.vector.tensor_tensor(Bc[q], Bc[q], KKc[q], ALU.mult))

        def rates_act(act, step, q):
            act.wait_ge(S("b_low"), q + 1)
            step(nc.scalar.activation(Gc[q], bank[4][:, :], ACT.Sigmoid, bias=pc("w0", q)))
            step(nc.scalar.activation(Bc[q], bank[5][:, :], ACT.Sigmoid, bias=pc("a0", q)))
            nc.scalar.activation(GATE[q], bank[6][:, :], ACT.Copy).then_inc(S("b_rates"), 1)
            act.wait_ge(S("b_kraw"), q + 1)
            nc.scalar.activation(K_SQ, KKc[q], ACT.Square).then_inc(S("head_squared"), 1)

        def key_norm_act(act, step, q):
            act.wait_ge(S("head_summed"), q + 1 + 8)
            step(nc.scalar.activation(K_LN, bank[7][:, :], ACT.Ln, bias=eps6))
            if q > 0:
                act.wait_ge(S("b_kk"), q)
            nc.scalar.activation(K_RN, K_LN, ACT.Exp, scale=-0.5).then_inc(S("head_rstd"), 1)
            act.wait_ge(S("head_rstd"), q + 1 + 8)

        def low_pe(pe, q):
            w2 = par[0:64, PC["w2a2"]:PC["w2a2"] + 512]
            a2 = par[64:128, PC["w2a2"]:PC["w2a2"] + 512]
            g2w = par[:, PC["g2"]:PC["g2"] + 512]
            if q > 0:
                pe.wait_ge(S("b_rates"), q)
            nc.tensor.matmul(bank[4][:, :], w2[:, q * P:q * P + P], TH[0:64, :], start=True, stop=True)
            nc.tensor.matmul(bank[5][:, :], a2[:, q * P:q * P + P], proj[64:128, 28, :], start=True, stop=True)
            nc.tensor.matmul(bank[6][:, :], g2w[:, q * P:q * P + P], SGL, start=True, stop=True).then_inc(S("b_low"), 1)

        def key_sums_pe(pe, q):
            pe.wait_ge(S("head_squared"), q + 1 + 8)
            if q > 0:
                pe.wait_ge(S("head_rstd"), q + 8)
            nc.tensor.matmul(bank[7][:, :], bones, K_SQ, start=True, stop=True).then_inc(S("head_summed"), 1)

        def scale_dve(dve, step, q, part):
            kr = KR[q % 3]
            if part == 0:
                nc.vector.tensor_tensor(chunks(E3), chunks(Gc[q]), mid(q).unsqueeze(2).broadcast_to([P, CH, P]),
                                        ALU.subtract).then_inc(S("b_diff"), 1)
            elif part == 1:
                dve.wait_ge(S("b_exps"), q + 1)
                step(nc.vector.tensor_tensor(kr[:, :, 1, :], chunks(proj[:, 16 + q, :]), chunks(E1), ALU.mult))
            elif part == 2:
                step(nc.vector.tensor_tensor(kr[:, :, 0, 1:P], chunks(KKc[q])[:, :, 1:P], chunks(E1)[:, :, 0:P - 1], ALU.mult))
                step(nc.vector.tensor_tensor(kr[:, :, 0, 0], KKc[q][:, 0:T:P], engm, ALU.mult))
            elif part == 3:
                step(nc.vector.tensor_tensor(KM, proj[:, 20 + q, :], E3, ALU.mult))
            elif part == 4:
                nc.vector.tensor_tensor(BM, Bc[q], E3, ALU.mult).then_inc(S("b_scaled"), 1)
                dve.wait_ge(S("b_scaled"), q + 1)

        def scale_act(act, step, q):
            act.wait_ge(S("b_diff"), q + 1)
            step(nc.scalar.activation(E1, E3, ACT.Exp))
            step(nc.scalar.activation(E3, E3, ACT.Exp, scale=-1.0))
            step(nc.scalar.activation(egc[q % 3], E1[:, P - 1:T:P], ACT.Copy))
            step(nc.scalar.activation(egm[q % 3], mid(q), ACT.Exp))
            nc.scalar.activation(engm, mid(q), ACT.Exp, scale=-1.0).then_inc(S("b_exps"), 1)

        def scores_pe(pe, q):
            pe.wait_ge(S("b_scaled"), q + 1)
            if q >= 2:
                pe.wait_ge(S("b_o"), CH * (q - 1))
            for g in range(2):
                sl = slice(64 * g, 64 * g + 64)
                for c in range(CH):
                    o = slice((c % 2) * 256, (c % 2) * 256 + 256)
                    kr = KR[q % 3][sl, c, :, :].rearrange("p x n -> p (x n)")
                    nc.tensor.matmul(bank[4 * g + c // 2][:, o], chunks(BM)[sl, c, :], kr, start=True, stop=True)
                    mm = nc.tensor.matmul(bank[4 * g + 2 + c // 2][:, o], chunks(KM)[sl, c, :], kr, start=True, stop=True)
                mm.then_inc(S("b_scores"), 1)
            pe.wait_ge(S("inv_mt1"), 2 + q + 1)
            for n, src in enumerate((proj[:, 24 + q, :], KM, BM)):
                for c in range(CH):
                    mm = nc.tensor.transpose(bank[4 + n][:, c * P:c * P + P], chunks(src)[:, c, :], ident)
            mm.then_inc(S("b_turned"), 1)
            pe.wait_ge(S("b_tok"), q + 1)

        def scores_dve(dve, step, q):
            m_i = incl.unsqueeze(1).broadcast_to([P, 2, P])
            m_s = strict.unsqueeze(1).broadcast_to([P, 2, P])
            for g in range(2):
                strict_v, with_y, with_v = b_scores(q, g)
                dve.wait_ge(S("b_scores"), 2 * q + g + 1)
                for cc in range(2):
                    by, bv = bank[4 * g + cc][:, :], bank[4 * g + 2 + cc][:, :]
                    by = by.rearrange("p (c x n) -> p c x n", c=2, x=2)
                    bv = bv.rearrange("p (c x n) -> p c x n", c=2, x=2)
                    two = slice(2 * cc, 2 * cc + 2)
                    step(nc.vector.tensor_tensor(chunks(with_y)[:, two, :], by[:, :, 1, :], m_i, ALU.mult))
                    step(nc.vector.tensor_tensor(chunks(strict_v)[:, two, :], bv[:, :, 0, :], m_s, ALU.mult))
                    step(nc.vector.tensor_tensor(chunks(with_v)[:, two, :], bv[:, :, 1, :], m_i, ALU.mult))
                    ins = nc.vector.tensor_copy(chunks(b_inv(q)[g][0])[:, two, :], by[:, :, 0, :])
                    if cc == 0:
                        step(ins)
                ins.then_inc(S(f"inv_mt{g}"), 1)
                dve.wait_ge(S(f"inv_mt{g}"), 2 + q + 1)

        def turned_act(act, step, q):
            act.wait_ge(S("b_turned"), q + 1)
            step(nc.scalar.activation(VT[q % 2], bank[4][:, :], ACT.Copy))
            step(nc.scalar.activation(KMT[q % 2], bank[5][:, :], ACT.Copy))
            nc.scalar.activation(BMT[q % 2], bank[6][:, :], ACT.Copy).then_inc(S("b_tok"), 1)

        def slot_pe(pe, q, k):
            if q < 0:
                return
            c, part = divmod(k, 3)
            n = CH * q + c
            kr = KR[q % 3]
            vt, kmt, bmt = VT[q % 2], KMT[q % 2], BMT[q % 2]
            if part == 0:
                if n > 0:
                    pe.wait_ge(S("b_o"), n)
                if c > 0:
                    pe.wait_ge(S("b_state"), (CH - 1) * q + c)
                    nc.tensor.matmul(bank[6][:, 0:P], kr[:, c, 0, :], Zb, start=True, stop=True)
                for g in range(2):
                    hs_ = slice(64 * g, 64 * g + 64)
                    mm = nc.tensor.matmul(bank[6][:, hs_], chunks(b_scores(q, g)[0])[:, c, :], chunks(vt)[:, c, hs_],
                                          start=(c == 0), stop=True, skip_group_check=True)
                mm.then_inc(S("b_r"), 1)
            elif part == 1:
                pe.wait_ge(S("b_rset"), n + 1)
                if c > 0:
                    pe.wait_ge(S("b_state"), (CH - 1) * q + c)
                for g in range(2):
                    hs_ = slice(64 * g, 64 * g + 64)
                    mm = nc.tensor.matmul(bank[7][:, hs_], chunks(b_inv(q)[g][2])[:, c, :], Rb[:, hs_], start=True, stop=True)
                mm.then_inc(S("b_y"), 1)
            else:
                pe.wait_ge(S("b_yset"), n + 1)
                nc.tensor.matmul(bank[7][:, 0:P], chunks(kmt)[:, c, :], chunks(vt)[:, c, :], start=True, stop=False)
                nc.tensor.matmul(bank[7][:, 0:P], chunks(bmt)[:, c, :], Yb, start=False, stop=True)
                if c > 0:
                    nc.tensor.matmul(bank[6][:, 0:P], Zb, kr[:, c, 1, :], start=True, stop=True)
                for g in range(2):
                    hs_ = slice(64 * g, 64 * g + 64)
                    _, wy, wv = b_scores(q, g)
                    nc.tensor.matmul(bank[6][hs_, 0:P], chunks(vt)[:, c, hs_], chunks(wv)[:, c, :], start=(c == 0), stop=(c > 0),
                                     skip_group_check=True)
                    mm = nc.tensor.matmul(bank[6][hs_, 0:P], Yb[:, hs_], chunks(wy)[:, c, :], start=False, stop=True,
                                          skip_group_check=True)
                mm.then_inc(S("b_out"), 1)

        def slot_dve(dve, step, q, k):
            if q < 0:
                return
            c, part = divmod(k, 3)
            n = CH * q + c
            if part == 0:
                dve.wait_ge(S("b_r"), n + 1)
                nc.vector.tensor_copy(Rb, bank[6][:, 0:P]).then_inc(S("b_rset"), 1)
            elif part == 1:
                dve.wait_ge(S("b_y"), n + 1)
                nc.vector.tensor_scalar(Yb, bank[7][:, 0:P], -1.0, None, ALU.mult).then_inc(S("b_yset"), 1)
            elif c < CH - 1:
                dve.wait_ge(S("b_out"), n + 1)
                step(nc.vector.tensor_tensor(Zt, bank[7][:, 0:P], bones, ALU.mult))
                if c > 0:
                    step(nc.vector.tensor_tensor(Zt, Zt, Zb, ALU.add))
                nc.vector.tensor_scalar(Zb, Zt, egc[q % 3][:, c:c + 1], egm[q % 3][:, c + 1:c + 2], ALU.mult,
                                        ALU.mult).then_inc(S("b_state"), 1)
                dve.wait_ge(S("b_state"), (CH - 1) * q + c + 1)

        def slot_act(act, q, k):
            c, part = divmod(k, 3)
            if q >= 0 and part == 2:
                act.wait_ge(S("b_out"), CH * q + c + 1)
                nc.scalar.activation(hT[:, 4 + q, c * P:c * P + P], bank[6][:, 0:P], ACT.Copy).then_inc(S("b_o"), 1)

        def norm_turns(last_slot):
            return [divmod(k, 4) for k in ((last_slot,) if last_slot < 12 else range(12, 17))]

        def rwkv_norm_dve(dve, step, k):
            for q, part in norm_turns(k):
                if part == 0 and q > 0:
                    o = hT[:, 3 + q, :]
                    dve.wait_ge(S("b_bonus"), q)
                    step(nc.vector.tensor_tensor(BV[(q - 1) % 2], bank[2 + (q - 1) % 2][:, :], proj[:, 23 + q, :], ALU.mult))
                    dve.wait_ge(S("head_rstd"), q + 16)
                    step(nc.vector.scalar_tensor_tensor(out=o, in0=o, scalar=pc("lnw", q - 1), in1=B_RS[(q - 1) % 2],
                                                        op0=ALU.mult, op1=ALU.mult))
                    step(nc.vector.scalar_tensor_tensor(out=o, in0=o, scalar=pc("lnb", q - 1), in1=BV[(q - 1) % 2],
                                                        op0=ALU.add, op1=ALU.add))
                    nc.vector.tensor_tensor(o, o, GATE[q - 1], ALU.mult).then_inc(S("b_done"), 1)
                if part == 0 and q < BT:
                    if q >= 2:
                        dve.wait_ge(S("b_bonus"), q - 1)
                    nc.vector.scalar_tensor_tensor(out=RK[q % 2], in0=proj[:, 16 + q, :], scalar=pc("rk", q),
                                                   in1=proj[:, 20 + q, :], op0=ALU.mult, op1=ALU.mult).then_inc(S("b_rk"), 1)
                if part == 1:
                    o = hT[:, 4 + q, :]
                    dve.wait_ge(S("b_mean"), q + 1)
                    nc.vector.scalar_tensor_tensor(out=o, in0=bank[q % 2][:, :], scalar=-1.0 / 64, in1=o, op0=ALU.mult,
                                                   op1=ALU.add).then_inc(S("b_centred"), 1)

        def rwkv_norm_act(act, step, k):
            for q, part in norm_turns(k):
                if part == 2:
                    act.wait_ge(S("b_centred"), q + 1)
                    nc.scalar.activation(B_SQ[q % 2], hT[:, 4 + q, :], ACT.Square).then_inc(S("head_squared"), 1)
                if part == 3:
                    act.wait_ge(S("head_summed"), q + 1 + 16)
                    step(nc.scalar.activation(B_LN, bank[4 + q % 2][:, :], ACT.Ln, bias=epsg, scale=1.0 / 64))
                    if q >= 2:
                        act.wait_ge(S("b_done"), q - 1)
                    nc.scalar.activation(B_RS[q % 2], B_LN, ACT.Exp, scale=-0.5).then_inc(S("head_rstd"), 1)
                    act.wait_ge(S("head_rstd"), q + 1 + 16)

        def rwkv_norm_pe(pe, k):
            for q, part in norm_turns(k):
                if part == 0 and q < BT:
                    pe.wait_ge(S("b_o"), CH * (q + 1))
                    if q >= 2:
                        pe.wait_ge(S("b_centred"), q - 1)
                    nc.tensor.matmul(bank[q % 2][:, :], bones, hT[:, 4 + q, :], start=True, stop=True).then_inc(S("b_mean"), 1)
                if part == 1:
                    pe.wait_ge(S("b_rk"), q + 1)
                    if q >= 2:
                        pe.wait_ge(S("b_done"), q - 1)
                    nc.tensor.matmul(bank[2 + q % 2][:, :], bones, RK[q % 2], start=True, stop=True).then_inc(S("b_bonus"), 1)
                if part == 2:
                    pe.wait_ge(S("head_squared"), q + 1 + 16)
                    if q >= 2:
                        pe.wait_ge(S("head_rstd"), q - 1 + 16)
                    nc.tensor.matmul(bank[4 + q % 2][:, :], bones, B_SQ[q % 2], start=True, stop=True).then_inc(S("head_summed"), 1)

        def mixer0_dve(dve, step):
            delta_prep_dve(dve, step)
            dve.wait_ge(S("tile_free0"), 2 + N_IN)
            dve.wait_ge(S("tile_free1"), 2 + N_IN)
            step(nc.vector.tensor_scalar(omka, par[:, PC["ka"]:PC["ka"] + 4], -1.0, 1.0, ALU.mult, ALU.add))
            for r in range(2):
                delta_round_dve(dve, step, r, lambda k: lerp_dve(dve, step, 7 * r + k // 2) if k % 2 == 0 else
                                (lerp_dve(dve, step, 7 * r + 6) if k == 11 else None))
            for c in range(CH + 2):
                if c < CH:
                    delta_chunk_dve(dve, step, c)
                if c >= 2:
                    unit_keys_dve(dve, step, c - 2)
                if c < CH:
                    delta_state_dve(dve, step, c)
                    raw_keys_dve(c)
                if 1 <= c <= CH:
                    keys_dve(dve, step, c - 1)
            for part in range(5):
                scale_dve(dve, step, 0, part)
            for h in range(AH):
                delta_norm_dve(dve, step, h)
            dve.wait_ge(S("a_done"), AH)
            for q in range(BT):
                scores_dve(dve, step, q)

                def between(k):
                    slot_dve(dve, step, q - 1, k)
                    if k % 2 == 0 and k < 10 and q + 1 < BT:
                        scale_dve(dve, step, q + 1, k // 2)
                inv_dve(dve, 2 + q, b_inv(q), between)
            for k in range(12):
                slot_dve(dve, step, BT - 1, k)
                rwkv_norm_dve(dve, step, k)
            rwkv_norm_dve(dve, step, 12)
            dve.wait_ge(S("b_done"), BT)

        def mixer0_act(act, step):
            delta_prep_act(act, step)
            for r in range(2):
                delta_round_act(act, step, r)
            act.wait_ge(S("b_lerp"), 14)
            step(nc.scalar.activation(TH[0:64, :], proj[0:64, 28, :], ACT.Tanh))
            nc.scalar.activation(SGL, proj[:, 29, :], ACT.Sigmoid).then_inc(S("b_lora"), 1)
            for c in range(CH + 1):
                if c < CH:
                    delta_chunk_act(act, step, c)
                    delta_out_act(act, step, c)
                if c > 0:
                    key_norm_act(act, step, c - 1)
                if c < CH:
                    rates_act(act, step, c)
            act.wait_ge(S("a_o"), CH)
            delta_square_act(act)
            scale_act(act, step, 0)
            delta_norm_act(act, step)
            for q in range(BT):
                turned_act(act, step, q)

                def between(k):
                    if k == 0 and q + 1 < BT:
                        scale_act(act, step, q + 1)
                    slot_act(act, q - 1, k)
                inv_act(act, 2 + q, b_inv(q), between)
            for k in range(12):
                slot_act(act, BT - 1, k)
                rwkv_norm_act(act, step, k)
            rwkv_norm_act(act, step, 12)

        def mixer0_pe(pe):
            delta_prep_pe(pe)
            for r in range(2):
                delta_round_pe(pe, r)
            for g in range(2):
                pe.wait_ge(S(f"inv_tt{g}"), 14)
            pe.wait_ge(S("b_lora"), 1)
            for c in range(CH + 1):
                if c < CH:
                    delta_chunk_pe(pe, c)
                    delta_out_pe(pe, c)
                if c > 0:
                    key_sums_pe(pe, c - 1)
                if c < CH:
                    low_pe(pe, c)
            pe.wait_ge(S("b_rates"), BT)
            pe.wait_ge(S("head_rstd"), 12)
            delta_norm_pe(pe)
            pe.wait_ge(S("a_done"), AH)
            pe.wait_ge(S("a_o"), CH)
            for q in range(BT):
                scores_pe(pe, q)
                inv_pe(pe, 2 + q, b_inv(q), lambda k: slot_pe(pe, q - 1, k))
                for g in range(2):
                    pe.wait_ge(S(f"inv_tt{g}"), 7 * (3 + q))
            for k in range(12):
                slot_pe(pe, BT - 1, k)
                rwkv_norm_pe(pe, k)
            rwkv_norm_pe(pe, 12)
            pe.wait_ge(S("b_done"), BT)

        Dt, Et, Qs, Ks = W[0:3] + [X[8]], W[3:6] + [X[9]], W[6:9], X[0:3]
        X_keys = extra[:, 0:3, :]
        ACC, KD, KDT, VTc = X[3:5], W[9:11], [X[5]] * 2, [X[6]] * 2
        St = [X[7]] * 2
        sqt, lnt, rst = W[11], W[12], W[13]
        UN = 8
        UNITS = UN * CHEADS
        sbk = [bank[0], bank[1], bank[7]]

        def ended(u, after):
            h, r = divmod(u - after + 1, UN)
            return [h - 1] if r == 0 and 1 <= h <= CHEADS else []

        def halves(ap, s):
            return ap.rearrange("p (b x s) -> p b x s", x=2, s=s)

        def middle(ap, s):
            return halves(ap, s)[:, :, 0, s - 1:s].broadcast_to([P, T // (2 * s), s])

        lbv, oml = small[:, 200:208], small[:, 208:216]
        eC = small[:, 216:224].rearrange("p (a c) -> p a c", a=2)

        def hgrn_dve(dve, step):
            nc.vector.tensor_tensor(small[:, 192:200], par[:, PC["lb"]:PC["lb"] + 8], par[:, PC["lb"] + 8:PC["lb"] + 16],
                                    ALU.subtract).then_inc(S("c_lb"), 1)
            drain_copies("dve", dve, B_CIN, 8, 1, proj, 0, T)
            for i in range(8):
                for h in (2 * i, 2 * i + 1) if i < 4 else ():
                    f = proj[:, 8 + h, :]
                    dve.wait_ge(S("c_sig"), h + 1)
                    nc.vector.tensor_scalar(f, f, oml[:, h:h + 1], lbv[:, h:h + 1], ALU.mult, ALU.add).then_inc(S("c_f"), 1)
                for h in (2 * i - 8, 2 * i - 7) if i >= 4 else ():
                    g = proj[:, 8 + h, :]
                    dve.wait_ge(S("c_ln"), h + 1)
                    step(nc.vector.tensor_tensor_scan(g, reset, g, 0.0, ALU.mult, ALU.add))
                drain_copies("dve", dve, B_CIN + 8 + i, 1, 1, proj, 16 + 2 * i, T)
            dve.wait_ge(S("tile_free0"), 2 + B_COUT)
            dve.wait_ge(S("tile_free1"), 2 + B_COUT)
            for h in range(CHEADS):
                nc.vector.tensor_scalar(hT[:, h, :], W[h], oml[:, h:h + 1], None, ALU.mult).then_inc(S("c_f"), 1)
            dve.wait_ge(S("c_f"), 2 * CHEADS)

            def spread(u):
                h, li = divmod(u, UN)
                if li == 7:
                    return
                n, s = 7 * h + li, LEVELS[li]
                g = proj[:, 8 + h, :]
                if n >= 4:
                    dve.wait_ge(S("c_e"), n - 3)
                nc.vector.tensor_tensor(halves(Dt[n % 4], s)[:, :, 1, :], halves(g, s)[:, :, 1, :], middle(g, s),
                                        ALU.subtract).then_inc(S("c_d"), 1)

            def queries(u):
                h, li = divmod(u, UN)
                if li == 7:
                    return
                n, s = 7 * h + li, LEVELS[li]
                dve.wait_ge(S("c_e"), n + 1)
                if n >= 3:
                    dve.wait_ge(S("c_s"), u - 2 - (1 if li < 3 and h > 0 else 0))
                nc.vector.tensor_tensor(halves(Qs[n % 3], s)[:, :, 1, :], halves(proj[:, h, :], s)[:, :, 1, :],
                                        halves(Et[n % 4], s)[:, :, 1, :], ALU.mult).then_inc(S("c_q"), 1)

            def gather(u):
                h, li = divmod(u, UN)
                acc = chunks(ACC[h % 2])
                if li == 0:
                    if h >= 2:
                        dve.wait_ge(S("c_o"), h - 1)
                    step(nc.vector.memset(ACC[h % 2], 0.0))
                dve.wait_ge(S("c_s"), u + 1)
                m = lvl[li] if li < 7 else ident
                nc.vector.copy_predicated(acc, over4(m).bitcast(I32), chunks(sbk[u % 3][:, :])).then_inc(S("c_acc"), 1)
                dve.wait_ge(S("c_acc"), u + 1)

            def rest(h):
                g = proj[:, 8 + h, :]
                last = chunks(g)[:, :, P - 1:P].broadcast_to([P, CH, P])
                if h >= 2:
                    dve.wait_ge(S("c_turned"), h - 1)
                nc.vector.tensor_tensor(chunks(KD[h % 2]), last, chunks(g), ALU.subtract).then_inc(S("c_rest"), 1)

            def decayed_q(h):
                dve.wait_ge(S("c_tail_e"), h + 1)
                nc.vector.tensor_tensor(proj[:, h, :], proj[:, h, :], proj[:, 8 + h, :], ALU.mult).then_inc(S("c_qg"), 1)

            def states(h):
                dve.wait_ge(S("c_incr"), h + 1)
                if h >= 1:
                    dve.wait_ge(S("c_o"), h)
                st = chunks(St[h % 2])
                step(nc.vector.tensor_copy(st[:, 1, :], bank[4][:, 0:P]))
                step(nc.vector.scalar_tensor_tensor(out=st[:, 2, :], in0=st[:, 1, :], scalar=eC[:, h % 2, 1:2],
                                                    in1=bank[4][:, P:2 * P], op0=ALU.mult, op1=ALU.add))
                nc.vector.scalar_tensor_tensor(out=st[:, 3, :], in0=st[:, 2, :], scalar=eC[:, h % 2, 2:3],
                                               in1=bank[4][:, 2 * P:3 * P], op0=ALU.mult, op1=ALU.add).then_inc(S("c_state"), 1)

            def close(h):
                o = hT[:, h, :]
                dve.wait_ge(S("head_rstd"), h + 1 + 20)
                step(nc.vector.scalar_tensor_tensor(out=o, in0=o, scalar=pc("onC"), in1=rst, op0=ALU.mult, op1=ALU.mult))
                nc.vector.tensor_tensor(o, o, proj[:, 24 + h, :], ALU.mult).then_inc(S("c_done"), 1)

            for u in range(3):
                spread(u)
            for u in range(UNITS + 16):
                if u + 3 < UNITS:
                    spread(u + 3)
                if u < UNITS:
                    queries(u)
                if 0 <= u - 2 < UNITS:
                    gather(u - 2)
                for h in ended(u, 1):
                    rest(h)
                for h in ended(u, 5):
                    decayed_q(h)
                for h in ended(u, 7):
                    states(h)
                for h in ended(u, 15):
                    close(h)
            dve.wait_ge(S("c_done"), CHEADS)

        def hgrn_act(act, step):
            act.wait_ge(S("c_lb"), 1)
            step(nc.scalar.activation(lbv, small[:, 192:200], ACT.Sigmoid, scale=-1.0))
            step(nc.scalar.activation(oml, small[:, 192:200], ACT.Sigmoid))
            drain_copies("act", act, B_CIN, 8, 0, proj, 0, T)
            act.wait_ge(S("tile_free1"), 2 + B_CIN + 8)
            for i in range(8):
                for h in (2 * i, 2 * i + 1) if i < 4 else ():
                    nc.scalar.activation(W[h], proj[:, 8 + h, :], ACT.Sigmoid, scale=-1.0).then_inc(S("c_sigk"), 1)
                    act.wait_ge(S("c_sigk"), h + 1)
                    nc.scalar.activation(proj[:, 8 + h, :], proj[:, 8 + h, :], ACT.Sigmoid).then_inc(S("c_sig"), 1)
                for h in (2 * i, 2 * i + 1) if i < 4 else ():
                    nc.scalar.activation(proj[:, h, :], proj[:, h, :], ACT.Silu).then_inc(S("c_silu"), 1)
                for h in (2 * i - 8, 2 * i - 7) if i >= 4 else ():
                    act.wait_ge(S("c_f"), h + 1)
                    nc.scalar.activation(proj[:, 8 + h, :], proj[:, 8 + h, :], ACT.Ln).then_inc(S("c_ln"), 1)
                for h in (2 * i - 10, 2 * i - 9) if i >= 5 else ():
                    for half in range(2):
                        act.wait_ge(S(f"tile_free{half}"), 2 + B_CIN + 8 + i)
                    step(nc.scalar.activation(proj[:, 24 + h, :], proj[:, 24 + h, :], ACT.Silu))
                drain_copies("act", act, B_CIN + 8 + i, 1, 0, proj, 16 + 2 * i, T)
            act.wait_ge(S("tile_free0"), 2 + B_COUT)
            act.wait_ge(S("tile_free1"), 2 + B_COUT)

            def exps(u):
                h, li = divmod(u, UN)
                if li == 7:
                    return
                n = 7 * h + li
                act.wait_ge(S("c_d"), n + 1)
                act.wait_ge(S("c_dk"), n + 1)
                if n >= 4:
                    act.wait_ge(S("c_q"), n - 3)
                    act.wait_ge(S("c_k"), n - 3)
                nc.scalar.activation(Et[n % 4], Dt[n % 4], ACT.Exp).then_inc(S("c_e"), 1)

            for u in range(3):
                exps(u)
            for h in (6, 7):
                step(nc.scalar.activation(proj[:, 24 + h, :], proj[:, 24 + h, :], ACT.Silu))
            for u in range(UNITS + 16):
                if u + 3 < UNITS:
                    exps(u + 3)
                for h in ended(u, 2):
                    act.wait_ge(S("c_rest"), h + 1)
                    step(nc.scalar.activation(KD[h % 2], KD[h % 2], ACT.Exp))
                    if h >= 2:
                        act.wait_ge(S("c_state"), h - 1)
                    step(nc.scalar.activation(eC[:, h % 2, :], proj[:, 8 + h, P - 1:T:P], ACT.Exp))
                    nc.scalar.activation(proj[:, 8 + h, :], proj[:, 8 + h, :], ACT.Exp).then_inc(S("c_tail_e"), 1)
                for h in ended(u, 4):
                    act.wait_ge(S("c_turned"), h + 1)
                    if h >= 1:
                        act.wait_ge(S("c_o"), h)
                    step(nc.scalar.activation(KDT[h % 2], bank[2][:, :], ACT.Copy))
                    nc.scalar.activation(VTc[h % 2], bank[3][:, :], ACT.Copy).then_inc(S("c_tok"), 1)
                for h in ended(u, 9):
                    act.wait_ge(S("c_o"), h + 1)
                    nc.scalar.activation(hT[:, h, :], bank[5][:, :], ACT.Copy).then_inc(S("c_oset"), 1)
                    act.wait_ge(S("c_oset"), h + 1)
                    nc.scalar.activation(sqt, hT[:, h, :], ACT.Square).then_inc(S("head_squared"), 1)
                for h in ended(u, 12):
                    act.wait_ge(S("head_summed"), h + 1 + 20)
                    step(nc.scalar.activation(lnt, bank[6][:, :], ACT.Ln, bias=eps6, scale=1.0 / P))
                    if h > 0:
                        act.wait_ge(S("c_done"), h)
                    nc.scalar.activation(rst, lnt, ACT.Exp, scale=-0.5).then_inc(S("head_rstd"), 1)

        def hgrn_pool(pool):
            pool.wait_ge(S("tile_free1"), 2 + B_COUT)
            nc.gpsimd.memset(X_keys, 0.0).then_inc(S("zero_set"), 1)
            pool.wait_ge(S("zero_set"), 1)

            def spread(u):
                h, li = divmod(u, UN)
                if u >= UNITS or li == 7:
                    return
                n, s, g = 7 * h + li, LEVELS[li], proj[:, 8 + h, :]
                if n >= 4:
                    pool.wait_ge(S("c_e"), n - 3)
                nc.gpsimd.tensor_tensor(halves(Dt[n % 4], s)[:, :, 0, :], middle(g, s), halves(g, s)[:, :, 0, :],
                                        ALU.subtract).then_inc(S("c_dk"), 1)

            pool.wait_ge(S("c_f"), 2 * CHEADS)
            for u in range(3):
                spread(u)
            for u in range(UNITS + 16):
                h, li = divmod(u, UN)
                if u >= 1:
                    spread(u + 2)
                if u < UNITS and li < 7:
                    n, s = 7 * h + li, LEVELS[li]
                    pool.wait_ge(S("c_e"), n + 1)
                    if n >= 3:
                        pool.wait_ge(S("c_s"), u - 2 - (1 if li < 3 and h > 0 else 0))
                    nc.gpsimd.tensor_tensor(halves(Ks[n % 3], s)[:, :, 0, :], halves(hT[:, h, :], s)[:, :, 0, :],
                                            halves(Et[n % 4], s)[:, :, 0, :], ALU.mult).then_inc(S("c_k"), 1)
                for h in ended(u, 3):
                    pool.wait_ge(S("c_tail_e"), h + 1)
                    nc.gpsimd.tensor_tensor(KD[h % 2], KD[h % 2], hT[:, h, :], ALU.mult).then_inc(S("c_kd"), 1)

        def hgrn_pe(pe):
            pe.wait_ge(S("c_silu"), CHEADS)
            pe.wait_ge(S("c_f"), 2 * CHEADS)
            for u in range(UNITS + 16):
                if u < UNITS:
                    h, li = divmod(u, UN)
                    if u >= 3:
                        pe.wait_ge(S("c_acc"), u - 2)
                    n = 7 * h + li
                    k, q = hT[:, h, :], proj[:, h, :]
                    if li < 7:
                        pe.wait_ge(S("c_q"), n + 1)
                        pe.wait_ge(S("c_k"), n + 1)
                        k, q = Ks[n % 3], Qs[n % 3]
                    for c in range(CH):
                        mm = nc.tensor.matmul(sbk[u % 3][:, c * P:c * P + P], chunks(k)[:, c, :], chunks(q)[:, c, :],
                                              start=True, stop=True)
                    mm.then_inc(S("c_s"), 1)
                for h in ended(u, 3):
                    if h > 0:
                        pe.wait_ge(S("c_tok"), h)
                    for c in range(CH):
                        nc.tensor.transpose(bank[3][:, c * P:c * P + P], chunks(proj[:, 16 + h, :])[:, c, :], ident)
                    pe.wait_ge(S("c_kd"), h + 1)
                    for c in range(CH):
                        mm = nc.tensor.transpose(bank[2][:, c * P:c * P + P], chunks(KD[h % 2])[:, c, :], ident)
                    mm.then_inc(S("c_turned"), 1)
                for h in ended(u, 5):
                    pe.wait_ge(S("c_tok"), h + 1)
                    if h > 0:
                        pe.wait_ge(S("c_state"), h)
                    for c in range(CH - 1):
                        mm = nc.tensor.matmul(bank[4][:, c * P:c * P + P], chunks(KDT[h % 2])[:, c, :], chunks(VTc[h % 2])[:, c, :],
                                              start=True, stop=True)
                    mm.then_inc(S("c_incr"), 1)
                for h in ended(u, 8):
                    pe.wait_ge(S("c_state"), h + 1)
                    pe.wait_ge(S("c_qg"), h + 1)
                    pe.wait_ge(S("c_acc"), UN * (h + 1))
                    if h > 0:
                        pe.wait_ge(S("c_oset"), h)
                    for c in range(CH):
                        if c > 0:
                            nc.tensor.matmul(bank[5][:, c * P:c * P + P], chunks(St[h % 2])[:, c, :], chunks(proj[:, h, :])[:, c, :],
                                             start=True, stop=False)
                        mm = nc.tensor.matmul(bank[5][:, c * P:c * P + P], chunks(VTc[h % 2])[:, c, :],
                                              chunks(ACC[h % 2])[:, c, :], start=(c == 0), stop=True)
                    mm.then_inc(S("c_o"), 1)
                for h in ended(u, 10):
                    pe.wait_ge(S("head_squared"), h + 1 + 20)
                    if h > 0:
                        pe.wait_ge(S("head_rstd"), h + 20)
                    nc.tensor.matmul(bank[6][:, :], ones, sqt, start=True, stop=True).then_inc(S("head_summed"), 1)

        memn = proj[:, 24:32, :]
        PX = [work[:, 2 * i:2 * i + 2, :].rearrange("p a (t n) -> p (a t) n", n=M) for i in range(2)]
        PXT = W[4:6]
        mx = small[:, 224:232].rearrange("p (a t) -> p a t", a=2)
        sm = small[:, 232:240].rearrange("p (a t) -> p a t", a=2)
        XSC = (D // XH) ** -0.5

        def sbank(x):
            return [bank[4 + 2 * (x % 2) + i][:, :].rearrange("p (t n) -> p t n", n=M) for i in range(2)]

        def xattn_dve(dve, step, L):
            for x in range(XH):
                n = XH * L + x
                dve.wait_ge(S("x_scores"), n + 1)
                if x >= 1:
                    dve.wait_ge(S("x_probs"), n)
                for i in range(2):
                    step(nc.vector.tensor_reduce(mx[:, x % 2, 2 * i:2 * i + 2], sbank(x)[i], AX.X, ALU.max))
                nc.vector.tensor_scalar(mx[:, x % 2, :], mx[:, x % 2, :], -XSC, None, ALU.mult).then_inc(S("x_max"), 1)
                dve.wait_ge(S("x_exp"), n + 1)
                step(nc.vector.reciprocal(sm[:, x % 2, :], sm[:, x % 2, :]))
                for t in range(CH):
                    ins = nc.vector.tensor_scalar(PX[x % 2][:, t, :], PX[x % 2][:, t, :], sm[:, x % 2, t:t + 1], None, ALU.mult)
                ins.then_inc(S("x_probs"), 1)
                dve.wait_ge(S("x_turned"), n + 1)
                step(nc.vector.tensor_copy(PXT[0], bank[0][:, :]))
                nc.vector.tensor_copy(PXT[1], bank[1][:, :]).then_inc(S("x_pt"), 1)

        def xattn_act(act, step, L):
            def out(x):
                act.wait_ge(S("x_out"), XH * L + x + 1)
                step(nc.scalar.activation(hT[:, 2 * x, :], bank[2][:, :], ACT.Copy))
                step(nc.scalar.activation(hT[:, 2 * x + 1, :], bank[3][:, :], ACT.Copy))
                nc.scalar.activation(x_hi[:, 2 * x, :], bank[2][:, :], ACT.Copy).then_inc(S("x_high"), 1)
                nc.scalar.activation(x_hi[:, 2 * x + 1, :], bank[3][:, :], ACT.Copy).then_inc(S("x_high"), 1)
                act.wait_ge(S("x_high"), DT * (3 * L + 2) + 2 * x + 2)
                act.sem_inc(S("x_o"), 1)

            for x in range(XH):
                n = XH * L + x
                act.wait_ge(S("x_max"), n + 1)
                if x >= 2:
                    act.wait_ge(S("x_turned"), n - 1)
                for t in range(CH):
                    ins = nc.scalar.activation(PX[x % 2][:, t, :], sbank(x)[t // 2][:, t % 2, :], ACT.Exp, bias=mx[:, x % 2, t:t + 1],
                                               scale=XSC, accum_out=sm[:, x % 2, t:t + 1])
                    if t < CH - 1:
                        step(ins)
                ins.then_inc(S("x_exp"), 1)
                if x > 0:
                    out(x - 1)
            out(XH - 1)

        def xattn_pe(pe, L):
            first = B_XA0 if L == 0 else B_XA1
            pe.wait_ge(S("tile_free0"), 2 + first + 12)
            pe.wait_ge(S("tile_free1"), 2 + first + 12)

            def scores(x):
                if x >= 2:
                    pe.wait_ge(S("x_exp"), XH * L + x - 1)
                for t in range(CH):
                    for d in range(2):
                        mm = nc.tensor.matmul(sbank(x)[t // 2][:, t % 2, :], chunks(proj[:, 16 + 2 * x + d, :])[:, t, :],
                                              proj[:, 2 * x + d, 0:M], start=(d == 0), stop=(d == 1))
                mm.then_inc(S("x_scores"), 1)

            scores(0)
            for x in range(XH):
                n = XH * L + x
                if x + 1 < XH:
                    scores(x + 1)
                pe.wait_ge(S("x_probs"), n + 1)
                if x > 0:
                    pe.wait_ge(S("x_pt"), n)
                for m in range(2):
                    for t in range(CH):
                        mm = nc.tensor.transpose(bank[m][:, t * P:t * P + P], PX[x % 2][:, t, m * P:m * P + P], ident)
                mm.then_inc(S("x_turned"), 1)
                pe.wait_ge(S("x_pt"), n + 1)
                if x > 0:
                    pe.wait_ge(S("x_o"), n)
                for d in range(2):
                    for m in range(2):
                        mm = nc.tensor.matmul(bank[2 + d][:, :], proj[:, 8 + 2 * x + m, d * P:d * P + P], PXT[m],
                                              start=(m == 0), stop=(m == 1))
                mm.then_inc(S("x_out"), 1)
            pe.wait_ge(S("x_o"), XH * (L + 1))

        htok = proj[:, 0:8, :].rearrange("p (t a) n -> p t (a n)", a=2)
        y1 = htok
        y2 = proj[:, 8:16, :].rearrange("p (t a) n -> p t (a n)", a=2)
        xg = [proj[:, 8 + 2 * i:10 + 2 * i, :].rearrange("p a n -> p (a n)") for i in range(2)]
        xgT = [proj[:, 12 + 2 * i:14 + 2 * i, :].rearrange("p a (b n) -> p (a b) n", n=P) for i in range(2)]
        ysb = [proj[:, 16 + 2 * i:18 + 2 * i, :] for i in range(2)]
        hs = [W[i][:, 0:FF] for i in range(2)]
        hid = [W[2 + i][:, 0:FF] for i in range(2)]
        hidT = [W[4 + i][:, 0:FF].rearrange("p (a n) -> p a n", a=2) for i in range(2)]
        w13 = [ring[:, 3 * i:3 * i + 2, :].rearrange("p a n -> p (a n)").rearrange("p (k n) -> p k n", k=DT) for i in range(2)]
        w2e = [ring[:, 3 * i + 2, :].rearrange("p (k n) -> p k n", k=2) for i in range(2)]

        xbank = [(bank[0], bank[1]), (bank[4], bank[5])]
        ybank = [(bank[6], bank[7]), (bank[2], bank[3])]

        def sm3(o, *dims):
            n = int(np.prod(dims))
            names = ["a", "b", "c"][:len(dims)]
            pat = f"p ({' '.join(names)}) -> p {' '.join(names)}"
            return small[:, o:o + n].rearrange(pat, **dict(zip(names, dims)))

        lgT = W[7][0:20, :]
        lg = sm3(256, CH, 20)
        gl, el = lg[:, :, 0:4], lg[:, :, 4:20].rearrange("p t (g i) -> p t g i", g=4)
        oh = sm3(336, CH, NG)
        oh1, oh2 = sm3(352, CH, EG), sm3(368, CH, EG)
        ing, sh = sm3(384, CH, EG), sm3(400, CH, NG)
        wt = sm3(416, CH, 4)
        gmax, gsum, m1, m2 = (small[:, 432 + 4 * i:436 + 4 * i] for i in range(4))
        gate1, gate2, e2, tmp4 = (small[:, 448 + 4 * i:452 + 4 * i] for i in range(4))
        sel1, sel2, sel = sm3(464, CH, NG, EG), sm3(528, CH, NG, EG), sm3(592, CH, NE)
        pre = sm3(656, CH, NE)
        tot = small[:, 720:736]
        nblk, incl_b = small[:, 736:752], small[:, 752:768]
        tmp64 = sm3(768, CH, NE)
        row12 = small[:, 832:840]
        rowbase = small[:, 840:856]
        emapf = small[:, 856:856 + ITEMS]
        rows_i = smalli[:, 0:8]
        emap_i = smalli[:, 8:8 + ITEMS]
        pairs_i = smalli[0:1, 8 + ITEMS:10 + ITEMS]
        pairs_f = small[:, 880:888]

        def item_turns(eng, L):
            def load(l):
                return eng.value_load(pairs_i[:, l:l + 1], min_val=2, max_val=ITEMS // 2)
            return load(L), (load(0) if L else 0)
        cmp = W[6][:, 0:ITEMS * NE].rearrange("p (i e) -> p i e", e=NE)
        wts = con[:, C_WTS:C_WTS + 4]
        iota = con[:, C_IOTA:C_IOTA + ITEMS]

        dg = [W[8 + j].rearrange("p (t n) -> p t n", n=P) for j in range(2)]

        def bc3(ap, n):
            return ap.unsqueeze(2).broadcast_to([P, CH, n])

        def first_only(step, dst, src, m):
            step(nc.vector.tensor_tensor(dst, src, bc3(m, 4), ALU.is_equal))
            step(nc.vector.tensor_tensor(dst, dst, wts.unsqueeze(1).broadcast_to([P, CH, 4]), ALU.mult))
            step(nc.vector.tensor_reduce(tmp4, dst, AX.X, ALU.max))
            step(nc.vector.tensor_tensor(dst, dst, bc3(tmp4, 4), ALU.is_equal))

        def moe_dve(dve, step, L):
            bge = par[:, PC["bge"] + 20 * L:PC["bge"] + 20 * L + 20]
            dve.wait_ge(S("m_logits"), 2 * L + 2)
            step(nc.vector.tensor_tensor(lg, bank[4][:, 0:80].rearrange("p (t n) -> p t n", n=20),
                                         bge.unsqueeze(1).broadcast_to([P, CH, 20]), ALU.add))
            step(nc.vector.tensor_reduce(gmax, gl, AX.X, ALU.max))
            nc.vector.tensor_tensor(sh, gl, bc3(gmax, 4), ALU.subtract).then_inc(S("m_shift"), 1)
            first_only(step, oh, gl, gmax)
            t4 = tmp64.rearrange("p t (g i) -> p t g i", g=4)
            step(nc.vector.tensor_tensor(t4, el, oh.unsqueeze(3).broadcast_to([P, CH, NG, EG]), ALU.mult))
            step(nc.vector.tensor_reduce(ing, t4.rearrange("p t g i -> p t i g"), AX.X, ALU.add))
            step(nc.vector.tensor_reduce(m1, ing, AX.X, ALU.max))
            first_only(step, oh1, ing, m1)
            step(nc.vector.scalar_tensor_tensor(out=wt, in0=oh1, scalar=-1e30, in1=ing, op0=ALU.mult, op1=ALU.add))
            step(nc.vector.tensor_reduce(m2, wt, AX.X, ALU.max))
            first_only(step, oh2, wt, m2)
            nc.vector.tensor_tensor(e2, m2, m1, ALU.subtract).then_inc(S("m_shift"), 1)
            for dst, o in ((sel1, oh1), (sel2, oh2)):
                step(nc.vector.tensor_tensor(dst, oh.unsqueeze(3).broadcast_to([P, CH, NG, EG]),
                                             o.unsqueeze(2).broadcast_to([P, CH, NG, EG]), ALU.mult))
            s1, s2 = (a.rearrange("p t g i -> p t (g i)") for a in (sel1, sel2))
            step(nc.vector.tensor_tensor(sel, s1, s2, ALU.add))
            step(nc.vector.memset(pre[:, 0, :], 0.0))
            for t in range(1, CH):
                step(nc.vector.tensor_tensor(pre[:, t, :], pre[:, t - 1, :], sel[:, t - 1, :], ALU.add))
            nc.vector.tensor_tensor(tot, pre[:, 3, :], sel[:, 3, :], ALU.add).then_inc(S("m_sel"), 1)
            dve.wait_ge(S("m_exp"), 2 * L + 2)
            step(nc.vector.tensor_reduce(gsum, sh, AX.X, ALU.add))
            step(nc.vector.tensor_scalar(gate1, e2, 1.0, None, ALU.add))
            step(nc.vector.tensor_tensor(gate1, gate1, gsum, ALU.mult))
            step(nc.vector.reciprocal(gate1, gate1))
            step(nc.vector.tensor_tensor(gate2, gate1, e2, ALU.mult))
            dve.wait_ge(S("m_ranks"), L + 1)
            cnt = bank[5][:, 64:80]
            step(nc.vector.tensor_scalar(nblk, cnt, 0.0, None, ALU.is_gt))
            for b in range(1, CH):
                step(nc.vector.scalar_tensor_tensor(out=nblk, in0=cnt, scalar=float(P * b), in1=nblk, op0=ALU.is_gt, op1=ALU.add))
            step(nc.vector.tensor_tensor_scan(incl_b, ones[:, 0:NE], nblk, 0.0, ALU.mult, ALU.add))
            step(nc.vector.tensor_tensor(rowbase, incl_b, nblk, ALU.subtract))
            step(nc.vector.tensor_tensor(cmp, incl_b.unsqueeze(1).broadcast_to([P, ITEMS, NE]),
                                         iota.unsqueeze(2).broadcast_to([P, ITEMS, NE]), ALU.is_le))
            step(nc.vector.tensor_reduce(emapf, cmp, AX.X, ALU.add))
            step(nc.vector.tensor_scalar(emapf, emapf, float(NE - 1), None, ALU.min))
            step(nc.vector.tensor_copy(emap_i, emapf))
            step(nc.vector.tensor_scalar(cmp[:, :, 0], iota, incl_b[:, NE - 1:NE], None, ALU.is_lt))
            step(nc.vector.tensor_reduce(pairs_f[:, 0:1], cmp[:, 0:ITEMS:2, 0], AX.X, ALU.add))
            nc.vector.tensor_copy(smalli[:, 8 + ITEMS + L:9 + ITEMS + L], pairs_f[:, 0:1]).then_inc(S("m_plan"), 1)
            step(nc.vector.tensor_scalar(rowbase, rowbase, float(P), None, ALU.mult))
            step(nc.vector.tensor_tensor(tmp64, bank[5][:, 0:64].rearrange("p (t e) -> p t e", e=NE),
                                         rowbase.unsqueeze(1).broadcast_to([P, CH, NE]), ALU.add))
            step(nc.vector.tensor_tensor(pre, tmp64, s1, ALU.mult))
            step(nc.vector.tensor_reduce(row12[:, 0:4], pre, AX.X, ALU.add))
            step(nc.vector.tensor_tensor(pre, tmp64, s2, ALU.mult))
            step(nc.vector.tensor_reduce(row12[:, 4:8], pre, AX.X, ALU.add))
            nc.vector.tensor_copy(rows_i, row12).then_inc(S("m_plan"), 1)
            dve.wait_ge(S("m_plan"), 2 * L + 2)
            turns, before = item_turns(dve, L)
            base = 2 * before
            for j, gate in enumerate((gate1, gate2)):
                for t in range(CH):
                    step(nc.vector.tensor_scalar(dg[j][:, t, :], ident, gate[:, t:t + 1], None, ALU.mult))
            with dve.Fori(0, turns) as i:
                for u in range(2):
                    n = 2 * i + (base + u)
                    dve.wait_ge(S("m_xt_ready"), n + 1)
                    for half in range(2):
                        nc.vector.tensor_copy(xgT[u][:, 4 * half:4 * half + 4, :], chunks(xbank[u][half][:, :])).then_inc(
                            S(f"m_xt{half}"), 1)
                for u in range(2):
                    n = 2 * i + (base + u)
                    dve.wait_ge(S("m_silu"), n + 1)
                    nc.vector.tensor_tensor(hid[u], hs[u], bank[2 + u][:, FF:2 * FF], ALU.mult).then_inc(S("m_hid"), 1)
                    dve.wait_ge(S("m_ht_ready"), n + 1)
                    nc.vector.tensor_copy(hidT[u], bank[4 + u][:, 0:256].rearrange("p (a n) -> p a n", a=2)).then_inc(
                        S("m_ht"), 1)
                for u in range(2):
                    n = 2 * i + (base + u)
                    dve.wait_ge(S("m_y_ready"), n + 3)
                    dve.wait_ge(S(f"m_y_sent{u}"), (i + before + 1) * 16)
                    nc.vector.tensor_copy(ysb[u][:, 0, :], ybank[u][0][:, :]).then_inc(S("m_y0"), 1)
            if L == 0:
                split_weights_dve(dve, B_CIN, low=False)
            for k in range(DT):
                dve.wait_ge(S("m_back"), DT * L + k + 1)
                nc.vector.tensor_tensor(xT[:, k, :], xT[:, k, :], bank[k % 7][:, :], ALU.add).then_inc(S("m_added"), 1)
            dve.wait_ge(S("m_added"), DT * (L + 1))

        def moe_act(act, step, L):
            act.wait_ge(S("m_logits"), 2 * L + 1)
            nc.scalar.activation(lgT, bank[5][0:20, :], ACT.Copy).then_inc(S("m_exp"), 1)
            for t in range(CH):
                if t == 0:
                    act.wait_ge(S("m_shift"), 2 * L + 1)
                    step(nc.scalar.activation(sh, sh, ACT.Exp))
                if t == 2:
                    act.wait_ge(S("m_shift"), 2 * L + 2)
                    nc.scalar.activation(e2, e2, ACT.Exp).then_inc(S("m_exp"), 1)
                act.wait_ge(S("m_tok_ready"), CH * L + t + 1)
                for half in range(2):
                    nc.scalar.activation(htok[:, t, half * T:half * T + T], bank[2 * (t % 2) + half][:, :],
                                         ACT.Copy).then_inc(S("m_tok"), 1)
            act.wait_ge(S("m_plan"), 2 * L + 2)
            turns, before = item_turns(act, L)
            base = 2 * before
            with act.Fori(0, turns) as i:
                for u in range(2):
                    n = 2 * i + (base + u)
                    act.wait_ge(S("m_h"), n + 3)
                    nc.scalar.activation(hs[u], bank[2 + u][:, 0:FF], ACT.Silu).then_inc(S("m_silu"), 1)
                for u in range(2):
                    n = 2 * i + (base + u)
                    act.wait_ge(S("m_y_ready"), n + 3)
                    act.wait_ge(S(f"m_y_sent{u}"), (i + before + 1) * 16)
                    nc.scalar.activation(ysb[u][:, 1, :], ybank[u][1][:, :], ACT.Copy).then_inc(S("m_y1"), 1)
                    act.wait_ge(S("m_y0"), n + 1)
                    act.wait_ge(S("m_y1"), n + 1)
                    dst = rows_d[bass.ds(i * (2 * P) + u * P, P), :]
                    act.dma_start(dst, ysb[u].rearrange("p a n -> p (a n)")).then_inc(S(f"m_y_sent{u}"), 16)
            for u in range(2):
                act.wait_ge(S(f"m_y_sent{u}"), (turns + before + 1) * 16)
            act.sem_inc(S("m_rows_sent"), 1)

        def moe_pe(pe, L):
            wge = par[:, PC["wge"] + 160 * L:PC["wge"] + 160 * L + 160].rearrange("p (k n) -> p k n", k=DT)
            for k in range(DT):
                pe.wait_ge(S("norm_done"), DT * (4 * L + 3) + k + 1)
                mm = nc.tensor.matmul(bank[5][0:20, :], wge[:, k, :], hT[:, k, :], start=(k == 0), stop=(k == DT - 1))
            mm.then_inc(S("m_logits"), 1)
            pe.wait_ge(S("m_exp"), 2 * L + 1)
            for t in range(CH):
                mm = nc.tensor.transpose(bank[4][:, 20 * t:20 * t + 20], lgT[:, t * P:t * P + P], ident[0:20, 0:20])
            mm.then_inc(S("m_logits"), 1)
            for t in range(CH):
                if t >= 2:
                    pe.wait_ge(S("m_tok"), 2 * (CH * L + t - 1))
                for k in range(DT):
                    mm = nc.tensor.transpose(bank[2 * (t % 2) + k // 4][:, (k % 4) * P:(k % 4) * P + P], chunks(hT[:, k, :])[:, t, :],
                                             ident)
                mm.then_inc(S("m_tok_ready"), 1)
                if t == CH - 1:
                    pe.wait_ge(S("m_sel"), L + 1)
                    sl = sel.rearrange("p t e -> p (t e)")
                    nc.tensor.matmul(bank[5][:, 0:64], strict, sl, start=True, stop=False)
                    nc.tensor.matmul(bank[5][:, 0:64], ones, pre.rearrange("p t e -> p (t e)"), start=False, stop=True)
                    nc.tensor.matmul(bank[5][:, 64:80], ones, tot, start=True, stop=True).then_inc(S("m_ranks"), 1)
            pe.wait_ge(S("m_plan"), 2 * L + 2)
            turns, before = item_turns(pe, L)
            base = 2 * before
            pe.wait_ge(S("m_tok"), 2 * CH * (L + 1))
            with pe.Fori(0, turns) as i:
                n0, n1 = 2 * i + base, 2 * i + (base + 1)

                def hidden(u, tiles):
                    for k in tiles:
                        if k == 4 and u == 0:
                            pe.wait_ge(S("m_xt1"), n0 + 1)
                        mm = nc.tensor.matmul(bank[2 + u][:, :], xgT[u][:, k, :], w13[u][:, k, :], start=(k == 0), stop=(k == DT - 1))
                    return mm

                def turn_hidden(u):
                    for a in range(2):
                        mm = nc.tensor.transpose(bank[4 + u][:, a * P:a * P + P], hid[u][:, a * P:a * P + P], ident)
                    mm.then_inc(S("m_ht_ready"), 1)

                def out_half(u, half):
                    for a in range(2):
                        mm = nc.tensor.matmul(ybank[u][half][:, :], hidT[u][:, a, :], w2e[u][:, a, half * T:half * T + T],
                                              start=(a == 0), stop=(a == 1))
                    return mm

                for u in range(2):
                    pe.wait_ge(S(f"m_x{u}"), (i + before + 1) * 16)
                    for k in range(DT):
                        mm = nc.tensor.transpose(xbank[u][k // 4][:, (k % 4) * P:(k % 4) * P + P], xg[u][:, k * P:k * P + P], ident)
                    mm.then_inc(S("m_xt_ready"), 1)
                pe.wait_ge(S("m_y0"), n0)
                pe.wait_ge(S("m_y1"), n0)
                pe.wait_ge(S("m_xt0"), n0 + 1)
                pe.wait_ge(S("m_w13_0"), (i + before + 1) * 16)
                hidden(0, range(DT)).then_inc(S("m_h"), 1)
                pe.wait_ge(S("m_xt0"), n1 + 1)
                pe.wait_ge(S("m_xt1"), n1 + 1)
                pe.wait_ge(S("m_w13_1"), (i + before + 1) * 16)
                hidden(1, range(0, 4))
                pe.wait_ge(S("m_hid"), n0 + 1)
                turn_hidden(0)
                hidden(1, range(4, DT)).then_inc(S("m_h"), 1)
                pe.wait_ge(S("m_ht"), n0 + 1)
                pe.wait_ge(S("m_w2_0"), (i + before + 1) * 16)
                out_half(0, 0)
                pe.wait_ge(S("m_hid"), n1 + 1)
                turn_hidden(1)
                out_half(0, 1).then_inc(S("m_y_ready"), 1)
                pe.wait_ge(S("m_ht"), n1 + 1)
                pe.wait_ge(S("m_w2_1"), (i + before + 1) * 16)
                out_half(1, 0)
                out_half(1, 1).then_inc(S("m_y_ready"), 1)
            pe.wait_ge(S("m_y0"), (turns + before) * 2)
            pe.wait_ge(S("m_y1"), (turns + before) * 2)
            pe.sem_inc(S("m_items_done"), 1)

            def combine(k, tiles):
                for t in tiles:
                    for j, y in enumerate((y1, y2)):
                        mm = nc.tensor.matmul(bank[k % 7][:, t * P:t * P + P], y[:, t, k * P:k * P + P], dg[j][:, t, :],
                                              start=(j == 0), stop=(j == 1))
                return mm

            pe.wait_ge(S("m_got0"), 64 * (L + 1))
            for k in range(DT - 1):
                combine(k, (0, 1))
            pe.wait_ge(S("m_got1"), 64 * (L + 1))
            for k in range(DT):
                if k == DT - 1:
                    pe.wait_ge(S("m_added"), DT * L + 1)
                combine(k, (2, 3) if k < DT - 1 else range(CH)).then_inc(S("m_back"), 1)
                if k >= 2:
                    norm_pe(pe, 4 * L + 4, T, [k - 2])
            norm_pe(pe, 4 * L + 4, T, [DT - 2, DT - 1])

        def moe_pool(pool, L):
            pool.wait_ge(S("m_plan"), 2 * L + 2)
            if L == 0:
                pool.wait_ge(S("rows_zeroed"), 16)
            for t in range(CH):
                pool.wait_ge(S("m_tok"), 2 * (CH * L + t + 1))
                for j in range(2):
                    pool.indirect_dma_start(rows_d[:, :], bass.IndirectOffsetOnAxis(ap=rows_i[:, 4 * j + t:4 * j + t + 1], axis=0),
                                            htok[:, t, :], None).then_inc(S("m_spread"), 16)
            pool.wait_ge(S("m_rows_sent"), L + 1)
            for t in range(CH):
                for j, y in enumerate((y1, y2)):
                    pool.indirect_dma_start(y[:, t, :], None, rows_d[:, :],
                                            bass.IndirectOffsetOnAxis(ap=rows_i[:, 4 * j + t:4 * j + t + 1], axis=0)).then_inc(
                        S(f"m_got{t // 2}"), 16)
            if L == 0:
                split_weights_pool(pool, B_CIN, 2)
            for half in range(2):
                pool.wait_ge(S(f"m_got{half}"), 64 * (L + 1))

        def moe_sync(sp, L):
            sp.wait_ge(S("m_plan"), 2 * L + 1)
            turns, before = item_turns(sp, L)
            base = 2 * before

            def w13_in(i, u):
                e = sp.value_load(emap_i[0:1, bass.ds(2 * i + u, 1)], min_val=0, max_val=NE - 1)
                sp.dma_start(ring[:, 3 * u:3 * u + 2, :].rearrange("p a n -> p (a n)"),
                             moe13[bass.ds(e * P + L * NE * P, P), :]).then_inc(S(f"m_w13_{u}"), 16)
                return e

            def w2_in(e, u):
                sp.dma_start(ring[:, 3 * u + 2, :], moe2[bass.ds(e * P + L * NE * P, P), :]).then_inc(S(f"m_w2_{u}"), 16)

            experts = [w13_in(0, 0), None]
            sp.wait_ge(S("m_spread"), 16 * 8 * (L + 1))
            for u in range(2):
                sp.dma_start(xg[u], rows_d[u * P:(u + 1) * P, :]).then_inc(S(f"m_x{u}"), 16)
            experts[1] = w13_in(0, 1)
            for u in range(2):
                w2_in(experts[u], u)
            with sp.Fori(1, turns) as i:
                for u in range(2):
                    n = 2 * i + (base + u)
                    sp.wait_ge(S("m_h"), n + 1)
                    sp.dma_start(xg[u], rows_d[bass.ds(i * (2 * P) + u * P, P), :]).then_inc(S(f"m_x{u}"), 16)
                    experts[u] = w13_in(i, u)
                for u in range(2):
                    sp.wait_ge(S("m_y_ready"), 2 * i + (base + u + 1))
                    w2_in(experts[u], u)
            sp.wait_ge(S("m_items_done"), L + 1)

        first_xa = [B_XA0, B_XA1]

        @block.sync
        def _(sp):
            sp.dma_start(xT[:, :, :], x_d.rearrange("(k p) t -> p k t", p=P)).then_inc(S("x_in"), 16)
            sp.dma_start(con[:, :], con_d).then_inc(S("con_in"), 16)
            sp.dma_start(par[:, :], par_d).then_inc(S("par_in"), 16)

            def load_blocks(first, count):
                before = first - RING
                was_split = before in BEFORE

                def load(i, b):
                    if was_split:
                        sp.wait_ge(S("w_split"), BEFORE[b - RING] + RING * i + 1)
                    else:
                        sp.wait_ge(S("tile_ready1"), b - RING + RING * i + 1)
                    fetch(i, b)
                each_block(sp, first, count, load)

            def fetch(i, b):
                src = wst[bass.ds((b + RING * i) * P, P), :] if not isinstance(i, int) else wst[(b + RING * i) * P:(b + RING * i + 1) * P, :]
                sp.dma_start(ring[:, b % RING, :], src).then_inc(S(f"weights{b % RING}"), 16)

            for b in range(RING):
                fetch(0, b)

            def load_mem(done, n):
                sp.wait_ge(S(done), n)
                sp.dma_start(memn[:, :, 0:M], mem_d.rearrange("(k p) t -> p k t", p=P)).then_inc(S("mem_in"), 16)

            load_blocks(RING, 15)
            load_mem("b_done", BT)
            load_blocks(RING + 15, 12)
            load_blocks(RING + B_XA0 + 8, 6)
            moe_sync(sp, 0)
            load_blocks(B_CIN, 2)
            load_blocks(B_CIN + 2, 16)
            load_mem("c_done", CHEADS)
            load_blocks(B_COUT + 2, 12)
            load_blocks(B_XA1 + 10, 6)
            moe_sync(sp, 1)
            for t in range(DT):
                sp.wait_ge(S("norm_done"), DT * 8 + t + 1)
                sp.dma_start(out_d[t * P:t * P + P, :], hT[:, t, :]).then_inc(S("out_sent"), 16)
            sp.wait_ge(S("out_sent"), 16 * DT)

        @block.scalar
        def _(act):
            step = Line(act, "act_order")
            act.sem_inc(S("m_y_sent0"), 16)
            act.sem_inc(S("m_y_sent1"), 16)
            act.wait_ge(S("x_in"), 16)
            norm_act(act, step, 0, xT, T)
            split_stream_act(act, 0, 0)
            drain_copies("act", act, B_IN, N_A, 0, proj, 0, T)
            mixer0_act(act, step)
            for L in range(2):
                fx = first_xa[L]
                if L == 1:
                    rstd_act(act, step, 4, T)
                    split_stream_act(act, 3, 4)
                    hgrn_act(act, step)
                act.wait_ge(S("b_done") if L == 0 else S("c_done"), BT if L == 0 else CHEADS)
                act.wait_ge(S("mem_in"), 16 * (L + 1))
                norm_act(act, step, 4 * L + 1, memn, M)
                for h in range(2):
                    act.wait_ge(S(f"tile_free{h}"), 2 + fx)
                drain_copies("act", act, fx, 4, 0, proj, 0, M)
                square_act(act, 4 * L + 2, xT, T)
                drain_copies("act", act, fx + 4, 2, 0, proj, 8, 256)
                rstd_act(act, step, 4 * L + 2, T)
                split_stream_act(act, 3 * L + 1, 4 * L + 2)
                drain_copies("act", act, fx + 6, 2, 0, proj, 12, 256)
                drain_copies("act", act, fx + 8, 4, 0, proj, 16, T)
                act.wait_ge(S("tile_free1"), 2 + fx + 12)
                xattn_act(act, step, L)
                norm_act(act, step, 4 * L + 3, xT, T,
                         lambda t: act.wait_ge(S(f"tile_free{t % 2}"), 2 + fx + 12 + t // 2 + 1))
                moe_act(act, step, L)
                square_act(act, 4 * L + 4, xT, T, lambda t: act.wait_ge(S("m_added"), DT * L + t + 1))
            rstd_act(act, step, 8, T)

        @block.tensor
        def _(pe):
            pe.sem_inc(S("m_h"), 2)
            pe.sem_inc(S("m_y_ready"), 2)
            pe.wait_ge(S("con_in"), 16)
            norm_pe(pe, 0, T)
            pe.wait_ge(S("par_in"), 16)
            rates_pe(pe)
            project_split_pe(pe, B_IN, N_A, 0)
            mixer0_pe(pe)
            for L in range(2):
                fx = first_xa[L]
                if L == 1:
                    project_split_pe(pe, B_CIN, 16, 3)
                    pe.wait_ge(S("tile_free0"), 2 + B_COUT)
                    pe.wait_ge(S("tile_free1"), 2 + B_COUT)
                    hgrn_pe(pe)
                    pe.wait_ge(S("c_done"), CHEADS)
                project_pe(pe, fx - 4, 2, hT, T)
                norm_pe(pe, 4 * L + 1, M)
                project_pe(pe, fx - 2, 2, hT, T)
                pe.wait_ge(S("norm_done"), DT * (4 * L + 2))
                project_pe(pe, fx, 4, memn, M)
                project_pe(pe, fx + 4, 2, memn, M, tokens_out=True)
                norm_pe(pe, 4 * L + 2, T)
                project_pe(pe, fx + 6, 2, memn, M, tokens_out=True)
                project_split_pe(pe, fx + 8, 4, 3 * L + 1)
                xattn_pe(pe, L)
                for b in range(4):
                    project_split_pe(pe, fx + 12 + b, 1, 3 * L + 2)
                    if b > 0:
                        norm_pe(pe, 4 * L + 3, T, [2 * b - 2, 2 * b - 1])
                norm_pe(pe, 4 * L + 3, T, [DT - 2, DT - 1])
                moe_pe(pe, L)

        @block.vector
        def _(dve):
            step = Line(dve, "dve_order")
            dve.sem_inc(S("tile_free0"), 2)
            dve.sem_inc(S("tile_free1"), 2)
            dve.wait_ge(S("x_in"), 16)
            dve.wait_ge(S("con_in"), 16)
            dve.wait_ge(S("par_in"), 16)
            split_weights_dve(dve, B_IN)
            norm_dve(dve, 0, xT, hT, T, gains("mix", 0))
            drain_copies("dve", dve, B_IN, N_A, 1, proj, 0, T)
            mixer0_dve(dve, step)
            for L in range(2):
                fx = first_xa[L]
                if L == 1:
                    norm_dve(dve, 4, xT, hT, T, gains("mix", 1))
                    hgrn_dve(dve, step)
                drain_residual(dve, fx - 4, 2, 0)
                norm_dve(dve, 4 * L + 1, memn, memn, M, gains("mem", L))
                drain_residual(dve, fx - 2, 2, 4)
                drain_copies("dve", dve, fx, 4, 1, proj, 0, M)
                drain_copies("dve", dve, fx + 4, 2, 1, proj, 8, 256)
                norm_dve(dve, 4 * L + 2, xT, hT, T, gains("xat", L))
                drain_copies("dve", dve, fx + 6, 2, 1, proj, 12, 256)
                split_weights_dve(dve, fx + 8)
                drain_copies("dve", dve, fx + 8, 4, 1, proj, 16, T)
                xattn_dve(dve, step, L)
                drain_residual(dve, fx + 12)
                norm_dve(dve, 4 * L + 3, xT, hT, T, gains("ffn", L))
                moe_dve(dve, step, L)
            norm_dve(dve, 8, xT, hT, T, gains("fin"))

        @block.gpsimd
        def _(pool):
            split_stream_pool(pool, 0)
            split_weights_pool(pool, B_IN + 1, 14)
            pool.wait_ge(S("con_in"), 16)
            zero = con[32:P, C_SEL:C_SEL + D]
            pool.dma_start(rows_d.rearrange("(i p) d -> p i d", p=P - 32),
                           zero.unsqueeze(1).broadcast_to([P - 32, ITEMS * P // (P - 32), D])).then_inc(S("rows_zeroed"), 16)
            for r in range(2):
                inv_pool(pool, r, a_bufs(r))
            for q in range(BT):
                inv_pool(pool, 2 + q, b_inv(q))
            for L in range(2):
                if L == 1:
                    split_stream_pool(pool, 3)
                    split_weights_pool(pool, B_CIN + 2, 14)
                    hgrn_pool(pool)
                fx = first_xa[L]
                split_stream_pool(pool, 3 * L + 1)
                split_weights_pool(pool, fx + 9, 1)
                split_weights_pool(pool, fx + 10, 4)
                split_stream_pool(pool, 3 * L + 2)
                split_weights_pool(pool, fx + 14, 2)
                moe_pool(pool, L)


def constants():
    c = np.zeros((P, NCONST), np.float32)
    i = np.arange(P)
    c[:, C_ID:C_ID + P] = np.eye(P)
    c[:, C_ONE:C_ONE + P] = 1
    c[:, C_BLK:C_BLK + P] = i[:, None] // 64 == i[None, :] // 64
    c[:, C_INC:C_INC + P] = i[:, None] <= i[None, :]
    c[:, C_STR:C_STR + P] = i[:, None] < i[None, :]
    for n, s in enumerate(LEVELS):
        same = i[:, None] // (2 * s) == i[None, :] // (2 * s)
        c[:, C_LVL + n * P:C_LVL + n * P + P] = same & (i[:, None] // s % 2 == 0) & (i[None, :] // s % 2 == 1)
    c[:, C_RST:C_RST + T] = np.arange(T) % P != 0
    for h in range(8):
        c[h, C_SEL + h * P:C_SEL + h * P + P] = 1
    c[:, C_IOTA:C_IOTA + ITEMS] = np.arange(ITEMS)
    c[:, C_WTS:C_WTS + 4] = [4, 3, 2, 1]
    c[:, C_EPS] = 1e-6
    c[:, C_EPS + 1] = 64e-5
    return c


def columns(v):
    v = np.asarray(v).reshape(-1, P)
    return v.T


def blocks(w):
    k, n = w.shape
    return np.asarray(w).reshape(DT, P, n // 256, 256).transpose(2, 1, 0, 3).reshape(n // 256, P, BLK)


def pack(i):
    f = {k: np.asarray(v) for k, v in i.items()}
    par = np.zeros((P, NPAR), np.float32)

    def put(name, a):
        par[:a.shape[0], PC[name]:PC[name] + a.shape[1]] = a

    for n, k in (("mix", "norm_mix"), ("xat", "norm_xattn"), ("mem", "norm_mem"), ("ffn", "norm_ffn"), ("fin", "norm_final"),
                 ("mu", "ab_shift_mu"), ("w0", "ab_w0"), ("a0", "ab_a0"), ("kk", "ab_k_k"), ("ka", "ab_k_a"), ("rk", "ab_r_k"),
                 ("lnw", "ab_ln_w"), ("lnb", "ab_ln_b"), ("lb", "c_lb_param"), ("onA", "ab_onorm"), ("onC", "c_onorm")):
        put(n, columns(f[k]))
    put("conv", f["ab_conv"][0].reshape(4, 12, P).transpose(2, 1, 0).reshape(P, 48))
    put("alog", f["ab_a_log"].reshape(4, 1))
    put("dt", f["ab_dt_bias"].reshape(4, 1))
    put("w2a2", np.concatenate([f["ab_w2"][0], f["ab_a2"][0]], axis=0))
    put("g2", f["ab_g2"][0])
    w_in = f["ab_w_in"][0]
    put("wdb", w_in[:, 2048:2056].reshape(DT, P, 8).transpose(1, 0, 2).reshape(P, 64))
    for L in range(2):
        wge = np.concatenate([f["moe_w_group"][L], f["moe_w_expert"][L]], axis=1)
        par[:, PC["wge"] + 160 * L:PC["wge"] + 160 * L + 160] = wge.reshape(DT, P, 20).transpose(1, 0, 2).reshape(P, 160)
        par[:, PC["bge"] + 20 * L:PC["bge"] + 20 * L + 20] = np.concatenate([f["moe_b_group"][L], f["moe_b_expert"][L]])
    wst = [blocks(w_in[:, :2048]), blocks(w_in[:, 2056:]), blocks(f["ab_w_out"][0])]
    for L in range(2):
        if L:
            wst += [blocks(f["c_w_in"][0]), blocks(f["c_w_out"][0])]
        wst += [blocks(f["xa_wkv"][L]), blocks(f["xa_wq"][L]), blocks(f["xa_wo"][L])]
    wst = np.concatenate(wst).reshape(NBLK * P, BLK)
    w13 = np.stack([f["moe_w1"], f["moe_w3"]], axis=3)
    w13 = w13.reshape(2, NE, DT, P, 2 * FF).transpose(0, 1, 3, 2, 4).reshape(2 * NE * P, 2 * BLK)
    w2 = f["moe_w2"].reshape(2, NE, 2, P, D).transpose(0, 1, 3, 2, 4).reshape(2 * NE * P, BLK)
    c = np.ascontiguousarray
    return {"wst": c(wst), "moe13": c(w13), "moe2": c(w2), "par": par, "con": constants(), "x": c(f["x"][0].T),
            "mem": c(f["mem"][0].T)}


def program(nc, arrays):
    ins = {n: nc.dram_tensor(f"in_{n}", a.shape, F32, kind="ExternalInput").ap() for n, a in arrays.items()}
    out = nc.dram_tensor("out_x", (D, T), F32, kind="ExternalOutput").ap()
    rows = nc.dram_tensor("sorted_rows", (ITEMS * P, D), F32, kind="Internal").ap()
    build(nc, ins["wst"], ins["moe13"], ins["moe2"], ins["par"], ins["con"], ins["x"], ins["mem"], out, rows)


def kernel(**inputs):
    import concourse.bacc as bacc
    from concourse.bass_utils import run_bass_kernel_spmd

    arrays = pack(inputs)
    nc = bacc.Bacc("TRN2", target_bir_lowering=False, num_devices=1)
    program(nc, arrays)
    r = run_bass_kernel_spmd(nc, [{f"in_{n}": a for n, a in arrays.items()}], core_ids=[0])
    return np.ascontiguousarray(r.results[0]["out_x"].T)[None]
```
